# Optimizing a Trainium2 kernel written in Bass

```python
import math
import jax, jax.numpy as jnp
from jax import lax
import numpy as np
import jax
import jax.numpy as jnp

D_MODEL = 1024
BATCH = 1
SEQ = 256
DEPTH = 2

POOL_WIDTH = D_MODEL // 4
POOL_WINDOWS = (2, 4, 8, 16)
POOL_GROUPS = len(POOL_WINDOWS)
POOL_GROUP_DIM = POOL_WIDTH // POOL_GROUPS
CONV_WIDTH = D_MODEL // 4
CONV_K = 3
HEAD_DIM = 64
ATTN_HEADS = 8
ATTN_WIDTH = ATTN_HEADS * HEAD_DIM
ROPE_DIM = HEAD_DIM // 4
ROPE_THETA = 500000.0
MOBA_BLOCK = 256
MOBA_TOPK = 3
Q_CHUNK = 32
N_BRANCH = 3
IN_WIDTH = POOL_WIDTH + 3 * CONV_WIDTH + 3 * ATTN_WIDTH + N_BRANCH * D_MODEL
D_FF = -(-8 * D_MODEL // (3 * 256)) * 256
EPS = 1e-6
NEG = -1e30
POS_OFFSET_MAX = 1024


def rmsnorm(x, w):
    xf = x.astype(jnp.float32)
    xf = xf * lax.rsqrt(jnp.mean(xf * xf, axis=-1, keepdims=True) + EPS)
    return xf.astype(x.dtype) * w

def rotary_tables(positions):
    freqs = ROPE_THETA ** (-jnp.arange(0, ROPE_DIM, 2, dtype=jnp.float32) / ROPE_DIM)
    ang = positions.astype(jnp.float32)[..., None] * freqs
    return jnp.cos(ang), jnp.sin(ang)

def apply_partial_rope(x, cos, sin):
    half = ROPE_DIM // 2
    xr = x[..., :ROPE_DIM].astype(jnp.float32)
    x1, x2 = xr[..., :half], xr[..., half:]
    c = cos[:, :, None, :]
    s = sin[:, :, None, :]
    rot = jnp.concatenate([x1 * c - x2 * s, x2 * c + x1 * s], axis=-1).astype(x.dtype)
    return jnp.concatenate([rot, x[..., ROPE_DIM:]], axis=-1)

def pool_mixer(u, pool_w, pool_scale):
    B, S, _ = u.shape
    uf = u.astype(jnp.float32)
    cs = jnp.pad(jnp.cumsum(uf, axis=1), ((0, 0), (1, 0), (0, 0)))
    t = jnp.arange(S)
    outs = []
    for g, w in enumerate(POOL_WINDOWS):
        sl = slice(g * POOL_GROUP_DIM, (g + 1) * POOL_GROUP_DIM)
        lo = jnp.maximum(t + 1 - w, 0)
        cs_g = cs[..., sl]
        window_sum = cs_g[:, 1:] - jnp.take(cs_g, lo, axis=1)
        count = (t + 1 - lo).astype(jnp.float32)[None, :, None]
        outs.append(window_sum / count - uf[..., sl])
    pooled = jnp.concatenate(outs, axis=-1).astype(u.dtype).reshape(B, S, POOL_GROUPS, POOL_GROUP_DIM)
    y = jnp.einsum('bsgi,gio->bsgo', pooled, pool_w).reshape(B, S, POOL_WIDTH)
    return y * pool_scale

def causal_short_conv(u, conv_w):
    C = u.shape[-1]
    return lax.conv_general_dilated(
        u, conv_w[:, None, :], window_strides=(1,), padding=((CONV_K - 1, 0),),
        dimension_numbers=('NWC', 'WIO', 'NWC'), feature_group_count=C)

def moba_attention(q, k, v):
    B, H, S, hd = q.shape
    nb = -(-S // MOBA_BLOCK)
    pad = nb * MOBA_BLOCK - S
    kb = jnp.pad(k, ((0, 0), (0, 0), (0, pad), (0, 0))).reshape(B, H, nb, MOBA_BLOCK, hd)
    vb = jnp.pad(v, ((0, 0), (0, 0), (0, pad), (0, 0))).reshape(B, H, nb, MOBA_BLOCK, hd)
    kmean = jnp.mean(kb.astype(jnp.float32), axis=3)
    n_sel = max(1, min(MOBA_TOPK, nb - 1))
    nc = S // Q_CHUNK
    q_chunks = q.reshape(B, H, nc, Q_CHUNK, hd).transpose(2, 0, 1, 3, 4)
    starts = jnp.arange(nc, dtype=jnp.int32) * Q_CHUNK
    scale = 1.0 / math.sqrt(hd)
    gather_blocks = jax.vmap(jax.vmap(lambda blocks, ix: blocks[ix]))

    def one_chunk(args):
        q_i, start = args
        qpos = start + jnp.arange(Q_CHUNK, dtype=jnp.int32)
        blk = start // MOBA_BLOCK
        gate = jnp.einsum('bhqd,bhnd->bhqn', q_i.astype(jnp.float32), kmean)
        past = jnp.arange(nb) < blk
        gate = jnp.where(past, gate, NEG)
        _, idx = lax.top_k(gate, n_sel)
        valid = idx < blk
        k_sel = gather_blocks(kb, idx)
        v_sel = gather_blocks(vb, idx)
        s_sel = jnp.einsum('bhqd,bhqjkd->bhqjk', q_i, k_sel).astype(jnp.float32) * scale
        s_sel = jnp.where(valid[..., None], s_sel, NEG).reshape(B, H, Q_CHUNK, n_sel * MOBA_BLOCK)
        k_own = lax.dynamic_index_in_dim(kb, blk, axis=2, keepdims=False)
        v_own = lax.dynamic_index_in_dim(vb, blk, axis=2, keepdims=False)
        s_own = jnp.einsum('bhqd,bhkd->bhqk', q_i, k_own).astype(jnp.float32) * scale
        kpos = blk * MOBA_BLOCK + jnp.arange(MOBA_BLOCK, dtype=jnp.int32)
        s_own = jnp.where(kpos[None, :] <= qpos[:, None], s_own, NEG)
        p = jax.nn.softmax(jnp.concatenate([s_sel, s_own], axis=-1), axis=-1).astype(v.dtype)
        p_sel = p[..., :n_sel * MOBA_BLOCK].reshape(B, H, Q_CHUNK, n_sel, MOBA_BLOCK)
        p_own = p[..., n_sel * MOBA_BLOCK:]
        return (jnp.einsum('bhqjk,bhqjkd->bhqd', p_sel, v_sel)
                + jnp.einsum('bhqk,bhkd->bhqd', p_own, v_own))

    out = lax.map(one_chunk, (q_chunks, starts))
    return out.transpose(1, 2, 0, 3, 4).reshape(B, H, S, hd)

def hybrid_layer(x, c_act, cos, sin, norm1_w, norm2_w, w_ada, b_ada, w_in, pool_w, pool_scale,
                 conv_w, q_norm_w, k_norm_w, p_pool, p_conv, p_attn, w_out, w_gate, w_up, w_down):
    B, S, D = x.shape
    mod = (c_act @ w_ada + b_ada)[:, None, :]
    sh1, sc1, g1, sh2, sc2, g2 = jnp.split(mod, 6, axis=-1)
    h = rmsnorm(x, norm1_w) * (1 + sc1) + sh1
    u = h @ w_in
    widths = [POOL_WIDTH, CONV_WIDTH, CONV_WIDTH, CONV_WIDTH, ATTN_WIDTH, ATTN_WIDTH, ATTN_WIDTH]
    offsets = [int(o) for o in np.cumsum(widths)]
    u_pool, u_conv, b_conv, c_conv, q, k, v, gate_logits = jnp.split(u, offsets, axis=-1)
    y_pool = pool_mixer(u_pool, pool_w, pool_scale)
    y_conv = b_conv * causal_short_conv(c_conv * u_conv, conv_w)
    q = apply_partial_rope(rmsnorm(q.reshape(B, S, ATTN_HEADS, HEAD_DIM), q_norm_w), cos, sin)
    k = apply_partial_rope(rmsnorm(k.reshape(B, S, ATTN_HEADS, HEAD_DIM), k_norm_w), cos, sin)
    v = v.reshape(B, S, ATTN_HEADS, HEAD_DIM)
    o = moba_attention(q.transpose(0, 2, 1, 3), k.transpose(0, 2, 1, 3), v.transpose(0, 2, 1, 3))
    y_attn = o.transpose(0, 2, 1, 3).reshape(B, S, ATTN_WIDTH)
    gates = jax.nn.sigmoid(gate_logits).reshape(B, S, N_BRANCH, D)
    merged = (gates[:, :, 0] * (y_pool @ p_pool)
              + gates[:, :, 1] * (y_conv @ p_conv)
              + gates[:, :, 2] * (y_attn @ p_attn))
    x = x + g1 * (merged @ w_out)
    h2 = rmsnorm(x, norm2_w) * (1 + sc2) + sh2
    x = x + g2 * ((jax.nn.silu(h2 @ w_gate) * (h2 @ w_up)) @ w_down)
    return x

def first_inputs(seed: int = 0) -> dict:
    key = jax.random.key(seed)
    ks = jax.random.split(key, 24)
    L = DEPTH

    def nrm(k, shape, fan_in, gain=1.0):
        return gain * fan_in ** -0.5 * jax.random.normal(k, shape, jnp.float32)

    def gain_init(k, shape):
        return 1.0 + 0.1 * jax.random.normal(k, shape, jnp.float32)

    x = jax.random.normal(ks[0], (BATCH, SEQ, D_MODEL), jnp.float32)
    c = jax.random.normal(ks[1], (BATCH, D_MODEL), jnp.float32)
    positions = (jnp.arange(SEQ, dtype=jnp.int32)[None, :]
                 + jax.random.randint(ks[2], (BATCH, 1), 0, POS_OFFSET_MAX, dtype=jnp.int32))
    return {
        "x": x,
        "c": c,
        "positions": positions,
        "norm1_w": gain_init(ks[3], (L, D_MODEL)),
        "norm2_w": gain_init(ks[4], (L, D_MODEL)),
        "w_ada": nrm(ks[5], (L, D_MODEL, 6 * D_MODEL), D_MODEL, 0.5),
        "b_ada": 0.02 * jax.random.normal(ks[6], (L, 6 * D_MODEL), jnp.float32),
        "w_in": nrm(ks[7], (L, D_MODEL, IN_WIDTH), D_MODEL),
        "pool_w": nrm(ks[8], (L, POOL_GROUPS, POOL_GROUP_DIM, POOL_GROUP_DIM), POOL_GROUP_DIM),
        "pool_scale": gain_init(ks[9], (L, POOL_WIDTH)),
        "conv_w": nrm(ks[10], (L, CONV_K, CONV_WIDTH), CONV_K),
        "q_norm_w": gain_init(ks[11], (L, HEAD_DIM)),
        "k_norm_w": gain_init(ks[12], (L, HEAD_DIM)),
        "p_pool": nrm(ks[13], (L, POOL_WIDTH, D_MODEL), POOL_WIDTH),
        "p_conv": nrm(ks[14], (L, CONV_WIDTH, D_MODEL), CONV_WIDTH),
        "p_attn": nrm(ks[15], (L, ATTN_WIDTH, D_MODEL), ATTN_WIDTH),
        "w_out": nrm(ks[16], (L, D_MODEL, D_MODEL), D_MODEL),
        "w_gate": nrm(ks[17], (L, D_MODEL, D_FF), D_MODEL),
        "w_up": nrm(ks[18], (L, D_MODEL, D_FF), D_MODEL),
        "w_down": nrm(ks[19], (L, D_FF, D_MODEL), D_FF),
    }

def first_block(x, c, positions, norm1_w, norm2_w, w_ada, b_ada, w_in, pool_w, pool_scale, conv_w,
              q_norm_w, k_norm_w, p_pool, p_conv, p_attn, w_out, w_gate, w_up, w_down):
    c_act = jax.nn.silu(c)
    cos, sin = rotary_tables(positions)
    for l in range(DEPTH):
        x = hybrid_layer(x, c_act, cos, sin, norm1_w[l], norm2_w[l], w_ada[l], b_ada[l], w_in[l],
                         pool_w[l], pool_scale[l], conv_w[l], q_norm_w[l], k_norm_w[l],
                         p_pool[l], p_conv[l], p_attn[l], w_out[l], w_gate[l], w_up[l], w_down[l])
    return x


CHUNK = 64
Q_BLOCK = 128

MLA_HEADS = 8
DIFF_HEADS = 4
FOX_HEADS = 4
D_MIX = (MLA_HEADS + DIFF_HEADS + FOX_HEADS) * HEAD_DIM

MLA_Q_RANK = 384
MLA_KV_RANK = 256
MLA_NOPE = 64
MLA_ROPE = 32
MLA_V = HEAD_DIM

DIFF_QK = HEAD_DIM // 2
DIFF_V = HEAD_DIM
DIFF_ROT = DIFF_QK // 4
DIFF_W = DIFF_HEADS * HEAD_DIM

FOX_W = FOX_HEADS * HEAD_DIM

IN_SPLITS = (MLA_Q_RANK, MLA_KV_RANK, MLA_ROPE,
             DIFF_W, DIFF_W, DIFF_W,
             FOX_W, FOX_W, FOX_W, FOX_HEADS)
IN_COLS = MLA_Q_RANK + MLA_KV_RANK + MLA_ROPE + 3 * DIFF_W + 3 * FOX_W + FOX_HEADS

N_EXPERTS = 16
N_GROUPS = 4
GROUP_SIZE = N_EXPERTS // N_GROUPS
TOP_K = 2
D_EXPERT = 512

DEEPNORM_ALPHA = (2 * DEPTH) ** 0.25
DEEPNORM_BETA = (8 * DEPTH) ** -0.25

LN_EPS = 1e-5
RMS_EPS = 1e-6
NEG_INF = -1e30
F32 = jnp.float32


def layer_norm(x, g, b):
    xf = x.astype(F32)
    mu = jnp.mean(xf, axis=-1, keepdims=True)
    var = jnp.mean(jnp.square(xf - mu), axis=-1, keepdims=True)
    return ((xf - mu) * lax.rsqrt(var + LN_EPS) * g.astype(F32) + b.astype(F32)).astype(x.dtype)

def rms_norm(x, g):
    xf = x.astype(F32)
    return (xf * lax.rsqrt(jnp.mean(xf * xf, axis=-1, keepdims=True) + RMS_EPS) * g.astype(F32)).astype(x.dtype)

def rope_tables(positions, rot_dim):
    inv_freq = ROPE_THETA ** (-jnp.arange(0, rot_dim, 2, dtype=F32) / rot_dim)
    ang = positions.astype(F32)[..., None] * inv_freq
    return jnp.cos(ang), jnp.sin(ang)

def apply_rope(x, cos, sin):
    xf = x.astype(F32)
    x1, x2 = jnp.split(xf, 2, axis=-1)
    c = cos[:, :, None, :]
    s = sin[:, :, None, :]
    return jnp.concatenate([x1 * c - x2 * s, x2 * c + x1 * s], axis=-1).astype(x.dtype)

def partial_rope(x, cos, sin, rot_dim):
    return jnp.concatenate([apply_rope(x[..., :rot_dim], cos, sin), x[..., rot_dim:]], axis=-1)

def q_block(a, i, axis=1):
    return lax.dynamic_slice_in_dim(a, i * Q_BLOCK, Q_BLOCK, axis)

def chunk_causal_mask(i, seq):
    q_idx = i * Q_BLOCK + jnp.arange(Q_BLOCK)
    k_idx = jnp.arange(seq)
    return (k_idx[None, :] // CHUNK) <= (q_idx[:, None] // CHUNK)

def frame_causal_mask(i, seq):
    q_idx = i * Q_BLOCK + jnp.arange(Q_BLOCK)
    k_idx = jnp.arange(seq)
    return k_idx[None, :] <= q_idx[:, None]

def sweep_query_blocks(block_fn, seq):
    out = lax.map(block_fn, jnp.arange(seq // Q_BLOCK))
    out = jnp.moveaxis(out, 0, 1)
    return out.reshape(out.shape[0], seq, out.shape[3], out.shape[4])

def mla_attention(c_q, c_kv, k_rope_raw, q_norm_g, kv_norm_g, w_uq, w_ukv, cos, sin):
    b, seq, _ = c_q.shape
    q = (rms_norm(c_q, q_norm_g) @ w_uq).reshape(b, seq, MLA_HEADS, MLA_NOPE + MLA_ROPE)
    q_nope = q[..., :MLA_NOPE]
    q_rope = apply_rope(q[..., MLA_NOPE:], cos, sin)
    kv = (rms_norm(c_kv, kv_norm_g) @ w_ukv).reshape(b, seq, MLA_HEADS, MLA_NOPE + MLA_V)
    k_nope = kv[..., :MLA_NOPE]
    v = kv[..., MLA_NOPE:]
    k_rope = apply_rope(k_rope_raw[:, :, None, :], cos, sin)[:, :, 0, :]
    scale = (MLA_NOPE + MLA_ROPE) ** -0.5

    def block(i):
        sc = (jnp.einsum('bqhd,bkhd->bhqk', q_block(q_nope, i), k_nope, preferred_element_type=F32)
              + jnp.einsum('bqhr,bkr->bhqk', q_block(q_rope, i), k_rope, preferred_element_type=F32)) * scale
        sc = jnp.where(chunk_causal_mask(i, seq), sc, NEG_INF)
        p = jax.nn.softmax(sc, axis=-1).astype(v.dtype)
        return jnp.einsum('bhqk,bkhd->bqhd', p, v)

    return sweep_query_blocks(block, seq)

def diff_attention(q, k, v, lam_q1, lam_k1, lam_q2, lam_k2, subln_g, lam_init, cos, sin):
    b, seq, _ = q.shape
    q = partial_rope(q.reshape(b, seq, 2 * DIFF_HEADS, DIFF_QK), cos, sin, DIFF_ROT)
    k = partial_rope(k.reshape(b, seq, 2 * DIFF_HEADS, DIFF_QK), cos, sin, DIFF_ROT)
    q1, q2 = q[:, :, 0::2], q[:, :, 1::2]
    k1, k2 = k[:, :, 0::2], k[:, :, 1::2]
    v = v.reshape(b, seq, DIFF_HEADS, DIFF_V)
    lam = (jnp.exp(jnp.sum(lam_q1.astype(F32) * lam_k1.astype(F32)))
           - jnp.exp(jnp.sum(lam_q2.astype(F32) * lam_k2.astype(F32))) + lam_init)
    scale = DIFF_QK ** -0.5

    def block(i):
        mask = chunk_causal_mask(i, seq)
        s1 = jnp.einsum('bqhd,bkhd->bhqk', q_block(q1, i), k1, preferred_element_type=F32) * scale
        s2 = jnp.einsum('bqhd,bkhd->bhqk', q_block(q2, i), k2, preferred_element_type=F32) * scale
        p = (jax.nn.softmax(jnp.where(mask, s1, NEG_INF), axis=-1)
             - lam * jax.nn.softmax(jnp.where(mask, s2, NEG_INF), axis=-1)).astype(v.dtype)
        return jnp.einsum('bhqk,bkhd->bqhd', p, v)

    o = sweep_query_blocks(block, seq)
    return rms_norm(o, subln_g) * (1.0 - lam_init)

def forgetting_attention(q, k, v, f_logit, f_bias):
    b, seq, _ = q.shape
    q = q.reshape(b, seq, FOX_HEADS, HEAD_DIM)
    k = k.reshape(b, seq, FOX_HEADS, HEAD_DIM)
    v = v.reshape(b, seq, FOX_HEADS, HEAD_DIM)
    log_f = jax.nn.log_sigmoid(f_logit.astype(F32) + f_bias.astype(F32))
    cum = jnp.cumsum(log_f, axis=1).transpose(0, 2, 1)
    scale = HEAD_DIM ** -0.5

    def block(i):
        sc = jnp.einsum('bqhd,bkhd->bhqk', q_block(q, i), k, preferred_element_type=F32) * scale
        sc = sc + q_block(cum, i, axis=2)[..., :, None] - cum[..., None, :]
        sc = jnp.where(frame_causal_mask(i, seq), sc, NEG_INF)
        p = jax.nn.softmax(sc, axis=-1).astype(v.dtype)
        return jnp.einsum('bhqk,bkhd->bqhd', p, v)

    return sweep_query_blocks(block, seq)

def mixer_sublayer(h, cos_m, sin_m, cos_d, sin_d, w_in, mla_q_norm_g, mla_kv_norm_g, mla_w_uq, mla_w_ukv,
                   diff_lam_q1, diff_lam_k1, diff_lam_q2, diff_lam_k2, diff_subln_g, lam_init, fox_f_bias, w_out):
    b, seq, _ = h.shape
    proj = h @ w_in
    parts = []
    start = 0
    for width in IN_SPLITS:
        parts.append(proj[..., start:start + width])
        start += width
    c_q, c_kv, k_rope, dq, dk, dv, fq, fk, fv, ff = parts
    o_mla = mla_attention(c_q, c_kv, k_rope, mla_q_norm_g, mla_kv_norm_g, mla_w_uq, mla_w_ukv, cos_m, sin_m)
    o_diff = diff_attention(dq, dk, dv, diff_lam_q1, diff_lam_k1, diff_lam_q2, diff_lam_k2,
                            diff_subln_g, lam_init, cos_d, sin_d)
    o_fox = forgetting_attention(fq, fk, fv, ff, fox_f_bias)
    o = jnp.concatenate([o_mla.reshape(b, seq, -1), o_diff.reshape(b, seq, -1),
                         o_fox.reshape(b, seq, -1)], axis=-1)
    return o @ w_out

def grouped_moe(h, router_w, router_bias, w_gate, w_up, w_down):
    n = h.shape[0]
    scores = jax.nn.sigmoid(jnp.einsum('nd,de->ne', h, router_w, preferred_element_type=F32))
    biased = (scores + router_bias.astype(F32)).reshape(n, N_GROUPS, GROUP_SIZE)
    group_score = jnp.sum(lax.top_k(biased, TOP_K)[0], axis=-1)
    group_sel = jnp.argmax(group_score, axis=-1)
    in_group = group_sel[:, None] == jnp.arange(N_GROUPS)[None, :]
    cand = jnp.where(in_group[:, :, None], biased, NEG_INF).reshape(n, N_EXPERTS)
    _, idx = lax.top_k(cand, TOP_K)
    sel = jnp.take_along_axis(scores, idx, axis=-1)
    gates = sel / jnp.sum(sel, axis=-1, keepdims=True)
    dense_gates = jnp.einsum('nk,nke->ne', gates, jax.nn.one_hot(idx, N_EXPERTS, dtype=F32)).astype(h.dtype)
    y = jnp.zeros_like(h)
    for e in range(N_EXPERTS):
        a = jax.nn.silu(h @ w_gate[e]) * (h @ w_up[e])
        y = y + dense_gates[:, e:e + 1] * (a @ w_down[e])
    return y

def second_inputs(seed: int = 0) -> dict:
    key = jax.random.key(seed)
    ks = jax.random.split(key, 24)

    def nrm(k, shape, scale):
        return jax.random.normal(k, shape, F32) * scale

    def gain(k, shape):
        return 1.0 + nrm(k, shape, 0.02)

    x = nrm(ks[0], (BATCH, SEQ, D_MODEL), 1.0)
    offsets = jax.random.randint(ks[1], (BATCH, 1), 0, 64, dtype=jnp.int32) * CHUNK
    positions = offsets + jnp.arange(SEQ, dtype=jnp.int32)[None, :]
    return {
        "x": x,
        "positions": positions,
        "ln_in_g": gain(ks[2], (D_MODEL,)),
        "ln_in_b": nrm(ks[3], (D_MODEL,), 0.02),
        "w_in": nrm(ks[4], (DEPTH, D_MODEL, IN_COLS), D_MODEL ** -0.5),
        "mla_q_norm_g": gain(ks[5], (DEPTH, MLA_Q_RANK)),
        "mla_kv_norm_g": gain(ks[6], (DEPTH, MLA_KV_RANK)),
        "mla_w_uq": nrm(ks[7], (DEPTH, MLA_Q_RANK, MLA_HEADS * (MLA_NOPE + MLA_ROPE)), MLA_Q_RANK ** -0.5),
        "mla_w_ukv": nrm(ks[8], (DEPTH, MLA_KV_RANK, MLA_HEADS * (MLA_NOPE + MLA_V)), MLA_KV_RANK ** -0.5),
        "diff_lam_q1": nrm(ks[9], (DEPTH, DIFF_QK), 0.1),
        "diff_lam_k1": nrm(ks[10], (DEPTH, DIFF_QK), 0.1),
        "diff_lam_q2": nrm(ks[11], (DEPTH, DIFF_QK), 0.1),
        "diff_lam_k2": nrm(ks[12], (DEPTH, DIFF_QK), 0.1),
        "diff_subln_g": gain(ks[13], (DEPTH, DIFF_V)),
        "fox_f_bias": jax.random.uniform(ks[14], (DEPTH, FOX_HEADS), F32, 1.0, 4.0),
        "w_out": nrm(ks[15], (DEPTH, D_MIX, D_MODEL), D_MIX ** -0.5 * DEEPNORM_BETA),
        "ln1_g": gain(ks[16], (DEPTH, D_MODEL)),
        "ln1_b": nrm(ks[17], (DEPTH, D_MODEL), 0.02),
        "router_w": nrm(ks[18], (D_MODEL, N_EXPERTS), D_MODEL ** -0.5),
        "router_bias": nrm(ks[19], (N_EXPERTS,), 0.01),
        "exp_w_gate": nrm(ks[20], (DEPTH, N_EXPERTS, D_MODEL, D_EXPERT), D_MODEL ** -0.5),
        "exp_w_up": nrm(ks[21], (DEPTH, N_EXPERTS, D_MODEL, D_EXPERT), D_MODEL ** -0.5),
        "exp_w_down": nrm(ks[22], (DEPTH, N_EXPERTS, D_EXPERT, D_MODEL), D_EXPERT ** -0.5 * DEEPNORM_BETA),
        "ln2_g": gain(ks[23], (DEPTH, D_MODEL)),
        "ln2_b": nrm(jax.random.fold_in(ks[23], 1), (DEPTH, D_MODEL), 0.02),
    }

def second_block(x, positions, ln_in_g, ln_in_b, w_in, mla_q_norm_g, mla_kv_norm_g, mla_w_uq, mla_w_ukv,
              diff_lam_q1, diff_lam_k1, diff_lam_q2, diff_lam_k2, diff_subln_g, fox_f_bias, w_out,
              ln1_g, ln1_b, router_w, router_bias, exp_w_gate, exp_w_up, exp_w_down, ln2_g, ln2_b):
    b, seq, d = x.shape
    cos_m, sin_m = rope_tables(positions, MLA_ROPE)
    cos_d, sin_d = rope_tables(positions, DIFF_ROT)
    h = layer_norm(x, ln_in_g, ln_in_b)
    for l in range(DEPTH):
        lam_init = 0.8 - 0.6 * math.exp(-0.3 * l)
        mix = mixer_sublayer(h, cos_m, sin_m, cos_d, sin_d, w_in[l], mla_q_norm_g[l], mla_kv_norm_g[l],
                             mla_w_uq[l], mla_w_ukv[l], diff_lam_q1[l], diff_lam_k1[l], diff_lam_q2[l],
                             diff_lam_k2[l], diff_subln_g[l], lam_init, fox_f_bias[l], w_out[l])
        h = layer_norm(DEEPNORM_ALPHA * h + mix, ln1_g[l], ln1_b[l])
        ffn = grouped_moe(h.reshape(b * seq, d), router_w, router_bias,
                          exp_w_gate[l], exp_w_up[l], exp_w_down[l]).reshape(b, seq, d)
        h = layer_norm(DEEPNORM_ALPHA * h + ffn, ln2_g[l], ln2_b[l])
    return h


def setup_inputs(seed=0):
    out = dict(first_inputs(seed))
    for name, value in second_inputs(seed + 1).items():
        if name != "x":
            out[name + "_2"] = value
    return out


def reference(
    x, c, positions, norm1_w, norm2_w, w_ada, b_ada, w_in, pool_w, pool_scale, conv_w, q_norm_w,
    k_norm_w, p_pool, p_conv, p_attn, w_out, w_gate, w_up, w_down, positions_2, ln_in_g_2,
    ln_in_b_2, w_in_2, mla_q_norm_g_2, mla_kv_norm_g_2, mla_w_uq_2, mla_w_ukv_2, diff_lam_q1_2,
    diff_lam_k1_2, diff_lam_q2_2, diff_lam_k2_2, diff_subln_g_2, fox_f_bias_2, w_out_2, ln1_g_2,
    ln1_b_2, router_w_2, router_bias_2, exp_w_gate_2, exp_w_up_2, exp_w_down_2, ln2_g_2,
    ln2_b_2,
):
    x = first_block(
        x, c, positions, norm1_w, norm2_w, w_ada, b_ada, w_in, pool_w, pool_scale, conv_w,
        q_norm_w, k_norm_w, p_pool, p_conv, p_attn, w_out, w_gate, w_up, w_down,
    )
    return second_block(
        x, positions_2, ln_in_g_2, ln_in_b_2, w_in_2, mla_q_norm_g_2, mla_kv_norm_g_2,
        mla_w_uq_2, mla_w_ukv_2, diff_lam_q1_2, diff_lam_k1_2, diff_lam_q2_2, diff_lam_k2_2,
        diff_subln_g_2, fox_f_bias_2, w_out_2, ln1_g_2, ln1_b_2, router_w_2, router_bias_2,
        exp_w_gate_2, exp_w_up_2, exp_w_down_2, ln2_g_2, ln2_b_2,
    )


_drawn_inputs = setup_inputs


def setup_inputs(seed=0):
    import zlib

    import numpy as np

    out = dict(_drawn_inputs(seed))
    spreads = {}
    factors = {'q_norm_w': 4.896,
     'k_norm_w': 3.933,
     'mla_q_norm_g_2': 8.0,
     'mla_kv_norm_g_2': 6.269,
     'diff_lam_q1_2': 3.51,
     'diff_lam_k1_2': 6.007,
     'diff_subln_g_2': 2.831}
    for name, (base, spread) in spreads.items():
        noise = np.random.default_rng([zlib.crc32(name.encode()), seed]).standard_normal(out[name].shape)
        drawn = base * np.exp(spread * noise) if base else spread * noise
        out[name] = jnp.asarray(drawn.astype(out[name].dtype))
    for name, factor in factors.items():
        out[name] = (out[name] * factor).astype(out[name].dtype)
    return out
```

```python
from contextlib import ExitStack

import numpy as np

import concourse.bass as bass
from concourse import mybir

F32 = mybir.dt.float32
F32R = mybir.dt.float32r
I32 = mybir.dt.int32
ALU = mybir.AluOpType
ACT = mybir.ActivationFunctionType
AX = mybir.AxisListType

P = 128
T = 256
D = 1024
KD = D // P
NT = T // P
LAYERS = 2
COLS = 512
UNITS = 4 * COLS
RAW = 3
SPLIT = 3
EPS = 1e-6

HEADS = 8
HD = 64
ROT = 16
WIN = (2, 4, 8, 16)
FF = 2816
FF_CHUNKS = FF // P
FF_BLOCKS = -(-FF // COLS)

WIN_COLS = [1024, 1536, 2048, 0, 512] + [2560 + COLS * j for j in range(6)]
WIN_JOBS = len(WIN_COLS)

S_WIN = 0
S_BR = S_WIN + 2 * WIN_JOBS
S_OUT = S_BR + 4
S_FF = S_OUT + 4
S_DOWN = S_FF + 4 * FF_BLOCKS
S_LAYER = S_DOWN + FF_CHUNKS // 2 + 1
assert S_LAYER % SPLIT == 0

ADA = 4
AFTER = {s: 1 for s in range(12)}
AFTER.update({S_FF + s: 1 for s in range(4)})


def ring_order():
    order = [("ada", a) for a in range(2 * ADA)]
    a = 2 * ADA
    for s in range(S_LAYER):
        order.append(("split", s))
        if s in AFTER:
            order.append(("ada", a))
            a += 1
    assert a == 6 * ADA and len(order) % RAW == 0
    return order


RING1 = ring_order()
G_LAYER = len(RING1)
G_OF = {item: g for g, item in enumerate(RING1)}

J_BR = WIN_JOBS
J_OUT = J_BR + 6
J_FF = J_OUT + 2
J_DOWN = J_FF + 2 * FF_BLOCKS
J_LAYER = J_DOWN + 2
PAIR_USES = ((J_LAYER + 1) // 2, J_LAYER // 2)

X_NORM1, X_POOL, X_CONV, X_ATT, X_MERGE, X_NORM2, X_ACT = 0, 4, 5, 6, 8, 12, 16
X_LAYER = X_ACT + FF_CHUNKS // 2

CHAIN = 1024

PC_BADA, PC_N1, PC_N2, PC_PS, PC_CW, PC_LAYER = 0, 48, 56, 64, 66, 72
PC_ROWS = PC_LAYER + KD
PAD = 16


IN2 = 2212
CQ, CKV, KR = 384, 256, 32
C_KR, C_DQ, C_DK, C_DV, C_FQ, C_FK, C_FV, C_FF = 640, 672, 928, 1184, 1440, 1696, 1952, 2208
MH, MQ, MN = 8, 96, 64
DH, DW, DROT = 4, 32, 8
FH, FW = 4, 66
NE, FE = 16, 512
ALPHA = (2 * LAYERS) ** 0.25
LN_EPS = 1e-5
IN2_JOBS = -(-IN2 // COLS)
S2_UQ = 2 * IN2_JOBS
S2_UKV = S2_UQ + 2
S2_OUT = S2_UKV + 2
S2_MOE = S2_OUT + 4
S2_LAYER = S2_MOE + 6 * NE
assert S2_MOE % SPLIT == 0 and 6 % SPLIT == 0 and SPLIT == RAW
J2_UQ = IN2_JOBS
J2_UKV = J2_UQ + 2
J2_OUT = J2_UKV + 2
J2_MOE = J2_OUT + 2
J2_LAYER = J2_MOE + 4 * NE
PAIR2_USES = ((J2_LAYER + 1) // 2, J2_LAYER // 2)
X2_IN, X2_MLA, X2_O, X2_MOE = 0, 4, 7, 15
X2_H = 11
X2_LAYER = X2_MOE + 2 * NE
AJ = MH + 2 * DH + FH
CHAIN2 = 2048


def job2_end(q):
    if q < J2_UQ:
        return 2 * q + 1
    return S2_UQ + q - J2_UQ if q < J2_OUT else S2_OUT + 2 * (q - J2_OUT) + 1


class Count:

    def __init__(self, sem, per, prime=0, per2=0):
        self.sem, self.per, self.prime, self.per2 = sem, per, prime, per2

    def at(self, l, k):
        return self.sem, l * self.per + (k + self.prime)

    def at2(self, l, k):
        return self.sem, l * self.per2 + (k + self.prime + LAYERS * self.per)


def group_jobs(s):
    if s < S_BR:
        h = s % 2
        return [(s // 2, 0, COLS, [(i, 4 * h + i) for i in range(4)], h == 0, h == 1, "xt")]
    if s < S_BR + 2:
        b = s - S_BR
        return [(J_BR + 2 * b + n, COLS * n, COLS, [(i, 2 * b + i) for i in range(2)], True, True, "bt") for n in range(2)]
    if s < S_OUT:
        return [(J_BR + 4 + s - S_BR - 2, 0, COLS, [(i, 4 + i) for i in range(4)], True, True, "bt")]
    if s < S_FF:
        j, h = divmod(s - S_OUT, 2)
        return [(J_OUT + j, 0, COLS, [(i, 4 * h + i) for i in range(4)], h == 0, h == 1, "xt")]
    if s < S_DOWN:
        j, h = divmod(s - S_FF, 2)
        return [(J_FF + j, 0, min(COLS, FF - COLS * (j // 2)), [(i, 4 * h + i) for i in range(4)], h == 0, h == 1, "xt")]
    first, units = down_chunks(s - S_DOWN)
    return [(J_DOWN + n, COLS * n, COLS, [(i, first + i) for i in range(units)], s == S_DOWN, s == S_LAYER - 1, "at")
            for n in range(2)]


def down_chunks(i):
    full = FF_CHUNKS // 2 - 1
    return (2 * i, 2) if i < full else (2 * full + i - full, 1)


JOB_END = {q: s for s in range(S_LAYER) for q, _, _, _, _, last, _ in group_jobs(s) if last}


def constants():
    ident = np.eye(P, dtype=np.float32)
    causal = np.where(np.arange(P)[None, :] <= np.arange(P)[:, None], 0.0, -1e30).astype(np.float32)
    mask = np.concatenate([causal, np.zeros((P, P), np.float32), causal], axis=1)
    count = np.zeros((P, 2, T), np.float32)
    for g, w in enumerate(WIN):
        count[64 * (g % 2):64 * (g % 2) + 64, g // 2, :] = np.float32(1.0) / np.minimum(np.arange(T) + 1, w).astype(np.float32)
    chunk = np.where(np.arange(P)[None, :] // 64 <= np.arange(P)[:, None] // 64, 0.0, -1e30).astype(np.float32)
    mask2 = np.concatenate([chunk, np.zeros((P, P), np.float32), chunk], axis=1)
    tri = (np.arange(P)[:, None] <= np.arange(P)[None, :]).astype(np.float32)
    freq = np.concatenate([np.float32(500000.0) ** (-np.arange(0, r, 2, dtype=np.float32) / np.float32(r))
                           for r in (ROT, KR, DROT)]).astype(np.float32)
    i, j = np.arange(4)[:, None], np.arange(4)[None, :]
    order = np.stack([(j < i), (j > i)]).astype(np.float32).reshape(32)
    lam = np.array([[0.8 - 0.6 * np.exp(-0.3 * l), 1 - (0.8 - 0.6 * np.exp(-0.3 * l))] for l in range(LAYERS)]).astype(np.float32)

    def rows(a):
        return np.ascontiguousarray(np.broadcast_to(a.reshape(-1), (P, a.size)))

    return {"c_ident": ident, "c_mask": mask, "c_mask2": mask2, "c_tri": tri, "c_count": count.reshape(P, 2 * T),
            "c_freq": rows(freq), "c_order": rows(order), "c_lam": rows(lam)}


def program(nc, A, out):
    with ExitStack() as top:
        def sb(name, shape, dt=F32, ctx=top):
            return ctx.enter_context(nc.sbuf_tensor(name, shape, dt))

        def sem(name):
            return top.enter_context(nc.semaphore(name))

        def counted(name, per, prime=0, per2=0):
            return Count(sem(name), per, prime, per2)

        gp = top.enter_context(nc.psum_tensor("gp", [P, 2, NT, COLS], F32))
        mp = top.enter_context(nc.psum_tensor("mp", [P, 4, COLS], F32))

        raw = sb("raw", [P, RAW, UNITS])
        whi = sb("whi", [P, SPLIT, UNITS], F32R)
        wlo = sb("wlo", [P, SPLIT, UNITS], F32R)
        x = sb("x", [P, NT, D])
        xt_hi = sb("xt_hi", [P, KD, T], F32R)
        xt_lo = sb("xt_lo", [P, KD, T], F32R)
        ft = sb("ft", [P, 2, 2 * T])
        ident = sb("ident", [P, P])
        ones = sb("ones", [P, P])
        mask = sb("mask", [P, 3 * P])
        NF = (ROT + KR + DROT) // 2
        freq = sb("freq", [P, NF])
        order = sb("order", [P, 2, 16])
        lamc = sb("lamc", [P, LAYERS, 2])
        posi = sb("posi", [P, 2, NT], I32)
        posf = sb("posf", [P, 2, NT])
        ang = sb("ang", [P, NT, 2, NF])
        angk = sb("angk", [P, NT, 2, NF])
        cos2, sin2 = ([sb(f"{n}{r}", [P, NT, r]) for r in (ROT, KR, DROT)] for n in ("cos", "sin"))
        rv = sb("rv", [P, 32])
        rs = sb("rs", [P, 32])
        rr = sb("rr", [P, 32])
        rt = sb("rt", [P, 32])
        ssq = sb("ssq", [P, NT])

        one = ExitStack()
        acc = sb("acc", [P, 2, D], ctx=one)
        grow = sb("grow", [P, 2, D], ctx=one)
        count = sb("count", [P, 2, T], ctx=one)
        stage = sb("stage", [PC_ROWS, LAYERS, P], ctx=one)
        pcol = sb("pcol", [P, LAYERS, PC_ROWS], ctx=one)
        pcur = sb("pcur", [P, PC_LAYER], ctx=one)
        cact = sb("cact", [P, KD], ctx=one)
        csig = sb("csig", [P, KD], ctx=one)
        qkw = sb("qkw", [P, LAYERS, 2, HD], ctx=one)
        qkcur = sb("qkcur", [P, 2, HD], ctx=one)
        poolcur = sb("poolcur", [P, 2, P], ctx=one)
        poolw = sb("poolw", [P, LAYERS, 2, P], ctx=one)
        modc = sb("modc", [P, 6, KD], ctx=one)
        scol = sb("scol", [P, 2, KD], ctx=one)
        mix = ExitStack()
        u = sb("u", [P, NT, 5 * COLS], ctx=mix)
        gl = sb("gl", [P, NT, 6 * COLS], ctx=mix)
        qt = sb("qt", [P, 4, T], ctx=mix)
        kt = sb("kt", [P, 4, T], ctx=mix)
        bt_hi = sb("bt_hi", [P, 8, T], F32R, ctx=mix)
        bt_lo = sb("bt_lo", [P, 8, T], F32R, ctx=mix)
        sc = sb("sc", [P, 2, 3 * P], ctx=mix)
        pt = sb("pt", [P, 3 * P], ctx=mix)
        nmax = sb("nmax", [P, 2, NT], ctx=mix)
        rsum = sb("rsum", [P, 2, NT], ctx=mix)
        rinv = sb("rinv", [P, 2, NT], ctx=mix)
        w1 = sb("w1", [P, 2, PAD + T], ctx=mix)
        pp, zp, w2 = (u[:, :, 3 * COLS + i * (PAD + T):3 * COLS + (i + 1) * (PAD + T)] for i in range(3))
        bg = sb("bg", [P, 2, T], ctx=mix)
        mix.close()
        ffn = ExitStack()
        at_hi = sb("at_hi", [P, FF_CHUNKS, T], F32R, ctx=ffn)
        at_lo = sb("at_lo", [P, FF_CHUNKS, T], F32R, ctx=ffn)
        sg = sb("sg", [P, NT, COLS], ctx=ffn)
        ab = sb("ab", [P, NT, COLS], ctx=ffn)
        xn2 = sb("xn2", [P, NT, D], ctx=ffn)
        ffn.close()
        one.close()

        two = ExitStack()
        mask2 = sb("mask2", [P, 3 * P], ctx=two)
        tri = sb("tri", [P, P], ctx=two)
        lnw = sb("lnw", [P, 2, D], ctx=two)
        cen = sb("cen", [P, NT, D], ctx=two)
        lsum = sb("lsum", [P, NT], ctx=two)
        lsum4 = sb("lsum4", [P, 2 * NT], ctx=two)
        mean = sb("mean", [P, NT], ctx=two)
        cg = sb("cg", [P, LAYERS, CQ + CKV], ctx=two)
        lamr = sb("lamr", [P, LAYERS, 4, DW], ctx=two)
        subg = sb("subg", [P, LAYERS, HD], ctx=two)
        fbias = sb("fbias", [P, LAYERS, FH], ctx=two)
        rw = sb("rw", [P, KD, NE], ctx=two)
        rw_hi = sb("rw_hi", [P, KD, NE], F32R, ctx=two)
        rw_lo = sb("rw_lo", [P, KD, NE], F32R, ctx=two)
        rbias = sb("rbias", [P, NE], ctx=two)
        cgc = sb("cgc", [P, CQ + CKV], ctx=two)
        subc = sb("subc", [P, HD], ctx=two)
        lamt = sb("lamt", [P, 2, DW], ctx=two)
        lame = sb("lame", [P, 2], ctx=two)
        nlam = sb("nlam", [P, 1], ctx=two)
        lamq = sb("lamq", [P, 4, DW], ctx=two)
        lami = sb("lami", [P, 1], ctx=two)
        fbc = sb("fbc", [P, FH], ctx=two)
        pr = sb("pr", [P, NT, IN2], ctx=two)
        mt_hi = sb("mt_hi", [P, 6, T], F32R, ctx=two)
        mt_lo = sb("mt_lo", [P, 6, T], F32R, ctx=two)
        qm = sb("qm", [P, NT, MH, MQ], ctx=two)
        km = sb("km", [P, NT, MH, MQ], ctx=two)
        vm = sb("vm", [P, NT, MH, HD], ctx=two)
        fq = sb("fq", [P, NT, FH, FW], ctx=two)
        fk = sb("fk", [P, NT, FH, FW], ctx=two)
        rt1 = sb("rt1", [P, NT * MH * KR], ctx=two)
        rt2 = sb("rt2", [P, NT * MH * KR], ctx=two)
        od = sb("od", [P, NT, DH * HD], ctx=two)
        qkt = sb("qkt", [P, 2, 4 * P], ctx=two)
        sc2 = sb("sc2", [P, 2, 3 * P], ctx=two)
        pt2 = sb("pt2", [P, 3 * P], ctx=two)
        nmax2 = sb("nmax2", [P, 2, NT], ctx=two)
        rsum2 = sb("rsum2", [P, 2, NT], ctx=two)
        rinv2 = sb("rinv2", [P, 2, NT], ctx=two)
        fz = sb("fz", [P, NT, FH], ctx=two)
        fe = sb("fe", [P, NT, FH], ctx=two)
        fl = sb("fl", [P, NT, FH], ctx=two)
        rsc = sb("rsc", [P, NT, NE], ctx=two)
        rb = sb("rb", [P, NT, NE], ctx=two)
        cmp1 = sb("cmp1", [P, 8, 16], ctx=two)
        cmp2 = sb("cmp2", [P, 8, 16], ctx=two)
        rank = sb("rank", [P, 8, 4], ctx=two)
        gs = sb("gs", [P, 8], ctx=two)
        gr = sb("gr", [P, 8], ctx=two)
        den = sb("den", [P, NT], ctx=two)
        dg = sb("dg", [P, NT, NE], ctx=two)
        two.close()
        sg2, ab2, junk = pr[:, :, 0:COLS], pr[:, :, COLS:2 * COLS], pr[:, :, D:2 * D]
        oa = cen
        xn1 = gl[:, :, 0:D]
        merged = u[:, :, 3 * COLS:5 * COLS]
        o = u[:, :, 0:COLS]
        stationary = {"xt": (xt_hi, xt_lo), "bt": (bt_hi, bt_lo), "at": (at_hi, at_lo)}

        landed = [counted(f"landed{i}", 16 * G_LAYER // RAW, 0, 16 * S2_LAYER // RAW) for i in range(RAW)]
        raw_read = counted("raw_read", G_LAYER, RAW, S2_LAYER)
        hi_done = counted("hi_done", S_LAYER, 0, S2_LAYER)
        w_used = counted("w_used", S_LAYER, SPLIT, S2_LAYER)
        pair_free = [counted(f"pair_free{p}", 2 * PAIR_USES[p], 2, 2 * PAIR2_USES[p]) for p in range(2)]
        consts_in, x_in, params_in, params_t, zeroed = map(sem, ("consts_in", "x_in", "params_in", "params_t", "zeroed"))
        params_ready, csig_ready, ang_ready, rope_ready = map(sem, ("params_ready", "csig_ready", "ang_ready", "rope_ready"))
        acc_done = counted("acc_done", 6)
        acc_read = counted("acc_read", 6, 2)
        mod_taken = counted("mod_taken", 6, 1)
        grow_in = counted("grow_in", 32)
        sq_done = counted("sq_done", 6)
        rv_ready = counted("rv_ready", 3)
        rs_ready = counted("rs_ready", 3)
        rr_ready = counted("rr_ready", 3)
        xn_ready = counted("xn_ready", 4)
        tr_done = counted("tr_done", X_LAYER - 1, 0, X2_LAYER)
        ft_ready = counted("ft_ready", X_LAYER, 0, X2_LAYER)
        ft_hi = counted("ft_hi", X_LAYER, 0, X2_LAYER)
        ft_lo = counted("ft_lo", X_LAYER, 2, X2_LAYER)
        x_final = counted("x_final", 4, 1)
        qk_ready = counted("qk_ready", 1)
        qkt_done = counted("qkt_done", 1)
        qkt_taken = counted("qkt_taken", 4)
        cu_ready = counted("cu_ready", 1)
        pct_done = counted("pct_done", 1)
        pct_taken = counted("pct_taken", 3)
        pads_zero = counted("pads_zero", 2)
        s_done = counted("s_done", HEADS)
        s_max = counted("s_max", HEADS)
        e_done = counted("e_done", 2 * HEADS)
        pt_done = counted("pt_done", HEADS)
        pt_taken = counted("pt_taken", HEADS)
        o_done = counted("o_done", HEADS)
        o_taken = counted("o_taken", HEADS)
        pooled = counted("pooled", 1)
        gates_ready = counted("gates_ready", 6)
        merged_ready = counted("merged_ready", 2)
        silu_done = counted("silu_done", FF_BLOCKS)
        ab_ready = counted("ab_ready", FF_BLOCKS)
        column_0 = sem("column_0")
        lnw_in = counted("lnw_in", 0, 32, 64)
        params2_in, rw_ready, rw_high = map(sem, ("params2_in", "rw_ready", "rw_high"))
        ln_sum = counted("ln_sum", 0, 2, 4)
        ln_cen = counted("ln_cen", 0, 2, 4)
        ln_sq = counted("ln_sq", 0, 2, 4)
        h_ready = counted("h_ready", 0, 2, 4)
        rv2_ready = counted("rv2_ready", 0, 1, 4)
        rs2_ready = counted("rs2_ready", 0, 1, 4)
        mla_sq = counted("mla_sq", 0, 0, 4)
        mla_ready = counted("mla_ready", 0, 0, 1)
        lam_sum = counted("lam_sum", 0, 0, 1)
        lam_exp = counted("lam_exp", 0, 0, 1)
        fz_ready = counted("fz_ready", 0, 0, 1)
        fe_ready = counted("fe_ready", 0, 0, 1)
        fl_ready = counted("fl_ready", 0, 0, 1)
        logf_ready = counted("logf_ready", 0, 0, 1)
        cum_done = counted("cum_done", 0, 0, 1)
        cum_taken = counted("cum_taken", 0, 0, 1)
        diff_ready = counted("diff_ready", 0, 0, 1)
        fox_ready = counted("fox_ready", 0, 0, 1)
        qm_ready = counted("qm_ready", 0, 0, 1)
        km_ready = counted("km_ready", 0, 0, 1)
        t2_done = counted("t2_done", 0, 0, AJ)
        t2_taken = counted("t2_taken", 0, 0, AJ)
        s2_done = counted("s2_done", 0, 0, AJ)
        s2_max = counted("s2_max", 0, 0, AJ)
        e2_done = counted("e2_done", 0, 0, 2 * AJ)
        p2_done = counted("p2_done", 0, 0, AJ)
        p2_taken = counted("p2_taken", 0, 0, AJ)
        o2_done = counted("o2_done", 0, 0, AJ)
        o2_taken = counted("o2_taken", 0, 0, AJ)
        od_sq = counted("od_sq", 0, 0, 1)
        oa_ready = counted("oa_ready", 0, 0, 1)
        logits_done = counted("logits_done", 0, 0, 1)
        rsc_ready = counted("rsc_ready", 0, 0, 1)
        silu2_done = counted("silu2_done", 0, 0, NE)
        ab2_ready = counted("ab2_ready", 0, 0, NE)
        x2_sum = counted("x2_sum", 0, 0, 2)
        y_taken = counted("y_taken", 0, 0, 2 * NE)
        out_done = sem("out_done")
        rows_free = sem("rows_free")
        v_chain = sem("v_chain")
        v_moe = sem("v_moe")

        block = top.enter_context(nc.Block())

        def weights(item, l):
            kind, n = item
            if kind == "ada":
                vec, i = divmod(n, ADA)
                return A["w_ada"][l, 2 * P * i:2 * P * (i + 1), D * vec:D * (vec + 1)], 2, D
            h = n % 2
            if n < S_BR:
                c = WIN_COLS[n // 2]
                return A["w_in"][l, 4 * P * h:4 * P * (h + 1), c:c + COLS], 4, COLS
            if n < S_BR + 2:
                return A[("p_pool", "p_conv")[n - S_BR]][l, :, :], 2, D
            if n < S_OUT:
                j = n - S_BR - 2
                return A["p_attn"][l, :, COLS * j:COLS * (j + 1)], 4, COLS
            if n < S_FF:
                j = (n - S_OUT) // 2
                return A["w_out"][l, 4 * P * h:4 * P * (h + 1), COLS * j:COLS * (j + 1)], 4, COLS
            if n < S_DOWN:
                j, r = divmod(n - S_FF, 4)
                wide = min(COLS, FF - COLS * j)
                return A["w_gate" if r < 2 else "w_up"][l, 4 * P * h:4 * P * (h + 1), COLS * j:COLS * j + wide], 4, wide
            first, units = down_chunks(n - S_DOWN)
            return A["w_down"][l, P * first:P * (first + units), :], units, D

        def weights2(s, l):
            if s < S2_UQ:
                j, h = divmod(s, 2)
                wide = min(COLS, IN2 - COLS * j)
                return A["w_in_2"][l, 4 * P * h:4 * P * (h + 1), COLS * j:COLS * j + wide], 4, wide
            if s < S2_UKV:
                wide = MH * MQ // 2
                return A["mla_w_uq_2"][l, :, wide * (s - S2_UQ):wide * (s - S2_UQ + 1)], 3, wide
            if s < S2_OUT:
                return A["mla_w_ukv_2"][l, :, COLS * (s - S2_UKV):COLS * (s - S2_UKV + 1)], 2, COLS
            j, h = divmod(s - S2_OUT, 2)
            return A["w_out_2"][l, 4 * P * h:4 * P * (h + 1), COLS * j:COLS * (j + 1)], 4, COLS

        def expert_weights(l, e, i):
            if i < 4:
                return A["exp_w_gate_2" if i < 2 else "exp_w_up_2"][l, e, 4 * P * (i % 2):4 * P * (i % 2 + 1), :]
            return A["exp_w_down_2"][l, e, :, COLS * (i - 4):COLS * (i - 3)]

        def slot(buf, n, units, cols):
            return buf[:, n, 0:units * cols].rearrange("p (k n) -> p k n", k=units)

        def job_width(j):
            return MQ if j < MH else DW if j < MH + 2 * DH else FW

        def job_operands(j):
            if j < MH:
                return qm[:, :, j, :], km[:, :, j, :], vm[:, :, j, :], MQ ** -0.5, mask2
            if j < MH + 2 * DH:
                i = j - MH
                return (pr[:, :, C_DQ + DW * i:C_DQ + DW * (i + 1)], pr[:, :, C_DK + DW * i:C_DK + DW * (i + 1)],
                        pr[:, :, C_DV + HD * (i // 2):C_DV + HD * (i // 2 + 1)], DW ** -0.5, mask2)
            i = j - MH - 2 * DH
            return fq[:, :, i, :], fk[:, :, i, :], pr[:, :, C_FV + HD * i:C_FV + HD * (i + 1)], HD ** -0.5, mask

        GATE_PAIR = J2_MOE % 2

        def chunks(bank):
            return bank.rearrange("p (k t) -> p k t", k=2)

        @block.sync
        def _(sp):
            for name, tile in (("c_ident", ident[:, :]), ("c_mask", mask[:, :]),
                               ("c_count", count[:, :, :].rearrange("p a t -> p (a t)")), ("c_freq", freq[:, :]),
                               ("c_order", order[:, :, :].rearrange("p a n -> p (a n)")),
                               ("c_lam", lamc[:, :, :].rearrange("p l n -> p (l n)"))):
                sp.dma_start(tile, A[name]).then_inc(consts_in, 16)
            sp.dma_start(x[:, :, :], A["x"].rearrange("b (t p) d -> p (b t) d", p=P)).then_inc(x_in, 16)
            with sp.Fori(0, LAYERS) as l:
                for g, item in enumerate(RING1):
                    src, units, cols = weights(item, l)
                    sp.wait_ge(*raw_read.at(l, g + 1 - RAW))
                    if item == ("split", 2 * WIN_COLS.index(0)):
                        sp.sem_inc(column_0, 1)
                    sp.dma_start(slot(raw, g % RAW, units, cols),
                                 src.rearrange("(k p) n -> p k n", p=P)).then_inc(landed[g % RAW].sem, 16)
            with sp.Fori(0, LAYERS) as l:
                def load(n, k, src, units, cols):
                    sp.wait_ge(*raw_read.at2(l, k + 1 - RAW))
                    sp.dma_start(slot(raw, n % RAW, units, cols),
                                 src.rearrange("(k p) n -> p k n", p=P)).then_inc(landed[n % RAW].sem, 16)

                for s in range(S2_MOE):
                    src, units, cols = weights2(s, l)
                    load(s, s, src, units, cols)
                for i in range(4):
                    load(S2_MOE + i, S2_MOE + i, expert_weights(l, 0, i), 4, COLS)
                with sp.Fori(1, NE) as e:
                    for i in range(6):
                        load(S2_MOE + 4 + i, (e - 1) * 6 + (S2_MOE + 4 + i), expert_weights(l, e if i < 4 else e - 1, i), 4, COLS)
                for i in range(4, 6):
                    load(S2_LAYER - 6 + i, S2_LAYER - 6 + i, expert_weights(l, NE - 1, i), 4, COLS)
            sp.wait_ge(*h_ready.at2(LAYERS, 0))
            sp.dma_start(out.rearrange("b (t p) d -> p (b t) d", p=P), x[:, :, :]).then_inc(out_done, 16)
            sp.wait_ge(out_done, 16)

        @block.gpsimd
        def _(pool):
            pool.memset(ones[:, :], 1.0).then_inc(zeroed, 1)
            pool.memset(poolw[:, :, :, :], 0.0).then_inc(zeroed, 1)
            pool.wait_ge(zeroed, 2)
            for l in range(LAYERS):
                rows = ((A["b_ada"][l], PC_BADA, 48), (A["norm1_w"][l], PC_N1, KD), (A["norm2_w"][l], PC_N2, KD),
                        (A["pool_scale"][l], PC_PS, 2), (A["c"][0], PC_LAYER, KD))
                for src, at, n in rows:
                    pool.dma_start(stage[at:at + n, l, :], src.rearrange("(a p) -> a p", p=P)).then_inc(params_in, 16)
                pool.dma_start(stage[PC_CW:PC_CW + 6, l, :],
                               A["conv_w"][l].rearrange("k (a p) -> (k a) p", p=P)).then_inc(params_in, 16)
                for i, name in enumerate(("q_norm_w", "k_norm_w")):
                    pool.dma_start(qkw[:, l, i, :], A[name][l].partition_broadcast(P)).then_inc(params_in, 16)
                for g in range(4):
                    h = 64 * (g % 2)
                    pool.dma_start(poolw[h:h + 64, l, g // 2, h:h + 64], A["pool_w"][l, g, :, :]).then_inc(params_in, 16)
            for i, name in enumerate(("positions", "positions_2")):
                for t in range(NT):
                    pool.dma_start(posi[:, i, t:t + 1],
                                   A[name][0, P * t:P * (t + 1)].rearrange("(p a) -> p a", a=1)).then_inc(params_in, 16)
            with pool.Fori(0, LAYERS) as l:
                pool.wait_ge(*x_final.at(l, 0))
                for i, vec in enumerate((2, 5)):
                    pool.dma_start(grow[:, i, :],
                                   A["b_ada"][l, D * vec:D * (vec + 1)].partition_broadcast(P)).then_inc(grow_in.sem, 16)
            pool.wait_ge(*x_final.at(LAYERS, 0))

            def norm_rows(gain, bias):
                pool.dma_start(lnw[:, 0, :], gain.partition_broadcast(P)).then_inc(lnw_in.sem, 16)
                pool.dma_start(lnw[:, 1, :], bias.partition_broadcast(P)).then_inc(lnw_in.sem, 16)

            norm_rows(A["ln_in_g_2"], A["ln_in_b_2"])
            pool.dma_start(mask2[:, :], A["c_mask2"]).then_inc(params2_in, 16)
            pool.dma_start(tri[:, :], A["c_tri"]).then_inc(params2_in, 16)
            for l in range(LAYERS):
                for dst, src in ((cg[:, l, 0:CQ], A["mla_q_norm_g_2"]), (cg[:, l, CQ:CQ + CKV], A["mla_kv_norm_g_2"]),
                                 (lamr[:, l, 0, :], A["diff_lam_q1_2"]), (lamr[:, l, 1, :], A["diff_lam_q2_2"]),
                                 (lamr[:, l, 2, :], A["diff_lam_k1_2"]), (lamr[:, l, 3, :], A["diff_lam_k2_2"]),
                                 (subg[:, l, :], A["diff_subln_g_2"]), (fbias[:, l, :], A["fox_f_bias_2"])):
                    pool.dma_start(dst, src[l].partition_broadcast(P)).then_inc(params2_in, 16)
            pool.dma_start(rw[:, :, :], A["router_w_2"].rearrange("(k p) n -> p k n", p=P)).then_inc(params2_in, 16)
            pool.dma_start(rbias[:, :], A["router_bias_2"].partition_broadcast(P)).then_inc(params2_in, 16)
            with pool.Fori(0, LAYERS) as l:
                pool.wait_ge(*h_ready.at2(l, 0))
                pool.sem_inc(rows_free, 1)
                norm_rows(A["ln1_g_2"][l], A["ln1_b_2"][l])
                pool.wait_ge(*h_ready.at2(l, 2))
                pool.sem_inc(rows_free, 1)
                norm_rows(A["ln2_g_2"][l], A["ln2_b_2"][l])

        PARAMS = 16 * (LAYERS * 12 + 2 * NT)
        PARAMS2 = 16 * (LAYERS * 8 + 4)

        @block.scalar
        def _(act):
            act.wait_ge(params_ready, LAYERS)
            act.activation(csig[:, :], pcol[:, 0, PC_LAYER:PC_ROWS], ACT.Sigmoid).then_inc(csig_ready, 1)
            act.wait_ge(ang_ready, 1)
            act.activation(angk[:, :, :, :], ang[:, :, :, :], ACT.Sin).then_inc(rope_ready, 1)
            act.wait_ge(x_in, 16)

            with act.Fori(0, LAYERS) as l:
                def split(s):
                    g = G_OF["split", s]
                    _, units, cols = weights(("split", s), l)
                    act.wait_ge(*landed[g % RAW].at(l, 16 * (g // RAW + 1)))
                    act.wait_ge(*w_used.at(l, s + 1 - SPLIT))
                    act.activation(slot(whi, s % SPLIT, units, cols), slot(raw, g % RAW, units, cols),
                                   ACT.Copy).then_inc(hi_done.sem, 1)

                def high(f, dst):
                    act.wait_ge(*ft_ready.at(l, f + 1))
                    act.activation(dst, chunks(ft[:, f % 2, :]), ACT.Copy).then_inc(ft_hi.sem, 1)

                def root(i, n):
                    act.wait_ge(*rv_ready.at(l, i + 1))
                    act.activation(rs[:, 0:n], rv[:, 0:n], ACT.Sqrt).then_inc(rs_ready.sem, 1)

                def normalise(xn, i):
                    for t in range(NT):
                        act.activation(xn[:, t, :], x[:, t, :], ACT.Square, accum_out=ssq[:, t:t + 1]).then_inc(sq_done.sem, 1)
                    root(i, NT)
                    act.wait_ge(*rr_ready.at(l, i + 1))
                    for t in range(NT):
                        act.activation(xn[:, t, :], x[:, t, :], ACT.Copy, scale=rr[:, t:t + 1]).then_inc(xn_ready.sem, 1)

                def take_w_in(j):
                    act.wait_ge(*w_used.at(l, JOB_END[j] + 1))
                    if j < 5:
                        act.activation(u[:, 0, COLS * j:COLS * (j + 1)], gp[:, j % 2, 0, :], ACT.Copy).then_inc(pair_free[j % 2].sem, 1)
                    else:
                        act.activation(gl[:, :, COLS * (j - 5):COLS * (j - 4)], gp[:, j % 2, :, :], ACT.Copy).then_inc(pair_free[j % 2].sem, 2)

                act.wait_ge(*x_final.at(l, 0))
                normalise(xn1, 0)
                split(0)
                split(1)
                for b in range(4):
                    high(X_NORM1 + b, xt_hi[:, 2 * b:2 * b + 2, :])
                for s in range(10):
                    split(s + 2)
                    if s % 2:
                        take_w_in(s // 2)
                    if s == 5:
                        act.wait_ge(*pair_free[0].at(l, 2))
                        act.wait_ge(*pair_free[1].at(l, 2))
                        for t in range(NT):
                            act.activation(gl[:, t, 0:D], u[:, t, 0:D], ACT.Square).then_inc(sq_done.sem, 1)
                        root(1, 2 * NT * HEADS)
                for i in range(12):
                    split(10 + i + 2)
                    if i % 2:
                        take_w_in(5 + i // 2)
                    if i == 0:
                        act.wait_ge(*qkt_done.at(l, 1))
                        for b in range(4):
                            dst = (qt, kt)[b // 2][:, 2 * (b % 2):2 * (b % 2) + 2, :]
                            act.activation(dst, chunks(mp[:, b, :]), ACT.Copy).then_inc(qkt_taken.sem, 1)
                    if i == 1:
                        act.wait_ge(*pct_done.at(l, 1))
                        for b, dst in enumerate((pp[:, :, PAD:PAD + T], zp[:, :, PAD:PAD + T], bg[:, :, :])):
                            act.activation(dst, chunks(mp[:, b, :]), ACT.Copy).then_inc(pct_taken.sem, 1)
                    h = i - 2
                    if 0 <= h < HEADS:
                        act.wait_ge(*s_max.at(l, h + 1))
                        for t, (a, b) in enumerate(((0, P), (P, 3 * P))):
                            act.activation(sc[:, h % 2, a:b], sc[:, h % 2, a:b], ACT.Exp, bias=nmax[:, h % 2, t:t + 1],
                                           accum_out=rsum[:, h % 2, t:t + 1]).then_inc(e_done.sem, 1)
                    h = i - 3
                    if 0 <= h < HEADS:
                        act.wait_ge(*pt_done.at(l, h + 1))
                        act.activation(pt[:, :], mp[:, 2, 0:3 * P], ACT.Copy).then_inc(pt_taken.sem, 1)
                high(X_POOL, bt_hi[:, 0:2, :])
                high(X_CONV, bt_hi[:, 2:4, :])
                for i in range(6):
                    act.wait_ge(*pair_free[(5 + i) % 2].at(l, 2 * ((5 + i) // 2) + 2))
                    act.activation(gl[:, :, COLS * i:COLS * (i + 1)], gl[:, :, COLS * i:COLS * (i + 1)], ACT.Sigmoid).then_inc(gates_ready.sem, 1)
                    if i == 1:
                        for b in range(2):
                            high(X_ATT + b, bt_hi[:, 4 + 2 * b:6 + 2 * b, :])
                for s in range(S_BR, S_OUT):
                    split(s + 2)
                for b in range(4):
                    high(X_MERGE + b, xt_hi[:, 2 * b:2 * b + 2, :])
                for s in range(S_OUT, S_FF):
                    split(s + 2)
                act.wait_ge(*x_final.at(l, 2))
                normalise(xn2, 2)
                for b in range(4):
                    high(X_NORM2 + b, xt_hi[:, 2 * b:2 * b + 2, :])
                for s in range(S_FF, S_DOWN):
                    split(s + 2)
                    j, r = divmod(s - S_FF, 4)
                    wide = min(COLS, FF - COLS * j)
                    if r == 2:
                        if j >= 1:
                            for b in range(2):
                                high(X_ACT + 2 * (j - 1) + b, at_hi[:, 4 * (j - 1) + 2 * b:4 * (j - 1) + 2 * b + 2, :])
                            act.wait_ge(*ab_ready.at(l, j))
                        q = J_FF + 2 * j
                        act.wait_ge(*w_used.at(l, JOB_END[q] + 1))
                        act.activation(sg[:, :, 0:wide], gp[:, q % 2, :, 0:wide], ACT.Silu).then_inc(silu_done.sem, 1)
                for s in range(S_DOWN, S_LAYER - 2):
                    split(s + 2)
                    if s == S_DOWN + 1:
                        high(X_ACT + 2 * (FF_BLOCKS - 1), at_hi[:, FF_CHUNKS - 2:FF_CHUNKS, :])

            def layer_norm(src, wait_sum, wait_cen, root_of):
                for t in range(NT):
                    act.activation(junk[:, t, :], src[:, t, :], ACT.Copy, accum_out=lsum[:, t:t + 1]).then_inc(ln_sum.sem, 1)
                act.wait_ge(*wait_cen)
                act.wait_ge(*wait_sum)
                for t in range(NT):
                    act.activation(junk[:, t, :], cen[:, t, :], ACT.Square, accum_out=ssq[:, t:t + 1]).then_inc(ln_sq.sem, 1)
                act.wait_ge(*root_of)
                act.activation(rs[:, 0:NT], rv[:, 0:NT], ACT.Sqrt).then_inc(rs2_ready.sem, 1)

            act.wait_ge(*x_final.at(LAYERS, 0))
            layer_norm(x, (ln_sum.sem, 2), (ln_cen.sem, 2), (rv2_ready.sem, 1))
            act.wait_ge(params2_in, PARAMS2)
            act.activation(rw_hi[:, :, :], rw[:, :, :], ACT.Copy).then_inc(rw_high, 1)

            with act.Fori(0, LAYERS) as l:
                def split_at(n, k, units, cols):
                    act.wait_ge(*landed[n % RAW].at2(l, k[0]))
                    act.wait_ge(*w_used.at2(l, k[1]))
                    act.activation(slot(whi, n % SPLIT, units, cols), slot(raw, n % RAW, units, cols),
                                   ACT.Copy).then_inc(hi_done.sem, 1)

                def split(s):
                    units, cols = weights2(s, l)[1:] if s < S2_MOE else (4, COLS)
                    split_at(s, (16 * (s // RAW + 1), s + 1 - SPLIT), units, cols)

                def high(f, dst, n=2, k=None):
                    act.wait_ge(*ft_ready.at2(l, f + 1 if k is None else k + 1))
                    act.activation(dst, ft[:, f % 2, 0:T * n].rearrange("p (k t) -> p k t", k=n), ACT.Copy).then_inc(ft_hi.sem, 1)

                def high_x(f0):
                    for b in range(4):
                        high(f0 + b, xt_hi[:, 2 * b:2 * b + 2, :])

                def take(q, dst):
                    act.wait_ge(*w_used.at2(l, job2_end(q) + 1))
                    act.activation(dst, gp[:, q % 2, 0, 0:dst.shape[-1]], ACT.Copy).then_inc(pair_free[q % 2].sem, 1)

                split(0)
                split(1)
                high_x(X2_IN)
                for s in range(S2_UQ):
                    split(s + 2)
                    if s % 2:
                        j = s // 2
                        take(j, pr[:, 0, COLS * j:min(COLS * (j + 1), IN2)])
                    if s == 3:
                        act.wait_ge(*pair_free[0].at2(l, 2))
                        act.wait_ge(*pair_free[1].at2(l, 2))
                        for t in range(NT):
                            act.activation(rt1[:, 0:CQ], pr[:, t, 0:CQ], ACT.Square, accum_out=lsum4[:, t:t + 1]).then_inc(mla_sq.sem, 1)
                            act.activation(rt2[:, 0:CKV], pr[:, t, CQ:CQ + CKV], ACT.Square, accum_out=lsum4[:, 2 + t:3 + t]).then_inc(mla_sq.sem, 1)
                            act.wait_ge(*mla_sq.at2(l, 2 * t + 2))
                        act.wait_ge(*rv2_ready.at2(l, 1))
                        act.activation(rs[:, 0:4], rv[:, 0:4], ACT.Sqrt).then_inc(rs2_ready.sem, 1)
                for b in range(3):
                    n = 2 if b < 2 else 1
                    high(X2_MLA + b, mt_hi[:, 2 * b:2 * b + n, :], n)
                act.wait_ge(*fz_ready.at2(l, 1))
                act.activation(fe[:, :, :], fe[:, :, :], ACT.Exp).then_inc(fe_ready.sem, 1)
                act.wait_ge(*lam_sum.at2(l, 1))
                act.activation(lame[:, :], lame[:, :], ACT.Exp).then_inc(lam_exp.sem, 1)
                act.wait_ge(*fe_ready.at2(l, 1))
                act.activation(fl[:, :, :], fe[:, :, :], ACT.Ln, bias=1.0).then_inc(fl_ready.sem, 1)
                for s in range(S2_UQ, S2_OUT):
                    split(s + 2)
                    q = J2_UQ + s - S2_UQ
                    if s < S2_UKV:
                        h = 4 * (s - S2_UQ)
                        take(q, qm[:, 0, h:h + 4, :].rearrange("p h d -> p (h d)"))
                for i in range(AJ + 3):
                    if i < AJ:
                        act.wait_ge(*t2_done.at2(l, i + 1))
                        w = job_width(i)
                        act.activation(qkt[0:w, i % 2, :], mp[0:w, 0, :], ACT.Copy).then_inc(t2_taken.sem, 1)
                    j = i - 1
                    if 0 <= j < AJ:
                        act.wait_ge(*s2_max.at2(l, j + 1))
                        for t, (a, b) in enumerate(((0, P), (P, 3 * P))):
                            act.activation(sc2[:, j % 2, a:b], sc2[:, j % 2, a:b], ACT.Exp, bias=nmax2[:, j % 2, t:t + 1],
                                           accum_out=rsum2[:, j % 2, t:t + 1]).then_inc(e2_done.sem, 1)
                    j = i - 2
                    if 0 <= j < AJ:
                        act.wait_ge(*p2_done.at2(l, j + 1))
                        act.activation(pt2[:, :], mp[:, 2, 0:3 * P], ACT.Copy).then_inc(p2_taken.sem, 1)
                act.wait_ge(*rv2_ready.at2(l, 2))
                act.activation(rs[:, 0:NT * DH], rv[:, 0:NT * DH], ACT.Sqrt).then_inc(rs2_ready.sem, 1)
                high_x(X2_O)
                for s in range(S2_OUT, S2_MOE):
                    split(s + 2)
                act.wait_ge(*x2_sum.at2(l, 2))
                layer_norm(x, ln_sum.at2(l, 2), ln_cen.at2(l, 2), rv2_ready.at2(l, 3))
                high_x(X2_H)
                act.wait_ge(*logits_done.at2(l, 1))
                act.activation(rsc[:, :, :], mp[:, 0, 0:NT * NE].rearrange("p (t n) -> p t n", t=NT), ACT.Sigmoid).then_inc(rsc_ready.sem, 1)

                def silu(e, k):
                    act.wait_ge(*w_used.at2(l, k))
                    act.wait_ge(*ab2_ready.at2(l, e))
                    act.activation(sg2, gp[:, GATE_PAIR, :, :], ACT.Silu).then_inc(silu2_done.sem, 1)

                for i in range(4):
                    split(S2_MOE + i + 2)
                    if i == 1:
                        silu(0, S2_MOE + 2)
                with act.Fori(1, NE) as e:
                    k = (e - 1) * 6
                    for i in range(6):
                        n = S2_MOE + 6 + i
                        split_at(n, ((e - 1) * 32 + 16 * (n // RAW + 1), k + (n + 1 - SPLIT)), 4, COLS)
                        if i == 1:
                            f = (e - 1) * 2
                            for b in range(2):
                                high(X2_MOE + b, mt_hi[:, 2 * b:2 * b + 2, :], 2, f + (X2_MOE + b))
                            silu(e, k + (S2_MOE + 6))
                for b in range(2):
                    high(X2_LAYER - 2 + b, mt_hi[:, 2 * b:2 * b + 2, :])
                act.wait_ge(*y_taken.at2(l, 2 * NE))
                layer_norm(cen, ln_sum.at2(l, 4), ln_cen.at2(l, 4), rv2_ready.at2(l, 4))

        @block.vector
        def _(dve):
            chain = [0]

            def link(ins, base=0):
                chain[0] += 1
                assert chain[0] < CHAIN
                ins.then_inc(v_chain, 1)
                dve.wait_ge(v_chain, base + chain[0])

            dve.sem_inc(raw_read.sem, raw_read.prime)
            dve.sem_inc(x_final.sem, x_final.prime)
            dve.sem_inc(mod_taken.sem, mod_taken.prime)
            dve.sem_inc(ft_lo.sem, ft_lo.prime)
            dve.wait_ge(consts_in, 16 * 6)
            dve.wait_ge(params_in, PARAMS)
            dve.wait_ge(params_t, LAYERS)
            for l in range(LAYERS):
                dve.tensor_copy(pcol[:, l, :], mp[:, l, 0:PC_ROWS]).then_inc(params_ready, 1)
            dve.wait_ge(csig_ready, 1)
            link(dve.tensor_tensor(cact[:, :], pcol[:, 0, PC_LAYER:PC_ROWS], csig[:, :], ALU.mult))
            link(dve.tensor_copy(posf[:, :, :], posi[:, :, :]))
            for t in range(NT):
                for i in range(2):
                    for which, a, b in ((0, 0, ROT // 2), (1, ROT // 2, NF)):
                        link(dve.tensor_scalar(ang[:, t, i, a:b], freq[:, a:b], posf[:, which, t:t + 1], None, ALU.mult))
            for i, quarter in enumerate((0.25, 0.0)):
                link(dve.tensor_scalar(angk[:, :, i, :], ang[:, :, i, :], float(1.0 / (2 * np.pi)), quarter, ALU.mult, ALU.add))
            nearest = 1.5 * 2.0 ** 23
            link(dve.tensor_scalar(angk[:, :, :, :], angk[:, :, :, :], nearest, None, ALU.add))
            link(dve.tensor_scalar(angk[:, :, :, :], angk[:, :, :, :], nearest, None, ALU.subtract))
            two_pi = 6.28125
            parts = [two_pi, float(np.round((2 * np.pi - two_pi) * 2.0 ** 22) / 2.0 ** 22)]
            parts.append(float(2 * np.pi - sum(parts)))
            for c in parts:
                for i in range(2):
                    link(dve.scalar_tensor_tensor(out=ang[:, :, i, :], in0=angk[:, :, i, :], scalar=-c, in1=ang[:, :, i, :],
                                                  op0=ALU.mult, op1=ALU.add))
            link(dve.tensor_scalar(ang[:, :, 0, :], ang[:, :, 0, :], float(np.pi / 2), None, ALU.add))
            dve.tensor_scalar(ang[:, :, :, :], ang[:, :, :, :], 3.1415925, -3.1415925, ALU.min, ALU.max).then_inc(ang_ready, 1)
            dve.wait_ge(rope_ready, 1)
            a = 0
            for c, sn in zip(cos2, sin2):
                h = c.shape[2] // 2
                for i in range(2):
                    link(dve.tensor_copy(c[:, :, h * i:h * (i + 1)], angk[:, :, 0, a:a + h]))
                link(dve.tensor_scalar(sn[:, :, 0:h], angk[:, :, 1, a:a + h], -1.0, None, ALU.mult))
                link(dve.tensor_copy(sn[:, :, h:2 * h], angk[:, :, 1, a:a + h]))
                a += h
            dve.wait_ge(x_in, 16)
            dve.sem_inc(v_chain, CHAIN - chain[0])
            chain[0] = 0

            with dve.Fori(0, LAYERS) as l:
                def lk(ins):
                    link(ins, (l + 1) * CHAIN)

                def split(s):
                    g = G_OF["split", s]
                    _, units, cols = weights(("split", s), l)
                    dve.wait_ge(*hi_done.at(l, s + 1))
                    dve.tensor_tensor(slot(wlo, s % SPLIT, units, cols), slot(raw, g % RAW, units, cols),
                                      slot(whi, s % SPLIT, units, cols).bitcast(F32), ALU.subtract).then_inc(raw_read.sem, 1)
                    if s in AFTER:
                        ada(2 * ADA + s if s < 12 else 5 * ADA + s - S_FF)

                def ada(n):
                    g = G_OF["ada", n]
                    vec, i = divmod(n, ADA)
                    dve.wait_ge(*landed[g % RAW].at(l, 16 * (g // RAW + 1)))
                    if i == 0:
                        dve.wait_ge(*acc_read.at(l, vec - 1))
                    w, a = slot(raw, g % RAW, 2, D), acc[:, vec % 2, :]
                    for k in range(2):
                        c = cact[:, 2 * i + k:2 * i + k + 1]
                        if i == 0 and k == 0:
                            ins = dve.tensor_scalar(a, w[:, k, :], c, None, ALU.mult)
                        else:
                            ins = dve.scalar_tensor_tensor(out=a, in0=w[:, k, :], scalar=c, in1=a, op0=ALU.mult, op1=ALU.add)
                        if k == 0:
                            lk(ins)
                    ins.then_inc(raw_read.sem, 1)
                    dve.wait_ge(*raw_read.at(l, g + 1))
                    if i == ADA - 1:
                        dve.sem_inc(acc_done.sem, 1)

                def take_mod(vec):
                    dve.wait_ge(*acc_read.at(l, vec + 1))
                    if vec in (2, 5):
                        i = vec // 3
                        dve.wait_ge(*grow_in.at(l, 32))
                        dve.tensor_tensor(grow[:, i, :], mp[:, 0:2, :].rearrange("p a n -> p (a n)"), grow[:, i, :], ALU.add).then_inc(mod_taken.sem, 1)
                    else:
                        bank = {0: 0, 1: 1, 3: 2, 4: 0}[vec]
                        dve.tensor_tensor(modc[:, vec, :], mp[:, bank, 0:KD], pcur[:, KD * vec:KD * (vec + 1)], ALU.add).then_inc(mod_taken.sem, 1)

                def norm_columns(i, vec):
                    dve.wait_ge(*mod_taken.at(l, vec + 2))
                    at = (PC_N1, PC_N2)[i]
                    lk(dve.scalar_tensor_tensor(out=scol[:, i, :], in0=modc[:, vec + 1, :], scalar=1.0,
                                                in1=pcur[:, at:at + KD], op0=ALU.add, op1=ALU.mult))

                def rsqrt(i, n):
                    dve.wait_ge(*rs_ready.at(l, i + 1))
                    lk(dve.reciprocal(rr[:, 0:n], rs[:, 0:n]))
                    lk(dve.tensor_tensor(rt[:, 0:n], rr[:, 0:n], rr[:, 0:n], ALU.mult))
                    lk(dve.tensor_tensor(rt[:, 0:n], rt[:, 0:n], rv[:, 0:n], ALU.mult))
                    lk(dve.tensor_scalar(rt[:, 0:n], rt[:, 0:n], -0.5, 1.5, ALU.mult, ALU.add))
                    dve.tensor_tensor(rr[:, 0:n], rr[:, 0:n], rt[:, 0:n], ALU.mult).then_inc(rr_ready.sem, 1)

                def row_norm(i):
                    dve.wait_ge(*sq_done.at(l, 2 * i + 2))
                    dve.tensor_scalar(rv[:, 0:NT], ssq[:, :], 1.0 / D, EPS, ALU.mult, ALU.add).then_inc(rv_ready.sem, 1)
                    rsqrt(i, NT)

                def low(f, hi, lo):
                    dve.wait_ge(*ft_hi.at(l, f + 1))
                    dve.tensor_tensor(lo, chunks(ft[:, f % 2, :]), hi.bitcast(F32), ALU.subtract).then_inc(ft_lo.sem, 1)

                def ft_free(f):
                    dve.wait_ge(*ft_lo.at(l, f - 1))

                def bank_done(f):
                    dve.wait_ge(*tr_done.at(l, f + 1 - (f > X_CONV)))
                    ft_free(f)

                def plain(f, bank):
                    bank_done(f)
                    dve.tensor_copy(ft[:, f % 2, :], mp[:, bank, :]).then_inc(ft_ready.sem, 1)

                def spread(f0, n, dst, c0, copy, bank0=0):
                    hi, lo = dst
                    for b in range(n + 1):
                        if b < n:
                            copy(f0 + b, bank0 + b)
                        if b:
                            c = c0 + 2 * (b - 1)
                            low(f0 + b - 1, hi[:, c:c + 2, :], lo[:, c:c + 2, :])

                def normed(i, vec):
                    def copy(f, bank):
                        bank_done(f)
                        for k in range(2):
                            c = 2 * bank + k
                            ins = dve.tensor_scalar(ft[:, f % 2, T * k:T * (k + 1)], mp[:, bank, T * k:T * (k + 1)],
                                                    scol[:, i, c:c + 1], modc[:, vec, c:c + 1], ALU.mult, ALU.add)
                            if k == 0:
                                lk(ins)
                        ins.then_inc(ft_ready.sem, 1)
                    return copy

                def take_w_in(j):
                    dve.wait_ge(*w_used.at(l, JOB_END[j] + 1))
                    dve.tensor_copy(u[:, 1, COLS * j:COLS * (j + 1)], gp[:, j % 2, 1, :]).then_inc(pair_free[j % 2].sem, 1)

                def qk_norm_rope():
                    qk = u[:, :, 0:2 * COLS].rearrange("p t (h d) -> p t h d", d=HD)
                    n = 2 * NT * HEADS
                    dve.wait_ge(*sq_done.at(l, 4))
                    lk(dve.tensor_reduce(rt[:, 0:n].rearrange("p (t h) -> p t h", t=NT),
                                         gl[:, :, 0:D].rearrange("p t (h d) -> p t h d", d=HD), AX.X, ALU.add))
                    dve.tensor_scalar(rv[:, 0:n], rt[:, 0:n], 1.0 / HD, EPS, ALU.mult, ALU.add).then_inc(rv_ready.sem, 1)
                    rsqrt(1, n)
                    dve.wait_ge(*rr_ready.at(l, 2))
                    rb = rr[:, 0:n].rearrange("p (t h) -> p t h", t=NT).unsqueeze(3).broadcast_to((P, NT, 2 * HEADS, HD))
                    lk(dve.tensor_tensor(qk, qk, rb, ALU.mult))
                    for i in range(2):
                        part = u[:, :, COLS * i:COLS * (i + 1)].rearrange("p t (h d) -> p t h d", d=HD)
                        wb = qkcur[:, i, :].unsqueeze(1).unsqueeze(1).broadcast_to((P, NT, HEADS, HD))
                        lk(dve.tensor_tensor(part, part, wb, ALU.mult))
                    half = ROT // 2
                    t1 = w1[:, :, 0:T].rearrange("p a (h d) -> p a h d", d=ROT)
                    t2 = sc[:, :, 0:T].rearrange("p a (h d) -> p a h d", d=ROT)
                    cb = cos2[0][:, :, :].unsqueeze(2).broadcast_to((P, NT, 2 * HEADS, ROT))
                    lk(dve.tensor_tensor(t1, qk[:, :, :, 0:ROT], cb, ALU.mult))
                    for i in range(2):
                        sb_ = sin2[0][:, :, half * i:half * (i + 1)].unsqueeze(2).broadcast_to((P, NT, 2 * HEADS, half))
                        lk(dve.tensor_tensor(t2[:, :, :, half * i:half * (i + 1)], qk[:, :, :, half * (1 - i):half * (2 - i)], sb_, ALU.mult))
                    dve.tensor_tensor(qk[:, :, :, 0:ROT], t1, t2, ALU.add).then_inc(qk_ready.sem, 1)

                def pool_windows():
                    e = PAD + T
                    dve.wait_ge(*pct_taken.at(l, 1))
                    dve.memset(pp[:, :, 0:PAD], 0.0).then_inc(pads_zero.sem, 1)
                    dve.memset(zp[:, :, 0:PAD], 0.0).then_inc(pads_zero.sem, 1)
                    dve.wait_ge(*pads_zero.at(l, 2))
                    lk(dve.tensor_tensor(w1[:, :, 1:e], pp[:, :, 1:e], pp[:, :, 0:e - 1], ALU.add))
                    lk(dve.tensor_tensor(w2[:, :, 3:e], w1[:, :, 3:e], w1[:, :, 1:e - 2], ALU.add))
                    lk(dve.tensor_tensor(w1[:, 1, 7:e], w2[:, 1, 7:e], w2[:, 1, 3:e - 4], ALU.add))
                    lk(dve.tensor_tensor(w2[:, 1, PAD:e], w1[:, 1, PAD:e], w1[:, 1, PAD - 8:e - 8], ALU.add))
                    for half, w in ((0, w1), (64, w2)):
                        r = slice(half, half + 64)
                        lk(dve.tensor_tensor(w[r, :, PAD:e], w[r, :, PAD:e], count[r, :, :], ALU.mult))
                        ins = dve.tensor_tensor(w1[r, :, PAD:e], w[r, :, PAD:e], pp[r, :, PAD:e], ALU.subtract)
                        if half == 0:
                            lk(ins)
                    ins.then_inc(pooled.sem, 1)

                def short_conv():
                    dve.wait_ge(*pct_taken.at(l, 3))
                    ft_free(X_CONV)
                    y = ft[:, X_CONV % 2, :].rearrange("p (a t) -> p a t", a=2)
                    for a in range(2):
                        for k in (2, 1, 0):
                            w = pcur[:, PC_CW + 2 * k + a:PC_CW + 2 * k + a + 1]
                            z = zp[:, a, PAD - 2 + k:PAD - 2 + k + T]
                            if k == 2:
                                lk(dve.tensor_scalar(y[:, a, :], z, w, None, ALU.mult))
                            else:
                                lk(dve.scalar_tensor_tensor(out=y[:, a, :], in0=z, scalar=w, in1=y[:, a, :], op0=ALU.mult, op1=ALU.add))
                    dve.tensor_tensor(y, y, bg[:, :, :], ALU.mult).then_inc(ft_ready.sem, 1)

                def soft_max(h):
                    dve.wait_ge(*s_done.at(l, h + 1))
                    lk(dve.scalar_tensor_tensor(out=sc[:, h % 2, :], in0=mp[:, h % 2, 0:3 * P], scalar=HD ** -0.5,
                                                in1=mask[:, :], op0=ALU.mult, op1=ALU.add))
                    dve.tensor_reduce(nmax[:, h % 2, 0:1], sc[:, h % 2, 0:P], AX.X, ALU.max, negate=True)
                    dve.tensor_reduce(nmax[:, h % 2, 1:2], sc[:, h % 2, P:3 * P], AX.X, ALU.max, negate=True).then_inc(s_max.sem, 1)

                def take_o(h):
                    dve.wait_ge(*e_done.at(l, 2 * h + 2))
                    lk(dve.reciprocal(rinv[:, h % 2, :], rsum[:, h % 2, :]))
                    dve.wait_ge(*o_done.at(l, h + 1))
                    for t in range(NT):
                        ins = dve.tensor_scalar(o[:, t, HD * h:HD * (h + 1)], mp[:, 3, HD * t:HD * (t + 1)],
                                                rinv[:, h % 2, t:t + 1], None, ALU.mult)
                        if t == 0:
                            lk(ins)
                    ins.then_inc(o_taken.sem, 1)

                def merge(b, n):
                    q = J_BR + 2 * b + n
                    dve.wait_ge(*w_used.at(l, JOB_END[q] + 1))
                    dve.wait_ge(*gates_ready.at(l, 2 * b + n + 1))
                    gate = gl[:, :, COLS * (2 * b + n):COLS * (2 * b + n + 1)]
                    m = merged[:, :, COLS * n:COLS * (n + 1)]
                    dve.tensor_tensor(m if b == 0 else gate, gp[:, q % 2, :, :], gate, ALU.mult).then_inc(pair_free[q % 2].sem, 2)
                    dve.wait_ge(*pair_free[q % 2].at(l, 2 * (q // 2) + 2))
                    if b == 1:
                        lk(dve.tensor_tensor(m, m, gate, ALU.add))
                    if b == 2:
                        dve.tensor_tensor(m, m, gate, ALU.add).then_inc(merged_ready.sem, 1)

                def residual(q, n, i, tmp):
                    dve.wait_ge(*w_used.at(l, JOB_END[q] + 1))
                    gb = grow[:, i, COLS * n:COLS * (n + 1)].unsqueeze(1).broadcast_to((P, NT, COLS))
                    dve.tensor_tensor(tmp, gp[:, q % 2, :, :], gb, ALU.mult).then_inc(pair_free[q % 2].sem, 2)
                    dve.wait_ge(*pair_free[q % 2].at(l, 2 * (q // 2) + 2))
                    xs = x[:, :, COLS * n:COLS * (n + 1)]
                    dve.tensor_tensor(xs, xs, tmp, ALU.add).then_inc(x_final.sem, 1)

                lk(dve.tensor_copy(pcur[:, :], pcol[:, bass.ds(l, 1), 0:PC_LAYER].rearrange("p a n -> p (a n)")))
                lk(dve.tensor_copy(qkcur[:, :, :].rearrange("p a n -> p (a n)"), qkw[:, bass.ds(l, 1), :, :].rearrange("p a b n -> p (a b n)")))
                lk(dve.tensor_copy(poolcur[:, :, :].rearrange("p a n -> p (a n)"), poolw[:, bass.ds(l, 1), :, :].rearrange("p a b n -> p (a b n)")))
                row_norm(0)
                for n in range(2 * ADA):
                    ada(n)
                take_mod(0)
                take_mod(1)
                norm_columns(0, 0)
                split(0)
                split(1)
                spread(X_NORM1, 4, (xt_hi, xt_lo), 0, normed(0, 0))
                for s in range(10):
                    split(s + 2)
                    if s % 2:
                        take_w_in(s // 2)
                    if s == 5:
                        qk_norm_rope()
                    if s == 7:
                        take_mod(2)
                dve.wait_ge(*pair_free[0].at(l, 6))
                cu = u[:, :, 3 * COLS + 256:4 * COLS]
                dve.tensor_tensor(cu, cu, u[:, :, 4 * COLS + 256:5 * COLS], ALU.mult).then_inc(cu_ready.sem, 1)
                for i in range(12):
                    split(10 + i + 2)
                    if i == 0:
                        take_mod(3)
                    if 0 <= i - 4 < HEADS:
                        take_o(i - 4)
                    if 0 <= i - 2 < HEADS:
                        soft_max(i - 2)
                    if i == 5:
                        pool_windows()
                take_mod(4)
                norm_columns(1, 3)

                def pool_scaled(f, bank):
                    bank_done(f)
                    for k in range(2):
                        ins = dve.tensor_scalar(ft[:, f % 2, T * k:T * (k + 1)], mp[:, bank, T * k:T * (k + 1)],
                                                pcur[:, PC_PS + k:PC_PS + k + 1], None, ALU.mult)
                        if k == 0:
                            lk(ins)
                    ins.then_inc(ft_ready.sem, 1)

                spread(X_POOL, 1, (bt_hi, bt_lo), 0, pool_scaled, 1)
                short_conv()
                low(X_CONV, bt_hi[:, 2:4, :], bt_lo[:, 2:4, :])
                spread(X_ATT, 2, (bt_hi, bt_lo), 4, plain, 2)
                for s in range(S_BR, S_OUT):
                    split(s + 2)
                    for q, _, _, _, _, _, _ in group_jobs(s):
                        merge((q - J_BR) // 2, (q - J_BR) % 2)
                spread(X_MERGE, 4, (xt_hi, xt_lo), 0, plain)
                for s in range(S_OUT, S_FF):
                    split(s + 2)
                    if s % 2 == (S_OUT + 1) % 2:
                        n = (s - S_OUT) // 2
                        residual(J_OUT + n, n, 0, gl[:, :, COLS * n:COLS * (n + 1)])
                row_norm(2)
                spread(X_NORM2, 4, (xt_hi, xt_lo), 0, normed(1, 3))
                for s in range(S_FF, S_DOWN):
                    split(s + 2)
                    j, r = divmod(s - S_FF, 4)
                    wide = min(COLS, FF - COLS * j)
                    if r == 2 and j >= 1:
                        spread(X_ACT + 2 * (j - 1), 2, (at_hi, at_lo), 4 * (j - 1), plain, 2 * ((j - 1) % 2))
                    if r == 3:
                        q = J_FF + 2 * j + 1
                        dve.wait_ge(*w_used.at(l, JOB_END[q] + 1))
                        dve.wait_ge(*silu_done.at(l, j + 1))
                        dve.tensor_tensor(ab[:, :, 0:wide], gp[:, q % 2, :, 0:wide], sg[:, :, 0:wide], ALU.mult).then_inc(ab_ready.sem, 1)
                        dve.wait_ge(*ab_ready.at(l, j + 1))
                        dve.sem_inc(pair_free[q % 2].sem, 2)
                        dve.sem_inc(pair_free[1 - q % 2].sem, 2)
                for s in range(S_DOWN, S_LAYER - 2):
                    split(s + 2)
                    if s == S_DOWN + 1:
                        spread(X_ACT + 2 * (FF_BLOCKS - 1), 1, (at_hi, at_lo), FF_CHUNKS - 2, plain, 2)
                    if s == S_DOWN + 3:
                        take_mod(5)
                for n in range(2):
                    residual(J_DOWN + n, n, 1, (sg, ab)[n][:, :, :])
                dve.wait_ge(*x_final.at(l, 4))
                dve.sem_inc(v_chain, CHAIN - chain[0])
            chain[0] = 0

            base2 = (LAYERS + 1) * CHAIN

            def reciprocal_root(n, wait, lk):
                dve.wait_ge(*wait)
                lk(dve.reciprocal(rr[:, 0:n], rs[:, 0:n]))
                lk(dve.tensor_tensor(rt[:, 0:n], rr[:, 0:n], rr[:, 0:n], ALU.mult))
                lk(dve.tensor_tensor(rt[:, 0:n], rt[:, 0:n], rv[:, 0:n], ALU.mult))
                lk(dve.tensor_scalar(rt[:, 0:n], rt[:, 0:n], -0.5, 1.5, ALU.mult, ALU.add))
                lk(dve.tensor_tensor(rr[:, 0:n], rr[:, 0:n], rt[:, 0:n], ALU.mult))

            def layer_norm(src, sums, squares, roots, rows, lk):
                dve.wait_ge(*sums)
                lk(dve.tensor_scalar(mean[:, :], lsum[:, :], 1.0 / D, None, ALU.mult))
                for t in range(NT):
                    dve.tensor_scalar(cen[:, t, :], src[:, t, :], mean[:, t:t + 1], None, ALU.subtract).then_inc(ln_cen.sem, 1)
                dve.wait_ge(*squares)
                dve.tensor_scalar(rv[:, 0:NT], ssq[:, :], 1.0 / D, LN_EPS, ALU.mult, ALU.add).then_inc(rv2_ready.sem, 1)
                reciprocal_root(NT, roots, lk)
                dve.wait_ge(*rows)
                for t in range(NT):
                    lk(dve.scalar_tensor_tensor(out=cen[:, t, :], in0=cen[:, t, :], scalar=rr[:, t:t + 1],
                                                in1=lnw[:, 0, :], op0=ALU.mult, op1=ALU.mult))
                    dve.tensor_tensor(x[:, t, :], cen[:, t, :], lnw[:, 1, :], ALU.add).then_inc(h_ready.sem, 1)

            def lk0(ins):
                link(ins, base2)

            layer_norm(x, (ln_sum.sem, 2), (ln_sq.sem, 2), (rs2_ready.sem, 1), (lnw_in.sem, 32), lk0)
            dve.wait_ge(rw_high, 1)
            lk0(dve.tensor_tensor(rw_lo[:, :, :], rw[:, :, :], rw_hi[:, :, :].bitcast(F32), ALU.subtract))
            dve.sem_inc(rw_ready, 1)
            dve.sem_inc(v_chain, CHAIN2 - chain[0])
            chain[0] = 0

            with dve.Fori(0, LAYERS) as l:
                def lk(ins):
                    link(ins, l * CHAIN2 + (base2 + CHAIN2))

                def split_at(n, k, units, cols):
                    dve.wait_ge(*hi_done.at2(l, k))
                    dve.tensor_tensor(slot(wlo, n % SPLIT, units, cols), slot(raw, n % RAW, units, cols),
                                      slot(whi, n % SPLIT, units, cols).bitcast(F32), ALU.subtract).then_inc(raw_read.sem, 1)

                def split(s):
                    units, cols = weights2(s, l)[1:] if s < S2_MOE else (4, COLS)
                    split_at(s, s + 1, units, cols)

                def plain(f, bank, n, k):
                    dve.wait_ge(*tr_done.at2(l, k + 1))
                    dve.wait_ge(*ft_lo.at2(l, k - 1))
                    dve.tensor_copy(ft[:, f % 2, 0:T * n], mp[:, bank, 0:T * n]).then_inc(ft_ready.sem, 1)

                def low(f, hi, lo, n, k):
                    dve.wait_ge(*ft_hi.at2(l, k + 1))
                    dve.tensor_tensor(lo, ft[:, f % 2, 0:T * n].rearrange("p (k t) -> p k t", k=n), hi.bitcast(F32),
                                      ALU.subtract).then_inc(ft_lo.sem, 1)

                def spread(f0, units, dst, bank0=0, k0=None):
                    hi, lo = dst
                    at = f0 if k0 is None else k0
                    for b in range(len(units) + 1):
                        if b < len(units):
                            plain(f0 + b, bank0 + b, units[b], at + b)
                        if b:
                            c, n = 2 * (b - 1), units[b - 1]
                            low(f0 + b - 1, hi[:, c:c + n, :], lo[:, c:c + n, :], n, at + (b - 1))

                def take(q, t, dst, src=None):
                    dve.wait_ge(*w_used.at2(l, job2_end(q) + 1))
                    src = gp[:, q % 2, t, 0:dst.shape[-1]] if src is None else src
                    dve.tensor_copy(dst, src).then_inc(pair_free[q % 2].sem, 1)

                def rotate(v, r, heads, rot):
                    h = rot // 2
                    n = NT * heads * rot
                    t1 = rt1[:, 0:n].rearrange("p (t h d) -> p t h d", t=NT, d=rot)
                    t2 = rt2[:, 0:n].rearrange("p (t h d) -> p t h d", t=NT, d=rot)
                    lk(dve.tensor_tensor(t1, v, cos2[r][:, :, :].unsqueeze(2).broadcast_to((P, NT, heads, rot)), ALU.mult))
                    for i in range(2):
                        sn = sin2[r][:, :, h * i:h * (i + 1)].unsqueeze(2).broadcast_to((P, NT, heads, h))
                        lk(dve.tensor_tensor(t2[:, :, :, h * i:h * (i + 1)], v[:, :, :, h * (1 - i):h * (2 - i)], sn, ALU.mult))
                    lk(dve.tensor_tensor(v, t1, t2, ALU.add))

                split(0)
                split(1)
                dve.wait_ge(params2_in, PARAMS2)
                lk(dve.tensor_copy(cgc[:, :], cg[:, bass.ds(l, 1), :].rearrange("p a n -> p (a n)")))
                lk(dve.tensor_scalar(subc[:, :], subg[:, bass.ds(l, 1), :].rearrange("p a n -> p (a n)"),
                                     lamc[:, bass.ds(l, 1), 1:2].rearrange("p a n -> p (a n)"), None, ALU.mult))
                lr = lamr[:, bass.ds(l, 1), :, :].rearrange("p a b n -> p (a b) n")
                lk(dve.tensor_copy(lamq[:, :, :], lr))
                lk(dve.tensor_tensor(lamt[:, :, :], lamq[:, 0:2, :], lamq[:, 2:4, :], ALU.mult))
                dve.tensor_reduce(lame[:, :], lamt[:, :, :], AX.X, ALU.add).then_inc(lam_sum.sem, 1)
                lk(dve.tensor_copy(lami[:, :], lamc[:, bass.ds(l, 1), 0:1].rearrange("p a n -> p (a n)")))
                lk(dve.tensor_copy(fbc[:, :], fbias[:, bass.ds(l, 1), :].rearrange("p a n -> p (a n)")))
                spread(X2_IN, (2, 2, 2, 2), (xt_hi, xt_lo))
                for s in range(S2_UQ):
                    split(s + 2)
                    if s % 2:
                        j = s // 2
                        take(j, 1, pr[:, 1, COLS * j:min(COLS * (j + 1), IN2)])
                    if s == 3:
                        dve.wait_ge(*mla_sq.at2(l, 4))
                        lk(dve.tensor_scalar(rv[:, 0:2], lsum4[:, 0:2], 1.0 / CQ, EPS, ALU.mult, ALU.add))
                        dve.tensor_scalar(rv[:, 2:4], lsum4[:, 2:4], 1.0 / CKV, EPS, ALU.mult, ALU.add).then_inc(rv2_ready.sem, 1)
                        reciprocal_root(4, rs2_ready.at2(l, 1), lk)
                        for t in range(NT):
                            for i, (a, b) in enumerate(((0, CQ), (CQ, CQ + CKV))):
                                lk(dve.scalar_tensor_tensor(out=pr[:, t, a:b], in0=pr[:, t, a:b], scalar=rr[:, 2 * i + t:2 * i + t + 1],
                                                            in1=cgc[:, a:b], op0=ALU.mult, op1=ALU.mult))
                        dve.sem_inc(mla_ready.sem, 1)
                dve.wait_ge(*pair_free[0].at2(l, 6))
                dve.wait_ge(*pair_free[1].at2(l, 4))
                lk(dve.tensor_tensor(fz[:, :, :], pr[:, :, C_FF:C_FF + FH], fbc[:, :].unsqueeze(1).broadcast_to((P, NT, FH)), ALU.add))
                lk(dve.tensor_scalar(fe[:, :, :], fz[:, :, :], -1.0, None, ALU.mult))
                dve.tensor_tensor(fe[:, :, :], fz[:, :, :], fe[:, :, :], ALU.min).then_inc(fz_ready.sem, 1)
                spread(X2_MLA, (2, 2, 1), (mt_hi, mt_lo))
                dve.wait_ge(*lam_exp.at2(l, 1))
                lk(dve.tensor_tensor(nlam[:, :], lame[:, 1:2], lame[:, 0:1], ALU.subtract))
                lk(dve.tensor_tensor(nlam[:, :], nlam[:, :], lami[:, :], ALU.subtract))
                dve.wait_ge(*fl_ready.at2(l, 1))
                lk(dve.tensor_scalar(fz[:, :, :], fz[:, :, :], 0.0, None, ALU.min))
                dve.tensor_tensor(fz[:, :, :], fz[:, :, :], fl[:, :, :], ALU.subtract).then_inc(logf_ready.sem, 1)
                for s in range(S2_UQ, S2_OUT):
                    split(s + 2)
                    q = J2_UQ + s - S2_UQ
                    h = 4 * ((s - S2_UQ) % 2)
                    if s < S2_UKV:
                        take(q, 1, qm[:, 1, h:h + 4, :].rearrange("p h d -> p (h d)"))
                    else:
                        for t in range(NT):
                            kv = gp[:, q % 2, t, :].rearrange("p (h d) -> p h d", h=4)
                            dve.wait_ge(*w_used.at2(l, job2_end(q) + 1))
                            lk(dve.tensor_copy(km[:, t, h:h + 4, 0:MN], kv[:, :, 0:MN]))
                            dve.tensor_copy(vm[:, t, h:h + 4, :], kv[:, :, MN:MN + HD]).then_inc(pair_free[q % 2].sem, 1)
                dve.wait_ge(*pair_free[0].at2(l, 8))
                dve.wait_ge(*pair_free[1].at2(l, 6))
                rotate(qm[:, :, :, MN:MQ], 1, MH, KR)
                kr = pr[:, :, C_KR:C_KR + KR].unsqueeze(2)
                rotate(kr, 1, 1, KR)
                lk(dve.tensor_copy(km[:, :, :, MN:MQ], kr.broadcast_to((P, NT, MH, KR))))
                dve.sem_inc(km_ready.sem, 1)
                for c in (C_DQ, C_DK):
                    rotate(pr[:, :, c:c + 2 * DH * DW].rearrange("p t (h d) -> p t h d", d=DW)[:, :, :, 0:DROT], 2, 2 * DH, DROT)
                dve.sem_inc(diff_ready.sem, 1)
                up = HD ** 0.5
                for dst, c in ((fq, C_FQ), (fk, C_FK)):
                    lk(dve.tensor_copy(dst[:, :, :, 0:HD], pr[:, :, c:c + FH * HD].rearrange("p t (h d) -> p t h d", d=HD)))
                lk(dve.memset(fq[:, :, :, HD + 1:HD + 2], 1.0))
                lk(dve.memset(fk[:, :, :, HD:HD + 1], 1.0))
                dve.wait_ge(*cum_done.at2(l, 1))
                cum = mp[:, 3, 0:NT * FH].rearrange("p (t h) -> p t h", t=NT)
                lk(dve.tensor_scalar(fq[:, :, :, HD:HD + 1].rearrange("p t h a -> p t (h a)"), cum, up, None, ALU.mult))
                dve.tensor_scalar(fk[:, :, :, HD + 1:HD + 2].rearrange("p t h a -> p t (h a)"), cum, -up, None, ALU.mult).then_inc(fox_ready.sem, 1)
                for i in range(AJ + 3):
                    j = i - 3
                    if 0 <= j < AJ:
                        dve.wait_ge(*e2_done.at2(l, 2 * j + 2))
                        lk(dve.reciprocal(rinv2[:, j % 2, :], rsum2[:, j % 2, :]))
                        dve.wait_ge(*o2_done.at2(l, j + 1))
                        for t in range(NT):
                            if j < MH:
                                dst = oa[:, t, HD * j:HD * (j + 1)]
                            elif j < MH + 2 * DH:
                                m, h = (j - MH) % 2, (j - MH) // 2
                                dst = od[:, t, HD * h:HD * (h + 1)] if m else oa[:, t, HD * (MH + h):HD * (MH + h + 1)]
                            else:
                                dst = oa[:, t, HD * (j - DH):HD * (j - DH + 1)]
                            ins = dve.tensor_scalar(dst, mp[:, 3, HD * t:HD * (t + 1)], rinv2[:, j % 2, t:t + 1], None, ALU.mult)
                            if t == 0:
                                lk(ins)
                        ins.then_inc(o2_taken.sem, 1)
                    j = i - 1
                    if 0 <= j < AJ:
                        scale, m = job_operands(j)[3:]
                        dve.wait_ge(*s2_done.at2(l, j + 1))
                        lk(dve.scalar_tensor_tensor(out=sc2[:, j % 2, :], in0=mp[:, 1, 0:3 * P], scalar=scale,
                                                    in1=m[:, :], op0=ALU.mult, op1=ALU.add))
                        dve.tensor_reduce(nmax2[:, j % 2, 0:1], sc2[:, j % 2, 0:P], AX.X, ALU.max, negate=True)
                        dve.tensor_reduce(nmax2[:, j % 2, 1:2], sc2[:, j % 2, P:3 * P], AX.X, ALU.max, negate=True).then_inc(s2_max.sem, 1)
                dve.wait_ge(*o2_taken.at2(l, AJ))
                d1 = oa[:, :, HD * MH:HD * (MH + DH)]
                lk(dve.scalar_tensor_tensor(out=d1, in0=od[:, :, :], scalar=nlam[:, :], in1=d1, op0=ALU.mult, op1=ALU.add))
                lk(dve.tensor_tensor(od[:, :, :], d1, d1, ALU.mult))
                n = NT * DH
                lk(dve.tensor_reduce(rt[:, 0:n].rearrange("p (t h) -> p t h", t=NT), od[:, :, :].rearrange("p t (h d) -> p t h d", d=HD), AX.X, ALU.add))
                dve.tensor_scalar(rv[:, 0:n], rt[:, 0:n], 1.0 / HD, EPS, ALU.mult, ALU.add).then_inc(rv2_ready.sem, 1)
                reciprocal_root(n, rs2_ready.at2(l, 2), lk)
                d1h = d1.rearrange("p t (h d) -> p t h d", d=HD)
                lk(dve.tensor_tensor(d1h, d1h, rr[:, 0:n].rearrange("p (t h) -> p t h", t=NT).unsqueeze(3).broadcast_to((P, NT, DH, HD)), ALU.mult))
                dve.tensor_tensor(d1h, d1h, subc[:, :].unsqueeze(1).unsqueeze(1).broadcast_to((P, NT, DH, HD)), ALU.mult).then_inc(oa_ready.sem, 1)
                spread(X2_O, (2, 2, 2, 2), (xt_hi, xt_lo))
                for s in range(S2_OUT, S2_MOE):
                    split(s + 2)
                    if s % 2 == (S2_OUT + 1) % 2:
                        n = (s - S2_OUT) // 2
                        q = J2_OUT + n
                        dve.wait_ge(*w_used.at2(l, job2_end(q) + 1))
                        xs = x[:, :, COLS * n:COLS * (n + 1)]
                        dve.scalar_tensor_tensor(out=xs, in0=xs, scalar=ALPHA, in1=gp[:, q % 2, :, :], op0=ALU.mult, op1=ALU.add).then_inc(x2_sum.sem, 1)
                        dve.wait_ge(*x2_sum.at2(l, n + 1))
                        dve.sem_inc(pair_free[q % 2].sem, 2)
                layer_norm(x, ln_sum.at2(l, 2), ln_sq.at2(l, 2), rs2_ready.at2(l, 3), lnw_in.at2(l, 32), lk)
                spread(X2_H, (2, 2, 2, 2), (xt_hi, xt_lo))
                dve.wait_ge(*h_ready.at2(l, 2))
                lk(dve.tensor_scalar(cen[:, :, :], x[:, :, :], ALPHA, None, ALU.mult))

                def beats(dst, v):
                    d = cmp1[:, 0:v.shape[1], :].rearrange("p g (i j) -> p g i j", i=4)
                    e_ = cmp2[:, 0:v.shape[1], :].rearrange("p g (i j) -> p g i j", i=4)
                    shape = (P, v.shape[1], 4, 4)
                    vi, vj = v.unsqueeze(3).broadcast_to(shape), v.unsqueeze(2).broadcast_to(shape)
                    lk(dve.tensor_tensor(d, vj, vi, ALU.is_ge))
                    lk(dve.tensor_tensor(e_, vj, vi, ALU.is_gt))
                    for a, c in ((cmp1, 0), (cmp2, 1)):
                        w = a[:, 0:v.shape[1], :]
                        lk(dve.tensor_tensor(w, w, order[:, c, :].unsqueeze(1).broadcast_to((P, v.shape[1], 16)), ALU.mult))
                    lk(dve.tensor_tensor(d, d, e_, ALU.add))
                    lk(dve.tensor_reduce(dst, d, AX.X, ALU.add))

                dve.wait_ge(*rsc_ready.at2(l, 1))
                lk(dve.tensor_tensor(rb[:, :, :], rsc[:, :, :], rbias[:, :].unsqueeze(1).broadcast_to((P, NT, NE)), ALU.add))
                four = rb[:, :, :].rearrange("p t (g i) -> p (t g) i", i=4)
                beats(rank[:, :, :], four)
                lk(dve.tensor_scalar(rank[:, :, :], rank[:, :, :], 2.0, None, ALU.is_lt))
                lk(dve.tensor_tensor(cmp1[:, :, 0:4], four, rank[:, :, :], ALU.mult))
                lk(dve.tensor_reduce(gs[:, :], cmp1[:, :, 0:4], AX.X, ALU.add))
                beats(gr[:, :].rearrange("p (t g) -> p t g", t=NT), gs[:, :].rearrange("p (t g) -> p t g", t=NT))
                lk(dve.tensor_scalar(gr[:, :], gr[:, :], 1.0, None, ALU.is_lt))
                lk(dve.tensor_tensor(rank[:, :, :], rank[:, :, :], gr[:, :].unsqueeze(2).broadcast_to((P, 8, 4)), ALU.mult))
                lk(dve.tensor_tensor(dg[:, :, :], rsc[:, :, :], rank[:, :, :].rearrange("p (t g) i -> p t (g i)", t=NT), ALU.mult))
                lk(dve.tensor_reduce(den[:, :], dg[:, :, :], AX.X, ALU.add))
                lk(dve.reciprocal(den[:, :], den[:, :]))
                for t in range(NT):
                    lk(dve.tensor_scalar(dg[:, t, :], dg[:, t, :], den[:, t:t + 1], None, ALU.mult))

                def gated(e, k):
                    dve.wait_ge(*w_used.at2(l, k))
                    dve.wait_ge(*silu2_done.at2(l, e + 1))
                    for t in range(NT):
                        ins = dve.scalar_tensor_tensor(out=ab2[:, t, :], in0=gp[:, 1 - GATE_PAIR, t, :], scalar=dg[:, t, bass.ds(e, 1)],
                                                       in1=sg2[:, t, :], op0=ALU.mult, op1=ALU.mult)
                        if t == 0:
                            lkm(ins)
                    ins.then_inc(ab2_ready.sem, 1)
                    dve.wait_ge(*ab2_ready.at2(l, e + 1))
                    for p in range(2):
                        dve.sem_inc(pair_free[p].sem, 2)

                def add_y(n, yk, k):
                    p = GATE_PAIR if n == 0 else 1 - GATE_PAIR
                    dve.wait_ge(*w_used.at2(l, k))
                    ys = cen[:, :, COLS * n:COLS * (n + 1)]
                    dve.tensor_tensor(ys, ys, gp[:, p, :, :], ALU.add).then_inc(y_taken.sem, 1)
                    dve.wait_ge(*y_taken.at2(l, yk))
                    dve.sem_inc(pair_free[p].sem, 2)

                lkm = lk
                for i in range(4):
                    split(S2_MOE + i + 2)
                gated(0, S2_MOE + 4)
                so_far = chain[0]

                def lkm(ins):
                    ins.then_inc(v_moe, 1)
                    dve.wait_ge(v_moe, l * (NE - 1) + e)

                with dve.Fori(1, NE) as e:
                    k = (e - 1) * 6
                    for i in range(6):
                        n = S2_MOE + 6 + i
                        split_at(n, k + (n + 1), 4, COLS)
                        if i == 1:
                            spread(X2_MOE, (2, 2), (mt_hi, mt_lo), 0, (e - 1) * 2 + X2_MOE)
                        if i == 3:
                            gated(e, k + (S2_MOE + 8))
                        if i == 4:
                            add_y(0, (e - 1) * 2 + 1, k + (S2_MOE + 9))
                        if i == 5:
                            add_y(1, (e - 1) * 2 + 2, k + (S2_MOE + 10))
                spread(X2_LAYER - 2, (2, 2), (mt_hi, mt_lo))
                add_y(0, 2 * NE - 1, S2_LAYER - 1)
                add_y(1, 2 * NE, S2_LAYER)
                layer_norm(cen, ln_sum.at2(l, 4), ln_sq.at2(l, 4), rs2_ready.at2(l, 4), lnw_in.at2(l, 64), lk)
                dve.wait_ge(*h_ready.at2(l, 4))
                dve.sem_inc(v_chain, CHAIN2 - chain[0])

        @block.tensor
        def _(pe):
            pe.sem_inc(w_used.sem, w_used.prime)
            pe.sem_inc(acc_read.sem, acc_read.prime)
            for p in range(2):
                pe.sem_inc(pair_free[p].sem, pair_free[p].prime)
            pe.wait_ge(consts_in, 16 * 6)
            pe.wait_ge(params_in, PARAMS)
            pe.wait_ge(zeroed, 2)
            for l in range(LAYERS):
                pe.transpose(mp[:, l, 0:PC_ROWS], stage[:, l, :], ident[0:PC_ROWS, 0:PC_ROWS]).then_inc(params_t, 1)

            with pe.Fori(0, LAYERS) as l:
                def product(s):
                    pe.wait_ge(*raw_read.at(l, G_OF["split", s] + 1))
                    _, units, cols = weights(("split", s), l)
                    w_hi, w_lo = slot(whi, s % SPLIT, units, cols), slot(wlo, s % SPLIT, units, cols)
                    for q, c0, wide, parts, first, last, name in group_jobs(s):
                        a_hi, a_lo = stationary[name]
                        if first:
                            pe.wait_ge(*pair_free[q % 2].at(l, 2 * (q // 2)))
                        for t in range(NT):
                            ts = slice(P * t, P * (t + 1))
                            for n, (unit, chunk) in enumerate(parts):
                                for m, (a, w) in enumerate(((a_hi, w_hi), (a_hi, w_lo), (a_lo, w_hi))):
                                    mm = pe.matmul(gp[:, q % 2, t, 0:wide], a[:, chunk, ts], w[:, unit, c0:c0 + wide],
                                                   start=first and n == 0 and m == 0, stop=last and n == len(parts) - 1 and m == 2)
                    mm.then_inc(w_used.sem, 1)

                def sum_mod(vec):
                    pe.wait_ge(*acc_done.at(l, vec + 1))
                    a = acc[:, vec % 2, :]
                    if vec in (2, 5):
                        for n in range(2):
                            mm = pe.matmul(mp[:, n, :], ones[:, :], a[:, COLS * n:COLS * (n + 1)], start=True, stop=True)
                    else:
                        bank = {0: 0, 1: 1, 3: 2, 4: 0}[vec]
                        for c in range(KD):
                            mm = pe.matmul(mp[:, bank, c:c + 1], a[:, P * c:P * (c + 1)], ones[:, 0:1], start=True, stop=True)
                    mm.then_inc(acc_read.sem, 1)

                def turn(bank, src, c0, n=2):
                    for k in range(n):
                        for t in range(NT):
                            mm = pe.transpose(mp[:, bank, T * k + P * t:T * k + P * (t + 1)], src[:, t, c0 + P * k:c0 + P * (k + 1)], ident[:, :])
                    return mm

                pe.wait_ge(*mod_taken.at(l, 0))
                sum_mod(0)
                sum_mod(1)
                pe.wait_ge(*mod_taken.at(l, 2))
                pe.wait_ge(*xn_ready.at(l, 2))
                for b in range(4):
                    turn(b, xn1, 2 * P * b).then_inc(tr_done.sem, 1)
                pe.wait_ge(*ft_lo.at(l, X_NORM1 + 4))
                for s in range(10):
                    product(s)
                    if s == 5:
                        sum_mod(2)
                sum_mod(3)

                def scores(h):
                    if h >= 2:
                        pe.wait_ge(*s_max.at(l, h - 1))
                    r, c = slice(HD * (h % 2), HD * (h % 2) + HD), h // 2
                    pe.matmul(mp[:, h % 2, 0:P], qt[r, c, 0:P], kt[r, c, 0:P], start=True, stop=True)
                    pe.matmul(mp[:, h % 2, P:3 * P], qt[r, c, P:T], kt[r, c, :], start=True, stop=True).then_inc(s_done.sem, 1)

                def turn_p(h):
                    pe.wait_ge(*e_done.at(l, 2 * h + 2))
                    if h >= 1:
                        pe.wait_ge(*pt_taken.at(l, h))
                    for a in range(3):
                        mm = pe.transpose(mp[:, 2, P * a:P * (a + 1)], sc[:, h % 2, P * a:P * (a + 1)], ident[:, :])
                    mm.then_inc(pt_done.sem, 1)

                def weigh(h):
                    pe.wait_ge(*pt_taken.at(l, h + 1))
                    if h >= 1:
                        pe.wait_ge(*o_taken.at(l, h))
                    v = u[:, :, 2 * COLS + HD * h:2 * COLS + HD * (h + 1)]
                    pe.matmul(mp[:, 3, 0:HD], pt[:, 0:P], v[:, 0, :], start=True, stop=True)
                    pe.matmul(mp[:, 3, HD:2 * HD], pt[:, P:2 * P], v[:, 0, :], start=True, stop=False)
                    pe.matmul(mp[:, 3, HD:2 * HD], pt[:, 2 * P:3 * P], v[:, 1, :], start=False, stop=True).then_inc(o_done.sem, 1)

                for i in range(12):
                    product(10 + i)
                    if i == 0:
                        pe.wait_ge(*qk_ready.at(l, 1))
                        pe.wait_ge(*mod_taken.at(l, 4))
                        for b in range(4):
                            mm = turn(b, u, 2 * P * b)
                        mm.then_inc(qkt_done.sem, 1)
                    if i == 1:
                        pe.wait_ge(*qkt_taken.at(l, 4))
                        pe.wait_ge(*cu_ready.at(l, 1))
                        for b in range(3):
                            mm = turn(b, u, 3 * COLS + 2 * P * b)
                        mm.then_inc(pct_done.sem, 1)
                    if i == 2:
                        pe.wait_ge(*pct_taken.at(l, 3))
                    if 0 <= i - 4 < HEADS:
                        weigh(i - 4)
                    if 0 <= i - 3 < HEADS:
                        turn_p(i - 3)
                    if 0 <= i - 2 < HEADS:
                        scores(i - 2)
                pe.wait_ge(*s_max.at(l, HEADS))
                sum_mod(4)
                pe.wait_ge(*pooled.at(l, 1))
                for c in range(2):
                    mm = pe.matmul(mp[:, 1, T * c:T * (c + 1)], poolcur[:, c, :], w1[:, c, PAD:PAD + T], start=True, stop=True)
                mm.then_inc(tr_done.sem, 1)
                pe.wait_ge(*o_taken.at(l, HEADS))
                for b in range(2):
                    turn(2 + b, o, 2 * P * b).then_inc(tr_done.sem, 1)
                for s in range(S_BR, S_OUT):
                    if s == S_BR:
                        pe.wait_ge(*ft_lo.at(l, X_POOL + 1))
                    if s == S_BR + 1:
                        pe.wait_ge(*ft_lo.at(l, X_CONV + 1))
                    if s == S_BR + 2:
                        pe.wait_ge(*ft_lo.at(l, X_ATT + 2))
                    product(s)
                pe.wait_ge(*mod_taken.at(l, 5))
                for b in range(4):
                    if b % 2 == 0:
                        pe.wait_ge(*merged_ready.at(l, b // 2 + 1))
                    turn(b, merged, 2 * P * b).then_inc(tr_done.sem, 1)
                pe.wait_ge(*ft_lo.at(l, X_MERGE + 4))
                for s in range(S_OUT, S_FF):
                    product(s)
                pe.wait_ge(*xn_ready.at(l, 4))
                for b in range(4):
                    turn(b, xn2, 2 * P * b).then_inc(tr_done.sem, 1)
                pe.wait_ge(*ft_lo.at(l, X_NORM2 + 4))

                def turn_ab(j):
                    pe.wait_ge(*ab_ready.at(l, j + 1))
                    if j >= 2:
                        pe.wait_ge(*ft_ready.at(l, X_ACT + 2 * (j - 2) + 2))
                    for b in range(2 if j < FF_BLOCKS - 1 else 1):
                        turn(2 * (j % 2) + b if j < FF_BLOCKS - 1 else 2, ab, 2 * P * b).then_inc(tr_done.sem, 1)

                for s in range(S_FF, S_DOWN):
                    product(s)
                    j, r = divmod(s - S_FF, 4)
                    if r == 1 and j >= 1:
                        turn_ab(j - 1)
                for s in range(S_DOWN, S_LAYER):
                    if s == S_DOWN:
                        pe.wait_ge(*ft_lo.at(l, X_ACT + 2 * (FF_BLOCKS - 1)))
                    if s == S_DOWN + 2:
                        turn_ab(FF_BLOCKS - 1)
                    if s == S_DOWN + 3:
                        pe.wait_ge(*ft_ready.at(l, X_ACT + 2 * (FF_BLOCKS - 1)))
                        sum_mod(5)
                    if s == S_LAYER - 2:
                        pe.wait_ge(*ft_lo.at(l, X_LAYER))
                    product(s)

            with pe.Fori(0, LAYERS) as l:
                def multiply(n, k, q, units, cols, chunk0, src, first, last, pair_k):
                    pe.wait_ge(*raw_read.at2(l, k))
                    w_hi, w_lo = slot(whi, n % SPLIT, units, cols), slot(wlo, n % SPLIT, units, cols)
                    a_hi, a_lo = src
                    if first:
                        pe.wait_ge(*pair_free[q % 2].at2(l, pair_k))
                    for t in range(NT):
                        ts = slice(P * t, P * (t + 1))
                        for unit in range(units):
                            for m, (a, w) in enumerate(((a_hi, w_hi), (a_hi, w_lo), (a_lo, w_hi))):
                                mm = pe.matmul(gp[:, q % 2, t, 0:cols], a[:, chunk0 + unit, ts], w[:, unit, :],
                                               start=first and unit == 0 and m == 0, stop=last and unit == units - 1 and m == 2)
                    mm.then_inc(w_used.sem, 1)

                def product(s):
                    _, units, cols = weights2(s, l)
                    if s < S2_UQ:
                        q, h, c, src = s // 2, s % 2, 4 * (s % 2), (xt_hi, xt_lo)
                        first, last = h == 0, h == 1
                    elif s < S2_OUT:
                        q, c, src, first, last = J2_UQ + s - S2_UQ, 0 if s < S2_UKV else 3, (mt_hi, mt_lo), True, True
                    else:
                        h = (s - S2_OUT) % 2
                        q, c, src, first, last = J2_OUT + (s - S2_OUT) // 2, 4 * h, (xt_hi, xt_lo), h == 0, h == 1
                    multiply(s, s + 1, q, units, cols, c, src, first, last, 2 * (q // 2))

                def turn(bank, src, c0, n=2):
                    for k in range(n):
                        for t in range(NT):
                            mm = pe.transpose(mp[:, bank, T * k + P * t:T * k + P * (t + 1)], src[:, t, c0 + P * k:c0 + P * (k + 1)], ident[:, :])
                    return mm

                pe.wait_ge(*h_ready.at2(l, 0))
                for b in range(4):
                    turn(b, x, 2 * P * b).then_inc(tr_done.sem, 1)
                pe.wait_ge(*ft_lo.at2(l, X2_IN + 4))
                for s in range(S2_UQ):
                    product(s)
                pe.wait_ge(*mla_ready.at2(l, 1))
                for b in range(3):
                    turn(b, pr, 2 * P * b, 2 if b < 2 else 1).then_inc(tr_done.sem, 1)
                pe.wait_ge(*logf_ready.at2(l, 1))
                pe.matmul(mp[:, 3, 0:FH], tri[:, :], fz[:, 0, :], start=True, stop=True)
                pe.matmul(mp[:, 3, FH:2 * FH], ones[:, :], fz[:, 0, :], start=True, stop=False)
                pe.matmul(mp[:, 3, FH:2 * FH], tri[:, :], fz[:, 1, :], start=False, stop=True).then_inc(cum_done.sem, 1)
                pe.wait_ge(*ft_lo.at2(l, X2_MLA + 3))
                for s in range(S2_UQ, S2_OUT):
                    product(s)

                def turn_qk(j):
                    q, k = job_operands(j)[:2]
                    w = job_width(j)
                    if j == 0:
                        pe.wait_ge(*km_ready.at2(l, 1))
                    if j == MH:
                        pe.wait_ge(*diff_ready.at2(l, 1))
                    if j == MH + 2 * DH:
                        pe.wait_ge(*fox_ready.at2(l, 1))
                    if j:
                        pe.wait_ge(*t2_taken.at2(l, j))
                    for i, v in enumerate((q, k)):
                        for t in range(NT):
                            mm = pe.transpose(mp[0:w, 0, T * i + P * t:T * i + P * (t + 1)], v[:, t, :], ident[:, :])
                    mm.then_inc(t2_done.sem, 1)

                def scores(j):
                    w = job_width(j)
                    pe.wait_ge(*t2_taken.at2(l, j + 1))
                    if j:
                        pe.wait_ge(*s2_max.at2(l, j))
                    qk = qkt[0:w, j % 2, :]
                    pe.matmul(mp[:, 1, 0:P], qk[:, 0:P], qk[:, T:T + P], start=True, stop=True)
                    pe.matmul(mp[:, 1, P:3 * P], qk[:, P:T], qk[:, T:2 * T], start=True, stop=True).then_inc(s2_done.sem, 1)

                def turn_p(j):
                    pe.wait_ge(*e2_done.at2(l, 2 * j + 2))
                    if j:
                        pe.wait_ge(*p2_taken.at2(l, j))
                    for a in range(3):
                        mm = pe.transpose(mp[:, 2, P * a:P * (a + 1)], sc2[:, j % 2, P * a:P * (a + 1)], ident[:, :])
                    mm.then_inc(p2_done.sem, 1)

                def weigh(j):
                    pe.wait_ge(*p2_taken.at2(l, j + 1))
                    if j:
                        pe.wait_ge(*o2_taken.at2(l, j))
                    else:
                        pe.wait_ge(*fox_ready.at2(l, 1))
                    v = job_operands(j)[2]
                    pe.matmul(mp[:, 3, 0:HD], pt2[:, 0:P], v[:, 0, :], start=True, stop=True)
                    pe.matmul(mp[:, 3, HD:2 * HD], pt2[:, P:2 * P], v[:, 0, :], start=True, stop=False)
                    pe.matmul(mp[:, 3, HD:2 * HD], pt2[:, 2 * P:3 * P], v[:, 1, :], start=False, stop=True).then_inc(o2_done.sem, 1)

                for i in range(AJ + 3):
                    if 0 <= i - 3 < AJ:
                        weigh(i - 3)
                    if 0 <= i - 2 < AJ:
                        turn_p(i - 2)
                    if 0 <= i - 1 < AJ:
                        scores(i - 1)
                    if i < AJ:
                        turn_qk(i)
                pe.wait_ge(*oa_ready.at2(l, 1))
                for b in range(4):
                    turn(b, oa, 2 * P * b).then_inc(tr_done.sem, 1)
                pe.wait_ge(*ft_lo.at2(l, X2_O + 4))
                for s in range(S2_OUT, S2_MOE):
                    product(s)
                pe.wait_ge(*h_ready.at2(l, 2))
                for b in range(4):
                    turn(b, x, 2 * P * b).then_inc(tr_done.sem, 1)
                pe.wait_ge(*ft_lo.at2(l, X2_H + 4))
                pe.wait_ge(rw_ready, 1)
                for t in range(NT):
                    ts = slice(P * t, P * (t + 1))
                    for c in range(KD):
                        for m, (a, w) in enumerate(((xt_lo, rw_lo), (xt_hi, rw_lo), (xt_lo, rw_hi), (xt_hi, rw_hi))):
                            mm = pe.matmul(mp[:, 0, NE * t:NE * (t + 1)], a[:, c, ts], w[:, c, :],
                                           start=c == 0 and m == 0, stop=c == KD - 1 and m == 3)
                mm.then_inc(logits_done.sem, 1)
                xt, mt = (xt_hi, xt_lo), (mt_hi, mt_lo)

                def turn_ab(e, banks_free):
                    pe.wait_ge(*ab2_ready.at2(l, e))
                    pe.wait_ge(*banks_free)
                    for b in range(2):
                        turn(b, ab2, 2 * P * b).then_inc(tr_done.sem, 1)

                uses = [2 * sum(1 for q in range(J2_MOE) if q % 2 == p) for p in range(2)]
                for i in range(4):
                    q = J2_MOE + i // 2
                    multiply(S2_MOE + i, S2_MOE + i + 1, q, 4, COLS, 4 * (i % 2), xt, i % 2 == 0, i % 2 == 1, uses[q % 2])
                with pe.Fori(1, NE) as e:
                    k, f = (e - 1) * 6, (e - 1) * 2
                    for i in range(6):
                        n = S2_MOE + 4 + i
                        q = J2_MOE + i // 2 if i < 4 else J2_MOE + (i - 4)
                        if i == 4:
                            pe.wait_ge(*ft_lo.at2(l, f + (X2_MOE + 2)))
                        use = (e - 1) * 4 + (uses[q % 2] + 2 + (2 if i >= 4 else 0))
                        multiply(n, k + (n + 1), q, 4, COLS, 4 * (i % 2) if i < 4 else 0, xt if i < 4 else mt,
                                 i % 2 == 0 or i >= 4, i % 2 == 1 or i >= 4, use)
                        if i == 0:
                            turn_ab(e, rsc_ready.at2(l, 1))
                turn_ab(NE, rsc_ready.at2(l, 1))
                pe.wait_ge(*ft_lo.at2(l, X2_LAYER))
                for i in range(2):
                    n = S2_LAYER - 2 + i
                    q = J2_MOE + i
                    multiply(n, n + 1, q, 4, COLS, 0, mt, True, True, uses[q % 2] + 2 + 4 * (NE - 1))


_INS = ["x", "c", "positions", "norm1_w", "norm2_w", "w_ada", "b_ada", "w_in", "pool_w", "pool_scale", "conv_w",
        "q_norm_w", "k_norm_w", "p_pool", "p_conv", "p_attn", "w_out", "w_gate", "w_up", "w_down",
        "positions_2", "ln_in_g_2", "ln_in_b_2", "w_in_2", "mla_q_norm_g_2", "mla_kv_norm_g_2", "mla_w_uq_2", "mla_w_ukv_2",
        "diff_lam_q1_2", "diff_lam_k1_2", "diff_lam_q2_2", "diff_lam_k2_2", "diff_subln_g_2", "fox_f_bias_2", "w_out_2",
        "ln1_g_2", "ln1_b_2", "router_w_2", "router_bias_2", "exp_w_gate_2", "exp_w_up_2", "exp_w_down_2", "ln2_g_2", "ln2_b_2"]


def kernel(**inputs):
    import concourse.bacc as bacc
    from concourse.bass_utils import run_bass_kernel_spmd

    nc = bacc.Bacc("TRN2", target_bir_lowering=False, num_devices=1)
    arrays, A = {}, {}
    for name in _INS:
        a = np.ascontiguousarray(inputs[name])
        arrays[f"in_{name}"] = a
    arrays.update(constants())
    for name, a in arrays.items():
        A[name.removeprefix("in_")] = nc.dram_tensor(name, a.shape, mybir.dt.from_np(a.dtype), kind="ExternalInput").ap()
    out = nc.dram_tensor("out_0", (1, T, D), F32, kind="ExternalOutput").ap()
    program(nc, A, out)
    return run_bass_kernel_spmd(nc, [arrays], core_ids=[0]).results[0]["out_0"]
```

```python
from contextlib import ExitStack

import numpy as np

import concourse.bass as bass
from concourse import mybir

F32 = mybir.dt.float32
F32R = mybir.dt.float32r
I32 = mybir.dt.int32
ALU = mybir.AluOpType
ACT = mybir.ActivationFunctionType
AX = mybir.AxisListType

P = 128
T = 256
D = 1024
KD = D // P
NT = T // P
LAYERS = 2
COLS = 512
UNITS = 4 * COLS
RAW = 3
SPLIT = 3
EPS = 1e-6

HEADS = 8
HD = 64
ROT = 16
WIN = (2, 4, 8, 16)
FF = 2816
FF_CHUNKS = FF // P
FF_BLOCKS = -(-FF // COLS)

WIN_COLS = [1024, 1536, 2048, 0, 512] + [2560 + COLS * j for j in range(6)]
WIN_JOBS = len(WIN_COLS)

S_WIN = 0
S_BR = S_WIN + 2 * WIN_JOBS
S_OUT = S_BR + 4
S_FF = S_OUT + 4
S_DOWN = S_FF + 4 * FF_BLOCKS
S_LAYER = S_DOWN + FF_CHUNKS // 2 + 1
assert S_LAYER % SPLIT == 0

ADA = 4
AFTER = {s: 1 for s in range(12)}
AFTER.update({S_FF + s: 1 for s in range(4)})


def ring_order():
    order = [("ada", a) for a in range(2 * ADA)]
    a = 2 * ADA
    for s in range(S_LAYER):
        order.append(("split", s))
        if s in AFTER:
            order.append(("ada", a))
            a += 1
    assert a == 6 * ADA and len(order) % RAW == 0
    return order


RING1 = ring_order()
G_LAYER = len(RING1)
G_OF = {item: g for g, item in enumerate(RING1)}

J_BR = WIN_JOBS
J_OUT = J_BR + 6
J_FF = J_OUT + 2
J_DOWN = J_FF + 2 * FF_BLOCKS
J_LAYER = J_DOWN + 2
PAIR_USES = ((J_LAYER + 1) // 2, J_LAYER // 2)

X_NORM1, X_POOL, X_CONV, X_ATT, X_MERGE, X_NORM2, X_ACT = 0, 4, 5, 6, 8, 12, 16
X_LAYER = X_ACT + FF_CHUNKS // 2

CHAIN = 1024

PC_BADA, PC_N1, PC_N2, PC_PS, PC_CW, PC_LAYER = 0, 48, 56, 64, 66, 72
PC_ROWS = PC_LAYER + KD
PAD = 16


IN2 = 2212
CQ, CKV, KR = 384, 256, 32
C_KR, C_DQ, C_DK, C_DV, C_FQ, C_FK, C_FV, C_FF = 640, 672, 928, 1184, 1440, 1696, 1952, 2208
MH, MQ, MN = 8, 96, 64
DH, DW, DROT = 4, 32, 8
FH, FW = 4, 66
NE, FE = 16, 512
ALPHA = (2 * LAYERS) ** 0.25
CAP = 64
LN_EPS = 1e-5
IN2_JOBS = -(-IN2 // COLS)
S2_UQ = 2 * IN2_JOBS
S2_UKV = S2_UQ + 2
S2_OUT = S2_UKV + 2
S2_MOE = S2_OUT + 4
S2_LAYER = S2_MOE + 6 * NE
assert S2_MOE % SPLIT == 0 and 6 % SPLIT == 0 and SPLIT == RAW
J2_UQ = IN2_JOBS
J2_UKV = J2_UQ + 2
J2_OUT = J2_UKV + 2
J2_MOE = J2_OUT + 2
J2_LAYER = J2_MOE + 4 * NE
PAIR2_USES = ((J2_LAYER + 1) // 2, J2_LAYER // 2)
X2_IN, X2_MLA, X2_O, X2_MOE = 0, 4, 7, 15
X2_H = 11
X2_LAYER = X2_MOE + 2 * NE
AJ = MH + 2 * DH + FH
CHAIN2 = 2048


def job2_end(q):
    if q < J2_UQ:
        return 2 * q + 1
    return S2_UQ + q - J2_UQ if q < J2_OUT else S2_OUT + 2 * (q - J2_OUT) + 1


class Count:

    def __init__(self, sem, per, prime=0, per2=0):
        self.sem, self.per, self.prime, self.per2 = sem, per, prime, per2

    def at(self, l, k):
        return self.sem, l * self.per + (k + self.prime)

    def at2(self, l, k):
        return self.sem, l * self.per2 + (k + self.prime + LAYERS * self.per)


def group_jobs(s):
    if s < S_BR:
        h = s % 2
        return [(s // 2, 0, COLS, [(i, 4 * h + i) for i in range(4)], h == 0, h == 1, "xt")]
    if s < S_BR + 2:
        b = s - S_BR
        return [(J_BR + 2 * b + n, COLS * n, COLS, [(i, 2 * b + i) for i in range(2)], True, True, "bt") for n in range(2)]
    if s < S_OUT:
        return [(J_BR + 4 + s - S_BR - 2, 0, COLS, [(i, 4 + i) for i in range(4)], True, True, "bt")]
    if s < S_FF:
        j, h = divmod(s - S_OUT, 2)
        return [(J_OUT + j, 0, COLS, [(i, 4 * h + i) for i in range(4)], h == 0, h == 1, "xt")]
    if s < S_DOWN:
        j, h = divmod(s - S_FF, 2)
        return [(J_FF + j, 0, min(COLS, FF - COLS * (j // 2)), [(i, 4 * h + i) for i in range(4)], h == 0, h == 1, "xt")]
    first, units = down_chunks(s - S_DOWN)
    return [(J_DOWN + n, COLS * n, COLS, [(i, first + i) for i in range(units)], s == S_DOWN, s == S_LAYER - 1, "at")
            for n in range(2)]


def down_chunks(i):
    full = FF_CHUNKS // 2 - 1
    return (2 * i, 2) if i < full else (2 * full + i - full, 1)


JOB_END = {q: s for s in range(S_LAYER) for q, _, _, _, _, last, _ in group_jobs(s) if last}


def constants():
    ident = np.eye(P, dtype=np.float32)
    causal = np.where(np.arange(P)[None, :] <= np.arange(P)[:, None], 0.0, -1e30).astype(np.float32)
    mask = np.concatenate([causal, np.zeros((P, P), np.float32), causal], axis=1)
    count = np.zeros((P, 2, T), np.float32)
    for g, w in enumerate(WIN):
        count[64 * (g % 2):64 * (g % 2) + 64, g // 2, :] = np.float32(1.0) / np.minimum(np.arange(T) + 1, w).astype(np.float32)
    chunk = np.where(np.arange(P)[None, :] // 64 <= np.arange(P)[:, None] // 64, 0.0, -1e30).astype(np.float32)
    mask2 = np.concatenate([chunk, np.zeros((P, P), np.float32), chunk], axis=1)
    tri = (np.arange(P)[:, None] <= np.arange(P)[None, :]).astype(np.float32)
    freq = np.concatenate([np.float32(500000.0) ** (-np.arange(0, r, 2, dtype=np.float32) / np.float32(r))
                           for r in (ROT, KR, DROT)]).astype(np.float32)
    i, j = np.arange(4)[:, None], np.arange(4)[None, :]
    order = np.stack([(j < i), (j > i)]).astype(np.float32).reshape(32)
    lam = np.array([[0.8 - 0.6 * np.exp(-0.3 * l), 1 - (0.8 - 0.6 * np.exp(-0.3 * l))] for l in range(LAYERS)]).astype(np.float32)

    def rows(a):
        return np.ascontiguousarray(np.broadcast_to(a.reshape(-1), (P, a.size)))

    return {"c_ident": ident, "c_mask": mask, "c_mask2": mask2, "c_tri": tri, "c_count": count.reshape(P, 2 * T),
            "c_slot": rows(np.tile(np.arange(1, CAP + 1), 2).astype(np.float32)), "c_freq": rows(freq), "c_order": rows(order), "c_lam": rows(lam)}


def program(nc, A, out):
    with ExitStack() as top:
        def sb(name, shape, dt=F32, ctx=top):
            return ctx.enter_context(nc.sbuf_tensor(name, shape, dt))

        def sem(name):
            return top.enter_context(nc.semaphore(name))

        def counted(name, per, prime=0, per2=0):
            return Count(sem(name), per, prime, per2)

        gp = top.enter_context(nc.psum_tensor("gp", [P, 2, NT, COLS], F32))
        mp = top.enter_context(nc.psum_tensor("mp", [P, 4, COLS], F32))

        raw = sb("raw", [P, RAW, UNITS])
        whi = sb("whi", [P, SPLIT, UNITS], F32R)
        wlo = sb("wlo", [P, SPLIT, UNITS], F32R)
        x = sb("x", [P, NT, D])
        xt_hi = sb("xt_hi", [P, KD, T], F32R)
        xt_lo = sb("xt_lo", [P, KD, T], F32R)
        ft = sb("ft", [P, 2, 2 * T])
        ident = sb("ident", [P, P])
        ones = sb("ones", [P, P])
        mask = sb("mask", [P, 3 * P])
        NF = (ROT + KR + DROT) // 2
        freq = sb("freq", [P, NF])
        order = sb("order", [P, 2, 16])
        lamc = sb("lamc", [P, LAYERS, 2])
        posi = sb("posi", [P, 2, NT], I32)
        posf = sb("posf", [P, 2, NT])
        ang = sb("ang", [P, NT, 2, NF])
        angk = sb("angk", [P, NT, 2, NF])
        cos2, sin2 = ([sb(f"{n}{r}", [P, NT, r]) for r in (ROT, KR, DROT)] for n in ("cos", "sin"))
        rv = sb("rv", [P, 32])
        rs = sb("rs", [P, 32])
        rr = sb("rr", [P, 32])
        rt = sb("rt", [P, 32])
        ssq = sb("ssq", [P, NT])

        one = ExitStack()
        acc = sb("acc", [P, 2, D], ctx=one)
        grow = sb("grow", [P, 2, D], ctx=one)
        count = sb("count", [P, 2, T], ctx=one)
        stage = sb("stage", [PC_ROWS, LAYERS, P], ctx=one)
        pcol = sb("pcol", [P, LAYERS, PC_ROWS], ctx=one)
        pcur = sb("pcur", [P, PC_LAYER], ctx=one)
        cact = sb("cact", [P, KD], ctx=one)
        csig = sb("csig", [P, KD], ctx=one)
        qkw = sb("qkw", [P, LAYERS, 2, HD], ctx=one)
        qkcur = sb("qkcur", [P, 2, HD], ctx=one)
        poolcur = sb("poolcur", [P, 2, P], ctx=one)
        poolw = sb("poolw", [P, LAYERS, 2, P], ctx=one)
        modc = sb("modc", [P, 6, KD], ctx=one)
        scol = sb("scol", [P, 2, KD], ctx=one)
        mix = ExitStack()
        u = sb("u", [P, NT, 5 * COLS], ctx=mix)
        gl = sb("gl", [P, NT, 6 * COLS], ctx=mix)
        qt = sb("qt", [P, 4, T], ctx=mix)
        kt = sb("kt", [P, 4, T], ctx=mix)
        bt_hi = sb("bt_hi", [P, 8, T], F32R, ctx=mix)
        bt_lo = sb("bt_lo", [P, 8, T], F32R, ctx=mix)
        sc = sb("sc", [P, 2, 3 * P], ctx=mix)
        pt = sb("pt", [P, 3 * P], ctx=mix)
        nmax = sb("nmax", [P, 2, NT], ctx=mix)
        rsum = sb("rsum", [P, 2, NT], ctx=mix)
        rinv = sb("rinv", [P, 2, NT], ctx=mix)
        w1 = sb("w1", [P, 2, PAD + T], ctx=mix)
        pp, zp, w2 = (u[:, :, 3 * COLS + i * (PAD + T):3 * COLS + (i + 1) * (PAD + T)] for i in range(3))
        bg = sb("bg", [P, 2, T], ctx=mix)
        mix.close()
        ffn = ExitStack()
        at_hi = sb("at_hi", [P, FF_CHUNKS, T], F32R, ctx=ffn)
        at_lo = sb("at_lo", [P, FF_CHUNKS, T], F32R, ctx=ffn)
        sg = sb("sg", [P, NT, COLS], ctx=ffn)
        ab = sb("ab", [P, NT, COLS], ctx=ffn)
        xn2 = sb("xn2", [P, NT, D], ctx=ffn)
        ffn.close()
        one.close()

        two = ExitStack()
        mask2 = sb("mask2", [P, 3 * P], ctx=two)
        tri = sb("tri", [P, P], ctx=two)
        lnw = sb("lnw", [P, 2, D], ctx=two)
        cen = sb("cen", [P, NT, D], ctx=two)
        lsum = sb("lsum", [P, NT], ctx=two)
        lsum4 = sb("lsum4", [P, 2 * NT], ctx=two)
        mean = sb("mean", [P, NT], ctx=two)
        cg = sb("cg", [P, LAYERS, CQ + CKV], ctx=two)
        lamr = sb("lamr", [P, LAYERS, 4, DW], ctx=two)
        subg = sb("subg", [P, LAYERS, HD], ctx=two)
        fbias = sb("fbias", [P, LAYERS, FH], ctx=two)
        rw = sb("rw", [P, KD, NE], ctx=two)
        rw_hi = sb("rw_hi", [P, KD, NE], F32R, ctx=two)
        rw_lo = sb("rw_lo", [P, KD, NE], F32R, ctx=two)
        rbias = sb("rbias", [P, NE], ctx=two)
        cgc = sb("cgc", [P, CQ + CKV], ctx=two)
        subc = sb("subc", [P, HD], ctx=two)
        lamt = sb("lamt", [P, 2, DW], ctx=two)
        lame = sb("lame", [P, 2], ctx=two)
        nlam = sb("nlam", [P, 1], ctx=two)
        lamq = sb("lamq", [P, 4, DW], ctx=two)
        lami = sb("lami", [P, 1], ctx=two)
        fbc = sb("fbc", [P, FH], ctx=two)
        pr = sb("pr", [P, NT, IN2], ctx=two)
        mt_hi = sb("mt_hi", [P, 6, T], F32R, ctx=two)
        mt_lo = sb("mt_lo", [P, 6, T], F32R, ctx=two)
        qm = sb("qm", [P, NT, MH, MQ], ctx=two)
        km = sb("km", [P, NT, MH, MQ], ctx=two)
        vm = sb("vm", [P, NT, MH, HD], ctx=two)
        fq = sb("fq", [P, NT, FH, FW], ctx=two)
        fk = sb("fk", [P, NT, FH, FW], ctx=two)
        rt1 = sb("rt1", [P, NT * MH * KR], ctx=two)
        rt2 = sb("rt2", [P, NT * MH * KR], ctx=two)
        od = sb("od", [P, NT, DH * HD], ctx=two)
        qkt = sb("qkt", [P, 2, 4 * P], ctx=two)
        sc2 = sb("sc2", [P, 3, 3 * P], ctx=two)
        pt2 = sb("pt2", [P, 3 * P], ctx=two)
        nmax2 = sb("nmax2", [P, 3, NT], ctx=two)
        rsum2 = sb("rsum2", [P, 3, NT], ctx=two)
        rinv2 = sb("rinv2", [P, 3, NT], ctx=two)
        fz = sb("fz", [P, NT, FH], ctx=two)
        fe = sb("fe", [P, NT, FH], ctx=two)
        fl = sb("fl", [P, NT, FH], ctx=two)
        rsc = sb("rsc", [P, NT, NE], ctx=two)
        rb = sb("rb", [P, NT, NE], ctx=two)
        cmp1 = sb("cmp1", [P, 8, 16], ctx=two)
        cmp2 = sb("cmp2", [P, 8, 16], ctx=two)
        rank = sb("rank", [P, 8, 4], ctx=two)
        gs = sb("gs", [P, 8], ctx=two)
        gr = sb("gr", [P, 8], ctx=two)
        den = sb("den", [P, NT], ctx=two)
        dg = sb("dg", [P, NT, NE], ctx=two)
        slots = sb("slots", [P, 2 * CAP], ctx=two)
        key = sb("key", [P, NT, NE + 1], ctx=two)
        many = sb("many", [P, 1], ctx=two)
        dense_i = sb("dense_i", [P, 1], I32, ctx=two)
        two.close()
        sg2, ab2, junk = pr[:, :, 0:COLS], pr[:, :, COLS:2 * COLS], pr[:, :, D:2 * D]
        gx, ux, gxl, uxl = pr[0:CAP, 0, 0:COLS], pr[0:CAP, 1, 0:COLS], pr[0:CAP, 0, COLS:D], pr[0:CAP, 1, COLS:D]
        ax, yx = pr[0:CAP, :, D:D + COLS // 2], pr[:, :, D + COLS:2 * D]
        pick, place = pr[:, :, D + COLS // 2:D + COLS // 2 + CAP], pr[:, :, D + COLS // 2 + CAP:D + COLS // 2 + 3 * CAP]
        back = cgc[:, 0:T]
        xg, ag = xt_hi[:, :, 0:2 * CAP], mt_hi[:, 0:4, 0:2 * CAP]
        oa = cen
        xn1 = gl[:, :, 0:D]
        merged = u[:, :, 3 * COLS:5 * COLS]
        o = u[:, :, 0:COLS]
        stationary = {"xt": (xt_hi, xt_lo), "bt": (bt_hi, bt_lo), "at": (at_hi, at_lo)}

        landed = [counted(f"landed{i}", 16 * G_LAYER // RAW, 0, 16 * S2_LAYER // RAW) for i in range(RAW)]
        raw_read = [counted(f"raw_read{i}", G_LAYER // RAW, 1, S2_LAYER // RAW) for i in range(RAW)]
        hi_done = counted("hi_done", S_LAYER, 0, S2_LAYER)
        w_used = counted("w_used", S_LAYER, SPLIT, S2_LAYER)
        pair_free = [counted(f"pair_free{p}", 2 * PAIR_USES[p], 2, 2 * PAIR2_USES[p]) for p in range(2)]
        consts_in, x_in, params_in, params_t, zeroed = map(sem, ("consts_in", "x_in", "params_in", "params_t", "zeroed"))
        params_ready, csig_ready, ang_ready, rope_ready = map(sem, ("params_ready", "csig_ready", "ang_ready", "rope_ready"))
        acc_done = counted("acc_done", 6)
        acc_read = counted("acc_read", 6, 2)
        mod_taken = counted("mod_taken", 6, 1)
        grow_in = counted("grow_in", 32)
        sq_done = counted("sq_done", 6)
        rv_ready = counted("rv_ready", 3)
        rs_ready = counted("rs_ready", 3)
        rr_ready = counted("rr_ready", 3)
        xn_ready = counted("xn_ready", 4)
        tr_done = counted("tr_done", X_LAYER - 1, 0, X2_LAYER)
        ft_ready = counted("ft_ready", X_LAYER, 0, X2_LAYER)
        ft_hi = counted("ft_hi", X_LAYER, 0, X2_LAYER)
        ft_lo = counted("ft_lo", X_LAYER, 2, X2_LAYER)
        x_final = counted("x_final", 4, 1)
        qk_ready = counted("qk_ready", 1)
        qkt_done = counted("qkt_done", 1)
        qkt_taken = counted("qkt_taken", 4)
        cu_ready = counted("cu_ready", 1)
        pct_done = counted("pct_done", 1)
        pct_taken = counted("pct_taken", 3)
        pads_zero = counted("pads_zero", 2)
        s_done = counted("s_done", HEADS)
        s_max = counted("s_max", HEADS)
        e_done = counted("e_done", 2 * HEADS)
        pt_done = counted("pt_done", HEADS)
        pt_taken = counted("pt_taken", HEADS)
        o_done = counted("o_done", HEADS)
        o_taken = counted("o_taken", HEADS)
        pooled = counted("pooled", 1)
        gates_ready = counted("gates_ready", 6)
        merged_ready = counted("merged_ready", 2)
        silu_done = counted("silu_done", FF_BLOCKS)
        ab_ready = counted("ab_ready", FF_BLOCKS)
        column_0 = sem("column_0")
        lnw_in = counted("lnw_in", 0, 32, 64)
        params2_in, rw_ready, rw_high = map(sem, ("params2_in", "rw_ready", "rw_high"))
        ln_sum = counted("ln_sum", 0, 2, 4)
        ln_cen = counted("ln_cen", 0, 2, 4)
        ln_sq = counted("ln_sq", 0, 2, 4)
        h_ready = counted("h_ready", 0, 2, 4)
        rv2_ready = counted("rv2_ready", 0, 1, 4)
        rs2_ready = counted("rs2_ready", 0, 1, 4)
        mla_sq = counted("mla_sq", 0, 0, 4)
        mla_ready = counted("mla_ready", 0, 0, 1)
        lam_sum = counted("lam_sum", 0, 0, 1)
        lam_exp = counted("lam_exp", 0, 0, 1)
        fz_ready = counted("fz_ready", 0, 0, 1)
        fe_ready = counted("fe_ready", 0, 0, 1)
        fl_ready = counted("fl_ready", 0, 0, 1)
        logf_ready = counted("logf_ready", 0, 0, 1)
        cum_done = counted("cum_done", 0, 0, 1)
        cum_taken = counted("cum_taken", 0, 0, 1)
        diff_ready = counted("diff_ready", 0, 0, 1)
        fox_ready = counted("fox_ready", 0, 0, 1)
        qm_ready = counted("qm_ready", 0, 0, 1)
        km_ready = counted("km_ready", 0, 0, 1)
        t2_done = counted("t2_done", 0, 0, AJ)
        t2_taken = counted("t2_taken", 0, 0, AJ)
        s2_done = counted("s2_done", 0, 0, AJ)
        s2_max = counted("s2_max", 0, 0, AJ)
        e2_done = counted("e2_done", 0, 0, 2 * AJ)
        p2_done = counted("p2_done", 0, 0, AJ)
        p2_taken = counted("p2_taken", 0, 0, AJ)
        o2_done = counted("o2_done", 0, 0, AJ)
        o2_taken = counted("o2_taken", 0, 0, AJ)
        od_sq = counted("od_sq", 0, 0, 1)
        oa_ready = counted("oa_ready", 0, 0, 1)
        logits_done = counted("logits_done", 0, 0, 1)
        rsc_ready = counted("rsc_ready", 0, 0, 1)
        silu2_done = counted("silu2_done", 0, 0, NE)
        ab2_ready = counted("ab2_ready", 0, 0, NE)
        x2_sum = counted("x2_sum", 0, 0, 2)
        y_taken = counted("y_taken", 0, 0, 2 * NE)
        chosen = counted("chosen", 0, 0, 1)
        chosen_sum = counted("chosen_sum", 0, 0, 1)
        flag_ready = counted("flag_ready", 0, 0, 1)
        flag_seen = sem("flag_seen")
        loads = sem("loads")
        pick_ready = counted("pick_ready", 0, 0, NE + 1)
        gathered = counted("gathered", 0, 0, NE + 1)
        xg_high = counted("xg_high", 0, 0, NE + 1)
        xg_low = counted("xg_low", 0, 0, NE + 1)
        gate_out = counted("gate_out", 0, 0, NE)
        gate_sum = counted("gate_sum", 0, 0, NE)
        silux = counted("silux", 0, 0, NE)
        up_out = counted("up_out", 0, 0, NE)
        up_sum = counted("up_sum", 0, 0, NE)
        ax_ready = counted("ax_ready", 0, 0, NE)
        place_ready = counted("place_ready", 0, 0, NE)
        ax_turned = counted("ax_turned", 0, 0, NE)
        back_ready = counted("back_ready", 0, 0, NE)
        ag_high = counted("ag_high", 0, 0, NE)
        ag_low = counted("ag_low", 0, 0, NE)
        yx_ready = counted("yx_ready", 0, 2, 2 * NE)
        y_zero = counted("y_zero", 0, 0, 2)
        y_done = counted("y_done", 0, 0, 1)
        out_done = sem("out_done")
        rows_free = sem("rows_free")
        v_chain = sem("v_chain")
        v_moe = sem("v_moe")

        block = top.enter_context(nc.Block())

        def weights(item, l):
            kind, n = item
            if kind == "ada":
                vec, i = divmod(n, ADA)
                return A["w_ada"][l, 2 * P * i:2 * P * (i + 1), D * vec:D * (vec + 1)], 2, D
            h = n % 2
            if n < S_BR:
                c = WIN_COLS[n // 2]
                return A["w_in"][l, 4 * P * h:4 * P * (h + 1), c:c + COLS], 4, COLS
            if n < S_BR + 2:
                return A[("p_pool", "p_conv")[n - S_BR]][l, :, :], 2, D
            if n < S_OUT:
                j = n - S_BR - 2
                return A["p_attn"][l, :, COLS * j:COLS * (j + 1)], 4, COLS
            if n < S_FF:
                j = (n - S_OUT) // 2
                return A["w_out"][l, 4 * P * h:4 * P * (h + 1), COLS * j:COLS * (j + 1)], 4, COLS
            if n < S_DOWN:
                j, r = divmod(n - S_FF, 4)
                wide = min(COLS, FF - COLS * j)
                return A["w_gate" if r < 2 else "w_up"][l, 4 * P * h:4 * P * (h + 1), COLS * j:COLS * j + wide], 4, wide
            first, units = down_chunks(n - S_DOWN)
            return A["w_down"][l, P * first:P * (first + units), :], units, D

        def weights2(s, l):
            if s < S2_UQ:
                j, h = divmod(s, 2)
                wide = min(COLS, IN2 - COLS * j)
                return A["w_in_2"][l, 4 * P * h:4 * P * (h + 1), COLS * j:COLS * j + wide], 4, wide
            if s < S2_UKV:
                wide = MH * MQ // 2
                return A["mla_w_uq_2"][l, :, wide * (s - S2_UQ):wide * (s - S2_UQ + 1)], 3, wide
            if s < S2_OUT:
                return A["mla_w_ukv_2"][l, :, COLS * (s - S2_UKV):COLS * (s - S2_UKV + 1)], 2, COLS
            j, h = divmod(s - S2_OUT, 2)
            return A["w_out_2"][l, 4 * P * h:4 * P * (h + 1), COLS * j:COLS * (j + 1)], 4, COLS

        def expert_weights(l, e, i):
            if i < 4:
                return A["exp_w_gate_2" if i < 2 else "exp_w_up_2"][l, e, 4 * P * (i % 2):4 * P * (i % 2 + 1), :]
            return A["exp_w_down_2"][l, e, :, COLS * (i - 4):COLS * (i - 3)]

        def slot(buf, n, units, cols):
            return buf[:, n, 0:units * cols].rearrange("p (k n) -> p k n", k=units)

        def job_width(j):
            return MQ if j < MH else DW if j < MH + 2 * DH else FW

        def job_operands(j):
            if j < MH:
                return qm[:, :, j, :], km[:, :, j, :], vm[:, :, j, :], MQ ** -0.5, mask2
            if j < MH + 2 * DH:
                i = j - MH
                return (pr[:, :, C_DQ + DW * i:C_DQ + DW * (i + 1)], pr[:, :, C_DK + DW * i:C_DK + DW * (i + 1)],
                        pr[:, :, C_DV + HD * (i // 2):C_DV + HD * (i // 2 + 1)], DW ** -0.5, mask2)
            i = j - MH - 2 * DH
            return fq[:, :, i, :], fk[:, :, i, :], pr[:, :, C_FV + HD * i:C_FV + HD * (i + 1)], HD ** -0.5, mask

        GATE_PAIR = J2_MOE % 2
        POOL_SPLITS = (2, 5)
        bank_gate, bank_up, bank_y1, bank_tr = gp[:, 0, 0, :], gp[:, 0, 1, :], gp[:, 1, 0, :], gp[:, 1, 1, :]

        def chunks(bank):
            return bank.rearrange("p (k t) -> p k t", k=2)

        @block.sync
        def _(sp):
            for name, tile in (("c_ident", ident[:, :]), ("c_mask", mask[:, :]),
                               ("c_count", count[:, :, :].rearrange("p a t -> p (a t)")), ("c_freq", freq[:, :]),
                               ("c_order", order[:, :, :].rearrange("p a n -> p (a n)")),
                               ("c_lam", lamc[:, :, :].rearrange("p l n -> p (l n)"))):
                sp.dma_start(tile, A[name]).then_inc(consts_in, 16)
            sp.dma_start(x[:, :, :], A["x"].rearrange("b (t p) d -> p (b t) d", p=P)).then_inc(x_in, 16)
            with sp.Fori(0, LAYERS) as l:
                for g, item in enumerate(RING1):
                    src, units, cols = weights(item, l)
                    sp.wait_ge(*raw_read[g % RAW].at(l, g // RAW))
                    if item == ("split", 2 * WIN_COLS.index(0)):
                        sp.sem_inc(column_0, 1)
                    sp.dma_start(slot(raw, g % RAW, units, cols),
                                 src.rearrange("(k p) n -> p k n", p=P)).then_inc(landed[g % RAW].sem, 16)
            with sp.Fori(0, LAYERS) as l:
                def load(n, k, src, units, cols):
                    sp.wait_ge(*raw_read[n % RAW].at2(l, k))
                    sp.dma_start(slot(raw, n % RAW, units, cols),
                                 src.rearrange("(k p) n -> p k n", p=P)).then_inc(landed[n % RAW].sem, 16)

                for s in range(S2_MOE):
                    src, units, cols = weights2(s, l)
                    load(s, s // RAW, src, units, cols)
                for i in range(4):
                    load(S2_MOE + i, (S2_MOE + i) // RAW, expert_weights(l, 0, i), 4, COLS)
                with sp.Fori(1, NE) as e:
                    for i in range(6):
                        load(S2_MOE + 4 + i, (e - 1) * 2 + (S2_MOE + 4 + i) // RAW, expert_weights(l, e if i < 4 else e - 1, i), 4, COLS)
                for i in range(4, 6):
                    load(S2_LAYER - 6 + i, (S2_LAYER - 6 + i) // RAW, expert_weights(l, NE - 1, i), 4, COLS)
            sp.wait_ge(*h_ready.at2(LAYERS, 0))
            sp.dma_start(out.rearrange("b (t p) d -> p (b t) d", p=P), x[:, :, :]).then_inc(out_done, 16)
            sp.wait_ge(out_done, 16)

        @block.gpsimd
        def _(pool):
            pool.memset(ones[:, :], 1.0).then_inc(zeroed, 1)
            pool.memset(poolw[:, :, :, :], 0.0).then_inc(zeroed, 1)
            pool.wait_ge(zeroed, 2)
            for l in range(LAYERS):
                rows = ((A["b_ada"][l], PC_BADA, 48), (A["norm1_w"][l], PC_N1, KD), (A["norm2_w"][l], PC_N2, KD),
                        (A["pool_scale"][l], PC_PS, 2), (A["c"][0], PC_LAYER, KD))
                for src, at, n in rows:
                    pool.dma_start(stage[at:at + n, l, :], src.rearrange("(a p) -> a p", p=P)).then_inc(params_in, 16)
                pool.dma_start(stage[PC_CW:PC_CW + 6, l, :],
                               A["conv_w"][l].rearrange("k (a p) -> (k a) p", p=P)).then_inc(params_in, 16)
                for i, name in enumerate(("q_norm_w", "k_norm_w")):
                    pool.dma_start(qkw[:, l, i, :], A[name][l].partition_broadcast(P)).then_inc(params_in, 16)
                for g in range(4):
                    h = 64 * (g % 2)
                    pool.dma_start(poolw[h:h + 64, l, g // 2, h:h + 64], A["pool_w"][l, g, :, :]).then_inc(params_in, 16)
            for i, name in enumerate(("positions", "positions_2")):
                for t in range(NT):
                    pool.dma_start(posi[:, i, t:t + 1],
                                   A[name][0, P * t:P * (t + 1)].rearrange("(p a) -> p a", a=1)).then_inc(params_in, 16)
            with pool.Fori(0, LAYERS) as l:
                pool.wait_ge(*x_final.at(l, 0))
                for i, vec in enumerate((2, 5)):
                    pool.dma_start(grow[:, i, :],
                                   A["b_ada"][l, D * vec:D * (vec + 1)].partition_broadcast(P)).then_inc(grow_in.sem, 16)
            pool.wait_ge(*x_final.at(LAYERS, 0))

            def norm_rows(gain, bias):
                pool.dma_start(lnw[:, 0, :], gain.partition_broadcast(P)).then_inc(lnw_in.sem, 16)
                pool.dma_start(lnw[:, 1, :], bias.partition_broadcast(P)).then_inc(lnw_in.sem, 16)

            norm_rows(A["ln_in_g_2"], A["ln_in_b_2"])
            pool.dma_start(mask2[:, :], A["c_mask2"]).then_inc(params2_in, 16)
            pool.dma_start(tri[:, :], A["c_tri"]).then_inc(params2_in, 16)
            pool.dma_start(slots[:, :], A["c_slot"]).then_inc(params2_in, 16)
            for l in range(LAYERS):
                for dst, src in ((cg[:, l, 0:CQ], A["mla_q_norm_g_2"]), (cg[:, l, CQ:CQ + CKV], A["mla_kv_norm_g_2"]),
                                 (lamr[:, l, 0, :], A["diff_lam_q1_2"]), (lamr[:, l, 1, :], A["diff_lam_q2_2"]),
                                 (lamr[:, l, 2, :], A["diff_lam_k1_2"]), (lamr[:, l, 3, :], A["diff_lam_k2_2"]),
                                 (subg[:, l, :], A["diff_subln_g_2"]), (fbias[:, l, :], A["fox_f_bias_2"])):
                    pool.dma_start(dst, src[l].partition_broadcast(P)).then_inc(params2_in, 16)
            pool.dma_start(rw[:, :, :], A["router_w_2"].rearrange("(k p) n -> p k n", p=P)).then_inc(params2_in, 16)
            pool.dma_start(rbias[:, :], A["router_bias_2"].partition_broadcast(P)).then_inc(params2_in, 16)
            with pool.Fori(0, LAYERS) as l:
                pool.wait_ge(*h_ready.at2(l, 0))
                pool.sem_inc(rows_free, 1)
                norm_rows(A["ln1_g_2"][l], A["ln1_b_2"][l])
                pool.wait_ge(*h_ready.at2(l, 2))
                pool.sem_inc(rows_free, 1)
                norm_rows(A["ln2_g_2"][l], A["ln2_b_2"][l])
                pool.wait_ge(*flag_ready.at2(l, 1))
                pool.sem_inc(loads, 1)
                dense = pool.value_load(dense_i[0:1, 0:1], min_val=0, max_val=1)
                with pool.If(dense == 0):
                    with pool.Fori(1, NE) as e:
                        for i in POOL_SPLITS:
                            n = S2_MOE + 6 + i
                            pool.wait_ge(*hi_done.at2(l, (e - 1) * 6 + (n + 1)))
                            pool.tensor_tensor(slot(wlo, n % SPLIT, 4, COLS), slot(raw, n % RAW, 4, COLS),
                                               slot(whi, n % SPLIT, 4, COLS).bitcast(F32), ALU.subtract).then_inc(raw_read[n % RAW].sem, 1)

        PARAMS = 16 * (LAYERS * 12 + 2 * NT)
        PARAMS2 = 16 * (LAYERS * 8 + 5)

        @block.scalar
        def _(act):
            act.wait_ge(params_ready, LAYERS)
            act.sem_inc(yx_ready.sem, yx_ready.prime)
            act.activation(csig[:, :], pcol[:, 0, PC_LAYER:PC_ROWS], ACT.Sigmoid).then_inc(csig_ready, 1)
            act.wait_ge(ang_ready, 1)
            act.activation(angk[:, :, :, :], ang[:, :, :, :], ACT.Sin).then_inc(rope_ready, 1)
            act.wait_ge(x_in, 16)

            with act.Fori(0, LAYERS) as l:
                def split(s):
                    g = G_OF["split", s]
                    _, units, cols = weights(("split", s), l)
                    act.wait_ge(*landed[g % RAW].at(l, 16 * (g // RAW + 1)))
                    act.wait_ge(*w_used.at(l, s + 1 - SPLIT))
                    act.activation(slot(whi, s % SPLIT, units, cols), slot(raw, g % RAW, units, cols),
                                   ACT.Copy).then_inc(hi_done.sem, 1)

                def high(f, dst):
                    act.wait_ge(*ft_ready.at(l, f + 1))
                    act.activation(dst, chunks(ft[:, f % 2, :]), ACT.Copy).then_inc(ft_hi.sem, 1)

                def root(i, n):
                    act.wait_ge(*rv_ready.at(l, i + 1))
                    act.activation(rs[:, 0:n], rv[:, 0:n], ACT.Sqrt).then_inc(rs_ready.sem, 1)

                def normalise(xn, i):
                    for t in range(NT):
                        act.activation(xn[:, t, :], x[:, t, :], ACT.Square, accum_out=ssq[:, t:t + 1]).then_inc(sq_done.sem, 1)
                    root(i, NT)
                    act.wait_ge(*rr_ready.at(l, i + 1))
                    for t in range(NT):
                        act.activation(xn[:, t, :], x[:, t, :], ACT.Copy, scale=rr[:, t:t + 1]).then_inc(xn_ready.sem, 1)

                def take_w_in(j):
                    act.wait_ge(*w_used.at(l, JOB_END[j] + 1))
                    if j < 5:
                        act.activation(u[:, 0, COLS * j:COLS * (j + 1)], gp[:, j % 2, 0, :], ACT.Copy).then_inc(pair_free[j % 2].sem, 1)
                    else:
                        act.activation(gl[:, :, COLS * (j - 5):COLS * (j - 4)], gp[:, j % 2, :, :], ACT.Copy).then_inc(pair_free[j % 2].sem, 2)

                act.wait_ge(*x_final.at(l, 0))
                normalise(xn1, 0)
                split(0)
                split(1)
                for b in range(4):
                    high(X_NORM1 + b, xt_hi[:, 2 * b:2 * b + 2, :])
                for s in range(10):
                    split(s + 2)
                    if s % 2:
                        take_w_in(s // 2)
                    if s == 5:
                        act.wait_ge(*pair_free[0].at(l, 2))
                        act.wait_ge(*pair_free[1].at(l, 2))
                        for t in range(NT):
                            act.activation(gl[:, t, 0:D], u[:, t, 0:D], ACT.Square).then_inc(sq_done.sem, 1)
                        root(1, 2 * NT * HEADS)
                for i in range(12):
                    split(10 + i + 2)
                    if i % 2:
                        take_w_in(5 + i // 2)
                    if i == 0:
                        act.wait_ge(*qkt_done.at(l, 1))
                        for b in range(4):
                            dst = (qt, kt)[b // 2][:, 2 * (b % 2):2 * (b % 2) + 2, :]
                            act.activation(dst, chunks(mp[:, b, :]), ACT.Copy).then_inc(qkt_taken.sem, 1)
                    if i == 1:
                        act.wait_ge(*pct_done.at(l, 1))
                        for b, dst in enumerate((pp[:, :, PAD:PAD + T], zp[:, :, PAD:PAD + T], bg[:, :, :])):
                            act.activation(dst, chunks(mp[:, b, :]), ACT.Copy).then_inc(pct_taken.sem, 1)
                    h = i - 2
                    if 0 <= h < HEADS:
                        act.wait_ge(*s_max.at(l, h + 1))
                        for t, (a, b) in enumerate(((0, P), (P, 3 * P))):
                            act.activation(sc[:, h % 2, a:b], sc[:, h % 2, a:b], ACT.Exp, bias=nmax[:, h % 2, t:t + 1],
                                           accum_out=rsum[:, h % 2, t:t + 1]).then_inc(e_done.sem, 1)
                    h = i - 3
                    if 0 <= h < HEADS:
                        act.wait_ge(*pt_done.at(l, h + 1))
                        act.activation(pt[:, :], mp[:, 2, 0:3 * P], ACT.Copy).then_inc(pt_taken.sem, 1)
                high(X_POOL, bt_hi[:, 0:2, :])
                high(X_CONV, bt_hi[:, 2:4, :])
                for i in range(6):
                    act.wait_ge(*pair_free[(5 + i) % 2].at(l, 2 * ((5 + i) // 2) + 2))
                    act.activation(gl[:, :, COLS * i:COLS * (i + 1)], gl[:, :, COLS * i:COLS * (i + 1)], ACT.Sigmoid).then_inc(gates_ready.sem, 1)
                    if i == 1:
                        for b in range(2):
                            high(X_ATT + b, bt_hi[:, 4 + 2 * b:6 + 2 * b, :])
                for s in range(S_BR, S_OUT):
                    split(s + 2)
                for b in range(4):
                    high(X_MERGE + b, xt_hi[:, 2 * b:2 * b + 2, :])
                for s in range(S_OUT, S_FF):
                    split(s + 2)
                act.wait_ge(*x_final.at(l, 2))
                normalise(xn2, 2)
                for b in range(4):
                    high(X_NORM2 + b, xt_hi[:, 2 * b:2 * b + 2, :])
                for s in range(S_FF, S_DOWN):
                    split(s + 2)
                    j, r = divmod(s - S_FF, 4)
                    wide = min(COLS, FF - COLS * j)
                    if r == 2:
                        if j >= 1:
                            for b in range(2):
                                high(X_ACT + 2 * (j - 1) + b, at_hi[:, 4 * (j - 1) + 2 * b:4 * (j - 1) + 2 * b + 2, :])
                            act.wait_ge(*ab_ready.at(l, j))
                        q = J_FF + 2 * j
                        act.wait_ge(*w_used.at(l, JOB_END[q] + 1))
                        act.activation(sg[:, :, 0:wide], gp[:, q % 2, :, 0:wide], ACT.Silu).then_inc(silu_done.sem, 1)
                for s in range(S_DOWN, S_LAYER - 2):
                    split(s + 2)
                    if s == S_DOWN + 1:
                        high(X_ACT + 2 * (FF_BLOCKS - 1), at_hi[:, FF_CHUNKS - 2:FF_CHUNKS, :])

            def layer_norm(src, wait_sum, wait_cen, root_of):
                for t in range(NT):
                    act.activation(junk[:, t, :], src[:, t, :], ACT.Copy, accum_out=lsum[:, t:t + 1]).then_inc(ln_sum.sem, 1)
                act.wait_ge(*wait_cen)
                act.wait_ge(*wait_sum)
                for t in range(NT):
                    act.activation(junk[:, t, :], cen[:, t, :], ACT.Square, accum_out=ssq[:, t:t + 1]).then_inc(ln_sq.sem, 1)
                act.wait_ge(*root_of)
                act.activation(rs[:, 0:NT], rv[:, 0:NT], ACT.Sqrt).then_inc(rs2_ready.sem, 1)

            act.wait_ge(*x_final.at(LAYERS, 0))
            layer_norm(x, (ln_sum.sem, 2), (ln_cen.sem, 2), (rv2_ready.sem, 1))
            act.wait_ge(params2_in, PARAMS2)
            act.activation(rw_hi[:, :, :], rw[:, :, :], ACT.Copy).then_inc(rw_high, 1)

            with act.Fori(0, LAYERS) as l:
                def split_at(n, k, units, cols):
                    act.wait_ge(*landed[n % RAW].at2(l, k[0]))
                    act.wait_ge(*w_used.at2(l, k[1]))
                    act.activation(slot(whi, n % SPLIT, units, cols), slot(raw, n % RAW, units, cols),
                                   ACT.Copy).then_inc(hi_done.sem, 1)

                def split(s):
                    units, cols = weights2(s, l)[1:] if s < S2_MOE else (4, COLS)
                    split_at(s, (16 * (s // RAW + 1), s + 1 - SPLIT), units, cols)

                def high(f, dst, n=2, k=None):
                    act.wait_ge(*ft_ready.at2(l, f + 1 if k is None else k + 1))
                    act.activation(dst, ft[:, f % 2, 0:T * n].rearrange("p (k t) -> p k t", k=n), ACT.Copy).then_inc(ft_hi.sem, 1)

                def high_x(f0):
                    for b in range(4):
                        high(f0 + b, xt_hi[:, 2 * b:2 * b + 2, :])

                def take(q, dst):
                    act.wait_ge(*w_used.at2(l, job2_end(q) + 1))
                    act.activation(dst, gp[:, q % 2, 0, 0:dst.shape[-1]], ACT.Copy).then_inc(pair_free[q % 2].sem, 1)

                split(0)
                split(1)
                high_x(X2_IN)
                for s in range(S2_UQ):
                    split(s + 2)
                    if s % 2:
                        j = s // 2
                        take(j, pr[:, 0, COLS * j:min(COLS * (j + 1), IN2)])
                    if s == 3:
                        act.wait_ge(*pair_free[0].at2(l, 2))
                        act.wait_ge(*pair_free[1].at2(l, 2))
                        for t in range(NT):
                            act.activation(rt1[:, 0:CQ], pr[:, t, 0:CQ], ACT.Square, accum_out=lsum4[:, t:t + 1]).then_inc(mla_sq.sem, 1)
                            act.activation(rt2[:, 0:CKV], pr[:, t, CQ:CQ + CKV], ACT.Square, accum_out=lsum4[:, 2 + t:3 + t]).then_inc(mla_sq.sem, 1)
                            act.wait_ge(*mla_sq.at2(l, 2 * t + 2))
                        act.wait_ge(*rv2_ready.at2(l, 1))
                        act.activation(rs[:, 0:4], rv[:, 0:4], ACT.Sqrt).then_inc(rs2_ready.sem, 1)
                for b in range(3):
                    n = 2 if b < 2 else 1
                    high(X2_MLA + b, mt_hi[:, 2 * b:2 * b + n, :], n)
                act.wait_ge(*fz_ready.at2(l, 1))
                act.activation(fe[:, :, :], fe[:, :, :], ACT.Exp).then_inc(fe_ready.sem, 1)
                act.wait_ge(*lam_sum.at2(l, 1))
                act.activation(lame[:, :], lame[:, :], ACT.Exp).then_inc(lam_exp.sem, 1)
                act.wait_ge(*fe_ready.at2(l, 1))
                act.activation(fl[:, :, :], fe[:, :, :], ACT.Ln, bias=1.0).then_inc(fl_ready.sem, 1)
                for s in range(S2_UQ, S2_OUT):
                    split(s + 2)
                    q = J2_UQ + s - S2_UQ
                    if s < S2_UKV:
                        h = 4 * (s - S2_UQ)
                        take(q, qm[:, 0, h:h + 4, :].rearrange("p h d -> p (h d)"))
                for i in range(AJ + 4):
                    if i < AJ:
                        act.wait_ge(*t2_done.at2(l, i + 1))
                        w = job_width(i)
                        act.activation(qkt[0:w, i % 2, :], mp[0:w, 0, :], ACT.Copy).then_inc(t2_taken.sem, 1)
                    j = i - 2
                    if 0 <= j < AJ:
                        act.wait_ge(*s2_max.at2(l, j + 1))
                        if j >= 3:
                            act.wait_ge(*o2_taken.at2(l, j - 2))
                        for t, (a, b) in enumerate(((0, P), (P, 3 * P))):
                            act.activation(sc2[:, j % 3, a:b], sc2[:, j % 3, a:b], ACT.Exp, bias=nmax2[:, j % 3, t:t + 1],
                                           accum_out=rsum2[:, j % 3, t:t + 1]).then_inc(e2_done.sem, 1)
                    j = i - 3
                    if 0 <= j < AJ:
                        act.wait_ge(*p2_done.at2(l, j + 1))
                        act.activation(pt2[:, :], mp[:, 2, 0:3 * P], ACT.Copy).then_inc(p2_taken.sem, 1)
                act.wait_ge(*rv2_ready.at2(l, 2))
                act.activation(rs[:, 0:NT * DH], rv[:, 0:NT * DH], ACT.Sqrt).then_inc(rs2_ready.sem, 1)
                high_x(X2_O)
                for s in range(S2_OUT, S2_MOE):
                    split(s + 2)
                act.wait_ge(*x2_sum.at2(l, 2))
                layer_norm(x, ln_sum.at2(l, 2), ln_cen.at2(l, 2), rv2_ready.at2(l, 3))
                high_x(X2_H)
                act.wait_ge(*logits_done.at2(l, 1))
                act.activation(rsc[:, :, :], mp[:, 0, 0:NT * NE].rearrange("p (t n) -> p t n", t=NT), ACT.Sigmoid).then_inc(rsc_ready.sem, 1)

                def silu(e, k):
                    act.wait_ge(*w_used.at2(l, k))
                    act.wait_ge(*ab2_ready.at2(l, e))
                    act.activation(sg2, gp[:, GATE_PAIR, :, :], ACT.Silu).then_inc(silu2_done.sem, 1)

                def part(src, dst, done):
                    act.activation(dst, src[CAP:2 * CAP, :], ACT.Copy).then_inc(done.sem, 1)

                def high_tokens(k):
                    act.wait_ge(*gathered.at2(l, k))
                    act.activation(xg[:, :, 0:CAP], bank_tr.rearrange("p (c s) -> p c s", c=KD), ACT.Copy).then_inc(xg_high.sem, 1)

                def take_turned(k):
                    act.wait_ge(*ax_turned.at2(l, k))
                    act.activation(back, bank_tr[:, T:2 * T], ACT.Copy).then_inc(back_ready.sem, 1)
                    act.activation(ag[:, :, 0:CAP], bank_tr[:, 0:T].rearrange("p (c s) -> p c s", c=4), ACT.Copy).then_inc(ag_high.sem, 1)

                def gate_part(n, e):
                    act.wait_ge(*w_used.at2(l, n))
                    if not isinstance(e, int):
                        act.wait_ge(*gate_sum.at2(l, e))
                    part(bank_gate, gxl, gate_out)

                def silu_x(e):
                    act.wait_ge(*gate_sum.at2(l, e + 1))
                    act.activation(gx, gx, ACT.Silu).then_inc(silux.sem, 1)

                def up_part(n, e):
                    act.wait_ge(*w_used.at2(l, n))
                    if not isinstance(e, int):
                        act.wait_ge(*up_sum.at2(l, e))
                    part(bank_up, uxl, up_out)

                def result(n, half):
                    act.wait_ge(*w_used.at2(l, n))
                    act.activation(yx[:, half, :], (bank_gate, bank_y1)[half], ACT.Copy).then_inc(yx_ready.sem, 1)

                def gathered_experts():
                    high_tokens(1)
                    for i in range(4):
                        split(S2_MOE + i + 2)
                        if i == 1:
                            gate_part(S2_MOE + 2, 0)
                        if i == 2:
                            silu_x(0)
                        if i == 3:
                            up_part(S2_MOE + 4, 0)
                            high_tokens(2)
                    with act.Fori(1, NE) as e:
                        k = (e - 1) * 6
                        for i in range(6):
                            n = S2_MOE + 6 + i
                            split_at(n, ((e - 1) * 32 + 16 * (n // RAW + 1), k + (n + 1 - SPLIT)), 4, COLS)
                            if i == 0:
                                take_turned(e)
                            if i == 1:
                                gate_part(k + (S2_MOE + 6), e)
                            if i == 2:
                                silu_x(e)
                            if i == 3:
                                up_part(k + (S2_MOE + 8), e)
                                high_tokens(e + 2)
                            if i >= 4:
                                result(k + (S2_MOE + 5 + i), i - 4)
                    take_turned(NE)
                    for half in range(2):
                        result(S2_LAYER - 1 + half, half)
                    act.sem_inc(ft_hi.sem, 2 * NE)
                    act.sem_inc(silu2_done.sem, NE)

                act.wait_ge(*flag_ready.at2(l, 1))
                act.sem_inc(loads, 1)
                dense = act.value_load(dense_i[0:1, 0:1], min_val=0, max_val=1)
                with act.If(dense == 0):
                    gathered_experts()
                with act.Else():
                    for i in range(4):
                        split(S2_MOE + i + 2)
                        if i == 1:
                            silu(0, S2_MOE + 2)
                    with act.Fori(1, NE) as e:
                        k = (e - 1) * 6
                        for i in range(6):
                            n = S2_MOE + 6 + i
                            split_at(n, ((e - 1) * 32 + 16 * (n // RAW + 1), k + (n + 1 - SPLIT)), 4, COLS)
                            if i == 1:
                                f = (e - 1) * 2
                                for b in range(2):
                                    high(X2_MOE + b, mt_hi[:, 2 * b:2 * b + 2, :], 2, f + (X2_MOE + b))
                                silu(e, k + (S2_MOE + 6))
                    for b in range(2):
                        high(X2_LAYER - 2 + b, mt_hi[:, 2 * b:2 * b + 2, :])
                    for c, n in ((xg_high, NE + 1), (gate_out, NE), (silux, NE), (up_out, NE), (back_ready, NE), (ag_high, NE), (yx_ready, 2 * NE)):
                        act.sem_inc(c.sem, n)
                act.wait_ge(*y_taken.at2(l, 2 * NE))
                layer_norm(cen, ln_sum.at2(l, 4), ln_cen.at2(l, 4), rv2_ready.at2(l, 4))

        @block.vector
        def _(dve):
            chain = [0]

            def link(ins, base=0):
                chain[0] += 1
                assert chain[0] < CHAIN
                ins.then_inc(v_chain, 1)
                dve.wait_ge(v_chain, base + chain[0])

            for slot_read in raw_read:
                dve.sem_inc(slot_read.sem, slot_read.prime)
            dve.sem_inc(x_final.sem, x_final.prime)
            dve.sem_inc(mod_taken.sem, mod_taken.prime)
            dve.sem_inc(ft_lo.sem, ft_lo.prime)
            dve.wait_ge(consts_in, 16 * 6)
            dve.wait_ge(params_in, PARAMS)
            dve.wait_ge(params_t, LAYERS)
            for l in range(LAYERS):
                dve.tensor_copy(pcol[:, l, :], mp[:, l, 0:PC_ROWS]).then_inc(params_ready, 1)
            dve.wait_ge(csig_ready, 1)
            link(dve.tensor_tensor(cact[:, :], pcol[:, 0, PC_LAYER:PC_ROWS], csig[:, :], ALU.mult))
            link(dve.tensor_copy(posf[:, :, :], posi[:, :, :]))
            for t in range(NT):
                for i in range(2):
                    for which, a, b in ((0, 0, ROT // 2), (1, ROT // 2, NF)):
                        link(dve.tensor_scalar(ang[:, t, i, a:b], freq[:, a:b], posf[:, which, t:t + 1], None, ALU.mult))
            for i, quarter in enumerate((0.25, 0.0)):
                link(dve.tensor_scalar(angk[:, :, i, :], ang[:, :, i, :], float(1.0 / (2 * np.pi)), quarter, ALU.mult, ALU.add))
            nearest = 1.5 * 2.0 ** 23
            link(dve.tensor_scalar(angk[:, :, :, :], angk[:, :, :, :], nearest, None, ALU.add))
            link(dve.tensor_scalar(angk[:, :, :, :], angk[:, :, :, :], nearest, None, ALU.subtract))
            two_pi = 6.28125
            parts = [two_pi, float(np.round((2 * np.pi - two_pi) * 2.0 ** 22) / 2.0 ** 22)]
            parts.append(float(2 * np.pi - sum(parts)))
            for c in parts:
                for i in range(2):
                    link(dve.scalar_tensor_tensor(out=ang[:, :, i, :], in0=angk[:, :, i, :], scalar=-c, in1=ang[:, :, i, :],
                                                  op0=ALU.mult, op1=ALU.add))
            link(dve.tensor_scalar(ang[:, :, 0, :], ang[:, :, 0, :], float(np.pi / 2), None, ALU.add))
            dve.tensor_scalar(ang[:, :, :, :], ang[:, :, :, :], 3.1415925, -3.1415925, ALU.min, ALU.max).then_inc(ang_ready, 1)
            dve.wait_ge(rope_ready, 1)
            a = 0
            for c, sn in zip(cos2, sin2):
                h = c.shape[2] // 2
                for i in range(2):
                    link(dve.tensor_copy(c[:, :, h * i:h * (i + 1)], angk[:, :, 0, a:a + h]))
                link(dve.tensor_scalar(sn[:, :, 0:h], angk[:, :, 1, a:a + h], -1.0, None, ALU.mult))
                link(dve.tensor_copy(sn[:, :, h:2 * h], angk[:, :, 1, a:a + h]))
                a += h
            dve.wait_ge(x_in, 16)
            dve.sem_inc(v_chain, CHAIN - chain[0])
            chain[0] = 0

            with dve.Fori(0, LAYERS) as l:
                def lk(ins):
                    link(ins, (l + 1) * CHAIN)

                def split(s):
                    g = G_OF["split", s]
                    _, units, cols = weights(("split", s), l)
                    dve.wait_ge(*hi_done.at(l, s + 1))
                    dve.tensor_tensor(slot(wlo, s % SPLIT, units, cols), slot(raw, g % RAW, units, cols),
                                      slot(whi, s % SPLIT, units, cols).bitcast(F32), ALU.subtract).then_inc(raw_read[g % RAW].sem, 1)
                    if s in AFTER:
                        ada(2 * ADA + s if s < 12 else 5 * ADA + s - S_FF)

                def ada(n):
                    g = G_OF["ada", n]
                    vec, i = divmod(n, ADA)
                    dve.wait_ge(*landed[g % RAW].at(l, 16 * (g // RAW + 1)))
                    if i == 0:
                        dve.wait_ge(*acc_read.at(l, vec - 1))
                    w, a = slot(raw, g % RAW, 2, D), acc[:, vec % 2, :]
                    for k in range(2):
                        c = cact[:, 2 * i + k:2 * i + k + 1]
                        if i == 0 and k == 0:
                            ins = dve.tensor_scalar(a, w[:, k, :], c, None, ALU.mult)
                        else:
                            ins = dve.scalar_tensor_tensor(out=a, in0=w[:, k, :], scalar=c, in1=a, op0=ALU.mult, op1=ALU.add)
                        if k == 0:
                            lk(ins)
                    ins.then_inc(raw_read[g % RAW].sem, 1)
                    dve.wait_ge(*raw_read[g % RAW].at(l, g // RAW + 1))
                    if i == ADA - 1:
                        dve.sem_inc(acc_done.sem, 1)

                def take_mod(vec):
                    dve.wait_ge(*acc_read.at(l, vec + 1))
                    if vec in (2, 5):
                        i = vec // 3
                        dve.wait_ge(*grow_in.at(l, 32))
                        dve.tensor_tensor(grow[:, i, :], mp[:, 0:2, :].rearrange("p a n -> p (a n)"), grow[:, i, :], ALU.add).then_inc(mod_taken.sem, 1)
                    else:
                        bank = {0: 0, 1: 1, 3: 2, 4: 0}[vec]
                        dve.tensor_tensor(modc[:, vec, :], mp[:, bank, 0:KD], pcur[:, KD * vec:KD * (vec + 1)], ALU.add).then_inc(mod_taken.sem, 1)

                def norm_columns(i, vec):
                    dve.wait_ge(*mod_taken.at(l, vec + 2))
                    at = (PC_N1, PC_N2)[i]
                    lk(dve.scalar_tensor_tensor(out=scol[:, i, :], in0=modc[:, vec + 1, :], scalar=1.0,
                                                in1=pcur[:, at:at + KD], op0=ALU.add, op1=ALU.mult))

                def rsqrt(i, n):
                    dve.wait_ge(*rs_ready.at(l, i + 1))
                    lk(dve.reciprocal(rr[:, 0:n], rs[:, 0:n]))
                    lk(dve.tensor_tensor(rt[:, 0:n], rr[:, 0:n], rr[:, 0:n], ALU.mult))
                    lk(dve.tensor_tensor(rt[:, 0:n], rt[:, 0:n], rv[:, 0:n], ALU.mult))
                    lk(dve.tensor_scalar(rt[:, 0:n], rt[:, 0:n], -0.5, 1.5, ALU.mult, ALU.add))
                    dve.tensor_tensor(rr[:, 0:n], rr[:, 0:n], rt[:, 0:n], ALU.mult).then_inc(rr_ready.sem, 1)

                def row_norm(i):
                    dve.wait_ge(*sq_done.at(l, 2 * i + 2))
                    dve.tensor_scalar(rv[:, 0:NT], ssq[:, :], 1.0 / D, EPS, ALU.mult, ALU.add).then_inc(rv_ready.sem, 1)
                    rsqrt(i, NT)

                def low(f, hi, lo):
                    dve.wait_ge(*ft_hi.at(l, f + 1))
                    dve.tensor_tensor(lo, chunks(ft[:, f % 2, :]), hi.bitcast(F32), ALU.subtract).then_inc(ft_lo.sem, 1)

                def ft_free(f):
                    dve.wait_ge(*ft_lo.at(l, f - 1))

                def bank_done(f):
                    dve.wait_ge(*tr_done.at(l, f + 1 - (f > X_CONV)))
                    ft_free(f)

                def plain(f, bank):
                    bank_done(f)
                    dve.tensor_copy(ft[:, f % 2, :], mp[:, bank, :]).then_inc(ft_ready.sem, 1)

                def spread(f0, n, dst, c0, copy, bank0=0):
                    hi, lo = dst
                    for b in range(n + 1):
                        if b < n:
                            copy(f0 + b, bank0 + b)
                        if b:
                            c = c0 + 2 * (b - 1)
                            low(f0 + b - 1, hi[:, c:c + 2, :], lo[:, c:c + 2, :])

                def normed(i, vec):
                    def copy(f, bank):
                        bank_done(f)
                        for k in range(2):
                            c = 2 * bank + k
                            ins = dve.tensor_scalar(ft[:, f % 2, T * k:T * (k + 1)], mp[:, bank, T * k:T * (k + 1)],
                                                    scol[:, i, c:c + 1], modc[:, vec, c:c + 1], ALU.mult, ALU.add)
                            if k == 0:
                                lk(ins)
                        ins.then_inc(ft_ready.sem, 1)
                    return copy

                def take_w_in(j):
                    dve.wait_ge(*w_used.at(l, JOB_END[j] + 1))
                    dve.tensor_copy(u[:, 1, COLS * j:COLS * (j + 1)], gp[:, j % 2, 1, :]).then_inc(pair_free[j % 2].sem, 1)

                def qk_norm_rope():
                    qk = u[:, :, 0:2 * COLS].rearrange("p t (h d) -> p t h d", d=HD)
                    n = 2 * NT * HEADS
                    dve.wait_ge(*sq_done.at(l, 4))
                    lk(dve.tensor_reduce(rt[:, 0:n].rearrange("p (t h) -> p t h", t=NT),
                                         gl[:, :, 0:D].rearrange("p t (h d) -> p t h d", d=HD), AX.X, ALU.add))
                    dve.tensor_scalar(rv[:, 0:n], rt[:, 0:n], 1.0 / HD, EPS, ALU.mult, ALU.add).then_inc(rv_ready.sem, 1)
                    rsqrt(1, n)
                    dve.wait_ge(*rr_ready.at(l, 2))
                    rb = rr[:, 0:n].rearrange("p (t h) -> p t h", t=NT).unsqueeze(3).broadcast_to((P, NT, 2 * HEADS, HD))
                    lk(dve.tensor_tensor(qk, qk, rb, ALU.mult))
                    for i in range(2):
                        part = u[:, :, COLS * i:COLS * (i + 1)].rearrange("p t (h d) -> p t h d", d=HD)
                        wb = qkcur[:, i, :].unsqueeze(1).unsqueeze(1).broadcast_to((P, NT, HEADS, HD))
                        lk(dve.tensor_tensor(part, part, wb, ALU.mult))
                    half = ROT // 2
                    t1 = w1[:, :, 0:T].rearrange("p a (h d) -> p a h d", d=ROT)
                    t2 = sc[:, :, 0:T].rearrange("p a (h d) -> p a h d", d=ROT)
                    cb = cos2[0][:, :, :].unsqueeze(2).broadcast_to((P, NT, 2 * HEADS, ROT))
                    lk(dve.tensor_tensor(t1, qk[:, :, :, 0:ROT], cb, ALU.mult))
                    for i in range(2):
                        sb_ = sin2[0][:, :, half * i:half * (i + 1)].unsqueeze(2).broadcast_to((P, NT, 2 * HEADS, half))
                        lk(dve.tensor_tensor(t2[:, :, :, half * i:half * (i + 1)], qk[:, :, :, half * (1 - i):half * (2 - i)], sb_, ALU.mult))
                    dve.tensor_tensor(qk[:, :, :, 0:ROT], t1, t2, ALU.add).then_inc(qk_ready.sem, 1)

                def pool_windows():
                    e = PAD + T
                    dve.wait_ge(*pct_taken.at(l, 1))
                    dve.memset(pp[:, :, 0:PAD], 0.0).then_inc(pads_zero.sem, 1)
                    dve.memset(zp[:, :, 0:PAD], 0.0).then_inc(pads_zero.sem, 1)
                    dve.wait_ge(*pads_zero.at(l, 2))
                    lk(dve.tensor_tensor(w1[:, :, 1:e], pp[:, :, 1:e], pp[:, :, 0:e - 1], ALU.add))
                    lk(dve.tensor_tensor(w2[:, :, 3:e], w1[:, :, 3:e], w1[:, :, 1:e - 2], ALU.add))
                    lk(dve.tensor_tensor(w1[:, 1, 7:e], w2[:, 1, 7:e], w2[:, 1, 3:e - 4], ALU.add))
                    lk(dve.tensor_tensor(w2[:, 1, PAD:e], w1[:, 1, PAD:e], w1[:, 1, PAD - 8:e - 8], ALU.add))
                    for half, w in ((0, w1), (64, w2)):
                        r = slice(half, half + 64)
                        lk(dve.tensor_tensor(w[r, :, PAD:e], w[r, :, PAD:e], count[r, :, :], ALU.mult))
                        ins = dve.tensor_tensor(w1[r, :, PAD:e], w[r, :, PAD:e], pp[r, :, PAD:e], ALU.subtract)
                        if half == 0:
                            lk(ins)
                    ins.then_inc(pooled.sem, 1)

                def short_conv():
                    dve.wait_ge(*pct_taken.at(l, 3))
                    ft_free(X_CONV)
                    y = ft[:, X_CONV % 2, :].rearrange("p (a t) -> p a t", a=2)
                    for a in range(2):
                        for k in (2, 1, 0):
                            w = pcur[:, PC_CW + 2 * k + a:PC_CW + 2 * k + a + 1]
                            z = zp[:, a, PAD - 2 + k:PAD - 2 + k + T]
                            if k == 2:
                                lk(dve.tensor_scalar(y[:, a, :], z, w, None, ALU.mult))
                            else:
                                lk(dve.scalar_tensor_tensor(out=y[:, a, :], in0=z, scalar=w, in1=y[:, a, :], op0=ALU.mult, op1=ALU.add))
                    dve.tensor_tensor(y, y, bg[:, :, :], ALU.mult).then_inc(ft_ready.sem, 1)

                def soft_max(h):
                    dve.wait_ge(*s_done.at(l, h + 1))
                    lk(dve.scalar_tensor_tensor(out=sc[:, h % 2, :], in0=mp[:, h % 2, 0:3 * P], scalar=HD ** -0.5,
                                                in1=mask[:, :], op0=ALU.mult, op1=ALU.add))
                    dve.tensor_reduce(nmax[:, h % 2, 0:1], sc[:, h % 2, 0:P], AX.X, ALU.max, negate=True)
                    dve.tensor_reduce(nmax[:, h % 2, 1:2], sc[:, h % 2, P:3 * P], AX.X, ALU.max, negate=True).then_inc(s_max.sem, 1)

                def take_o(h):
                    dve.wait_ge(*e_done.at(l, 2 * h + 2))
                    lk(dve.reciprocal(rinv[:, h % 2, :], rsum[:, h % 2, :]))
                    dve.wait_ge(*o_done.at(l, h + 1))
                    for t in range(NT):
                        ins = dve.tensor_scalar(o[:, t, HD * h:HD * (h + 1)], mp[:, 3, HD * t:HD * (t + 1)],
                                                rinv[:, h % 2, t:t + 1], None, ALU.mult)
                        if t == 0:
                            lk(ins)
                    ins.then_inc(o_taken.sem, 1)

                def merge(b, n):
                    q = J_BR + 2 * b + n
                    dve.wait_ge(*w_used.at(l, JOB_END[q] + 1))
                    dve.wait_ge(*gates_ready.at(l, 2 * b + n + 1))
                    gate = gl[:, :, COLS * (2 * b + n):COLS * (2 * b + n + 1)]
                    m = merged[:, :, COLS * n:COLS * (n + 1)]
                    dve.tensor_tensor(m if b == 0 else gate, gp[:, q % 2, :, :], gate, ALU.mult).then_inc(pair_free[q % 2].sem, 2)
                    dve.wait_ge(*pair_free[q % 2].at(l, 2 * (q // 2) + 2))
                    if b == 1:
                        lk(dve.tensor_tensor(m, m, gate, ALU.add))
                    if b == 2:
                        dve.tensor_tensor(m, m, gate, ALU.add).then_inc(merged_ready.sem, 1)

                def residual(q, n, i, tmp):
                    dve.wait_ge(*w_used.at(l, JOB_END[q] + 1))
                    gb = grow[:, i, COLS * n:COLS * (n + 1)].unsqueeze(1).broadcast_to((P, NT, COLS))
                    dve.tensor_tensor(tmp, gp[:, q % 2, :, :], gb, ALU.mult).then_inc(pair_free[q % 2].sem, 2)
                    dve.wait_ge(*pair_free[q % 2].at(l, 2 * (q // 2) + 2))
                    xs = x[:, :, COLS * n:COLS * (n + 1)]
                    dve.tensor_tensor(xs, xs, tmp, ALU.add).then_inc(x_final.sem, 1)

                lk(dve.tensor_copy(pcur[:, :], pcol[:, bass.ds(l, 1), 0:PC_LAYER].rearrange("p a n -> p (a n)")))
                lk(dve.tensor_copy(qkcur[:, :, :].rearrange("p a n -> p (a n)"), qkw[:, bass.ds(l, 1), :, :].rearrange("p a b n -> p (a b n)")))
                lk(dve.tensor_copy(poolcur[:, :, :].rearrange("p a n -> p (a n)"), poolw[:, bass.ds(l, 1), :, :].rearrange("p a b n -> p (a b n)")))
                row_norm(0)
                for n in range(2 * ADA):
                    ada(n)
                take_mod(0)
                take_mod(1)
                norm_columns(0, 0)
                split(0)
                split(1)
                spread(X_NORM1, 4, (xt_hi, xt_lo), 0, normed(0, 0))
                for s in range(10):
                    split(s + 2)
                    if s % 2:
                        take_w_in(s // 2)
                    if s == 5:
                        qk_norm_rope()
                    if s == 7:
                        take_mod(2)
                dve.wait_ge(*pair_free[0].at(l, 6))
                cu = u[:, :, 3 * COLS + 256:4 * COLS]
                dve.tensor_tensor(cu, cu, u[:, :, 4 * COLS + 256:5 * COLS], ALU.mult).then_inc(cu_ready.sem, 1)
                for i in range(12):
                    split(10 + i + 2)
                    if i == 0:
                        take_mod(3)
                    if 0 <= i - 4 < HEADS:
                        take_o(i - 4)
                    if 0 <= i - 2 < HEADS:
                        soft_max(i - 2)
                    if i == 5:
                        pool_windows()
                take_mod(4)
                norm_columns(1, 3)

                def pool_scaled(f, bank):
                    bank_done(f)
                    for k in range(2):
                        ins = dve.tensor_scalar(ft[:, f % 2, T * k:T * (k + 1)], mp[:, bank, T * k:T * (k + 1)],
                                                pcur[:, PC_PS + k:PC_PS + k + 1], None, ALU.mult)
                        if k == 0:
                            lk(ins)
                    ins.then_inc(ft_ready.sem, 1)

                spread(X_POOL, 1, (bt_hi, bt_lo), 0, pool_scaled, 1)
                short_conv()
                low(X_CONV, bt_hi[:, 2:4, :], bt_lo[:, 2:4, :])
                spread(X_ATT, 2, (bt_hi, bt_lo), 4, plain, 2)
                for s in range(S_BR, S_OUT):
                    split(s + 2)
                    for q, _, _, _, _, _, _ in group_jobs(s):
                        merge((q - J_BR) // 2, (q - J_BR) % 2)
                spread(X_MERGE, 4, (xt_hi, xt_lo), 0, plain)
                for s in range(S_OUT, S_FF):
                    split(s + 2)
                    if s % 2 == (S_OUT + 1) % 2:
                        n = (s - S_OUT) // 2
                        residual(J_OUT + n, n, 0, gl[:, :, COLS * n:COLS * (n + 1)])
                row_norm(2)
                spread(X_NORM2, 4, (xt_hi, xt_lo), 0, normed(1, 3))
                for s in range(S_FF, S_DOWN):
                    split(s + 2)
                    j, r = divmod(s - S_FF, 4)
                    wide = min(COLS, FF - COLS * j)
                    if r == 2 and j >= 1:
                        spread(X_ACT + 2 * (j - 1), 2, (at_hi, at_lo), 4 * (j - 1), plain, 2 * ((j - 1) % 2))
                    if r == 3:
                        q = J_FF + 2 * j + 1
                        dve.wait_ge(*w_used.at(l, JOB_END[q] + 1))
                        dve.wait_ge(*silu_done.at(l, j + 1))
                        dve.tensor_tensor(ab[:, :, 0:wide], gp[:, q % 2, :, 0:wide], sg[:, :, 0:wide], ALU.mult).then_inc(ab_ready.sem, 1)
                        dve.wait_ge(*ab_ready.at(l, j + 1))
                        dve.sem_inc(pair_free[q % 2].sem, 2)
                        dve.sem_inc(pair_free[1 - q % 2].sem, 2)
                for s in range(S_DOWN, S_LAYER - 2):
                    split(s + 2)
                    if s == S_DOWN + 1:
                        spread(X_ACT + 2 * (FF_BLOCKS - 1), 1, (at_hi, at_lo), FF_CHUNKS - 2, plain, 2)
                    if s == S_DOWN + 3:
                        take_mod(5)
                for n in range(2):
                    residual(J_DOWN + n, n, 1, (sg, ab)[n][:, :, :])
                dve.wait_ge(*x_final.at(l, 4))
                dve.sem_inc(v_chain, CHAIN - chain[0])
            chain[0] = 0

            base2 = (LAYERS + 1) * CHAIN

            def reciprocal_root(n, wait, lk):
                dve.wait_ge(*wait)
                lk(dve.reciprocal(rr[:, 0:n], rs[:, 0:n]))
                lk(dve.tensor_tensor(rt[:, 0:n], rr[:, 0:n], rr[:, 0:n], ALU.mult))
                lk(dve.tensor_tensor(rt[:, 0:n], rt[:, 0:n], rv[:, 0:n], ALU.mult))
                lk(dve.tensor_scalar(rt[:, 0:n], rt[:, 0:n], -0.5, 1.5, ALU.mult, ALU.add))
                lk(dve.tensor_tensor(rr[:, 0:n], rr[:, 0:n], rt[:, 0:n], ALU.mult))

            def layer_norm(src, sums, squares, roots, rows, lk):
                dve.wait_ge(*sums)
                lk(dve.tensor_scalar(mean[:, :], lsum[:, :], 1.0 / D, None, ALU.mult))
                for t in range(NT):
                    dve.tensor_scalar(cen[:, t, :], src[:, t, :], mean[:, t:t + 1], None, ALU.subtract).then_inc(ln_cen.sem, 1)
                dve.wait_ge(*squares)
                dve.tensor_scalar(rv[:, 0:NT], ssq[:, :], 1.0 / D, LN_EPS, ALU.mult, ALU.add).then_inc(rv2_ready.sem, 1)
                reciprocal_root(NT, roots, lk)
                dve.wait_ge(*rows)
                for t in range(NT):
                    lk(dve.scalar_tensor_tensor(out=cen[:, t, :], in0=cen[:, t, :], scalar=rr[:, t:t + 1],
                                                in1=lnw[:, 0, :], op0=ALU.mult, op1=ALU.mult))
                    dve.tensor_tensor(x[:, t, :], cen[:, t, :], lnw[:, 1, :], ALU.add).then_inc(h_ready.sem, 1)

            def lk0(ins):
                link(ins, base2)

            layer_norm(x, (ln_sum.sem, 2), (ln_sq.sem, 2), (rs2_ready.sem, 1), (lnw_in.sem, 32), lk0)
            dve.wait_ge(rw_high, 1)
            lk0(dve.tensor_tensor(rw_lo[:, :, :], rw[:, :, :], rw_hi[:, :, :].bitcast(F32), ALU.subtract))
            dve.sem_inc(rw_ready, 1)
            dve.sem_inc(v_chain, CHAIN2 - chain[0])
            chain[0] = 0

            with dve.Fori(0, LAYERS) as l:
                def lk(ins):
                    link(ins, l * CHAIN2 + (base2 + CHAIN2))

                def split_at(n, k, units, cols):
                    dve.wait_ge(*hi_done.at2(l, k))
                    dve.tensor_tensor(slot(wlo, n % SPLIT, units, cols), slot(raw, n % RAW, units, cols),
                                      slot(whi, n % SPLIT, units, cols).bitcast(F32), ALU.subtract).then_inc(raw_read[n % RAW].sem, 1)

                def split(s):
                    units, cols = weights2(s, l)[1:] if s < S2_MOE else (4, COLS)
                    split_at(s, s + 1, units, cols)

                def plain(f, bank, n, k):
                    dve.wait_ge(*tr_done.at2(l, k + 1))
                    dve.wait_ge(*ft_lo.at2(l, k - 1))
                    dve.tensor_copy(ft[:, f % 2, 0:T * n], mp[:, bank, 0:T * n]).then_inc(ft_ready.sem, 1)

                def low(f, hi, lo, n, k):
                    dve.wait_ge(*ft_hi.at2(l, k + 1))
                    dve.tensor_tensor(lo, ft[:, f % 2, 0:T * n].rearrange("p (k t) -> p k t", k=n), hi.bitcast(F32),
                                      ALU.subtract).then_inc(ft_lo.sem, 1)

                def spread(f0, units, dst, bank0=0, k0=None):
                    hi, lo = dst
                    at = f0 if k0 is None else k0
                    for b in range(len(units) + 1):
                        if b < len(units):
                            plain(f0 + b, bank0 + b, units[b], at + b)
                        if b:
                            c, n = 2 * (b - 1), units[b - 1]
                            low(f0 + b - 1, hi[:, c:c + n, :], lo[:, c:c + n, :], n, at + (b - 1))

                def take(q, t, dst, src=None):
                    dve.wait_ge(*w_used.at2(l, job2_end(q) + 1))
                    src = gp[:, q % 2, t, 0:dst.shape[-1]] if src is None else src
                    dve.tensor_copy(dst, src).then_inc(pair_free[q % 2].sem, 1)

                def rotate(v, r, heads, rot):
                    h = rot // 2
                    n = NT * heads * rot
                    t1 = rt1[:, 0:n].rearrange("p (t h d) -> p t h d", t=NT, d=rot)
                    t2 = rt2[:, 0:n].rearrange("p (t h d) -> p t h d", t=NT, d=rot)
                    lk(dve.tensor_tensor(t1, v, cos2[r][:, :, :].unsqueeze(2).broadcast_to((P, NT, heads, rot)), ALU.mult))
                    for i in range(2):
                        sn = sin2[r][:, :, h * i:h * (i + 1)].unsqueeze(2).broadcast_to((P, NT, heads, h))
                        lk(dve.tensor_tensor(t2[:, :, :, h * i:h * (i + 1)], v[:, :, :, h * (1 - i):h * (2 - i)], sn, ALU.mult))
                    lk(dve.tensor_tensor(v, t1, t2, ALU.add))

                split(0)
                split(1)
                dve.wait_ge(params2_in, PARAMS2)
                lk(dve.tensor_copy(cgc[:, :], cg[:, bass.ds(l, 1), :].rearrange("p a n -> p (a n)")))
                lk(dve.tensor_scalar(subc[:, :], subg[:, bass.ds(l, 1), :].rearrange("p a n -> p (a n)"),
                                     lamc[:, bass.ds(l, 1), 1:2].rearrange("p a n -> p (a n)"), None, ALU.mult))
                lr = lamr[:, bass.ds(l, 1), :, :].rearrange("p a b n -> p (a b) n")
                lk(dve.tensor_copy(lamq[:, :, :], lr))
                lk(dve.tensor_tensor(lamt[:, :, :], lamq[:, 0:2, :], lamq[:, 2:4, :], ALU.mult))
                dve.tensor_reduce(lame[:, :], lamt[:, :, :], AX.X, ALU.add).then_inc(lam_sum.sem, 1)
                lk(dve.tensor_copy(lami[:, :], lamc[:, bass.ds(l, 1), 0:1].rearrange("p a n -> p (a n)")))
                lk(dve.tensor_copy(fbc[:, :], fbias[:, bass.ds(l, 1), :].rearrange("p a n -> p (a n)")))
                spread(X2_IN, (2, 2, 2, 2), (xt_hi, xt_lo))
                for s in range(S2_UQ):
                    split(s + 2)
                    if s % 2:
                        j = s // 2
                        take(j, 1, pr[:, 1, COLS * j:min(COLS * (j + 1), IN2)])
                    if s == 3:
                        dve.wait_ge(*mla_sq.at2(l, 4))
                        lk(dve.tensor_scalar(rv[:, 0:2], lsum4[:, 0:2], 1.0 / CQ, EPS, ALU.mult, ALU.add))
                        dve.tensor_scalar(rv[:, 2:4], lsum4[:, 2:4], 1.0 / CKV, EPS, ALU.mult, ALU.add).then_inc(rv2_ready.sem, 1)
                        reciprocal_root(4, rs2_ready.at2(l, 1), lk)
                        for t in range(NT):
                            for i, (a, b) in enumerate(((0, CQ), (CQ, CQ + CKV))):
                                lk(dve.scalar_tensor_tensor(out=pr[:, t, a:b], in0=pr[:, t, a:b], scalar=rr[:, 2 * i + t:2 * i + t + 1],
                                                            in1=cgc[:, a:b], op0=ALU.mult, op1=ALU.mult))
                        dve.sem_inc(mla_ready.sem, 1)
                dve.wait_ge(*pair_free[0].at2(l, 6))
                dve.wait_ge(*pair_free[1].at2(l, 4))
                lk(dve.tensor_tensor(fz[:, :, :], pr[:, :, C_FF:C_FF + FH], fbc[:, :].unsqueeze(1).broadcast_to((P, NT, FH)), ALU.add))
                lk(dve.tensor_scalar(fe[:, :, :], fz[:, :, :], -1.0, None, ALU.mult))
                dve.tensor_tensor(fe[:, :, :], fz[:, :, :], fe[:, :, :], ALU.min).then_inc(fz_ready.sem, 1)
                spread(X2_MLA, (2, 2, 1), (mt_hi, mt_lo))
                dve.wait_ge(*lam_exp.at2(l, 1))
                lk(dve.tensor_tensor(nlam[:, :], lame[:, 1:2], lame[:, 0:1], ALU.subtract))
                lk(dve.tensor_tensor(nlam[:, :], nlam[:, :], lami[:, :], ALU.subtract))
                dve.wait_ge(*fl_ready.at2(l, 1))
                lk(dve.tensor_scalar(fz[:, :, :], fz[:, :, :], 0.0, None, ALU.min))
                dve.tensor_tensor(fz[:, :, :], fz[:, :, :], fl[:, :, :], ALU.subtract).then_inc(logf_ready.sem, 1)
                for s in range(S2_UQ, S2_OUT):
                    split(s + 2)
                    q = J2_UQ + s - S2_UQ
                    h = 4 * ((s - S2_UQ) % 2)
                    if s < S2_UKV:
                        take(q, 1, qm[:, 1, h:h + 4, :].rearrange("p h d -> p (h d)"))
                    else:
                        for t in range(NT):
                            kv = gp[:, q % 2, t, :].rearrange("p (h d) -> p h d", h=4)
                            dve.wait_ge(*w_used.at2(l, job2_end(q) + 1))
                            lk(dve.tensor_copy(km[:, t, h:h + 4, 0:MN], kv[:, :, 0:MN]))
                            dve.tensor_copy(vm[:, t, h:h + 4, :], kv[:, :, MN:MN + HD]).then_inc(pair_free[q % 2].sem, 1)
                dve.wait_ge(*pair_free[0].at2(l, 8))
                dve.wait_ge(*pair_free[1].at2(l, 6))
                rotate(qm[:, :, :, MN:MQ], 1, MH, KR)
                kr = pr[:, :, C_KR:C_KR + KR].unsqueeze(2)
                rotate(kr, 1, 1, KR)
                lk(dve.tensor_copy(km[:, :, :, MN:MQ], kr.broadcast_to((P, NT, MH, KR))))
                dve.sem_inc(km_ready.sem, 1)
                for c in (C_DQ, C_DK):
                    rotate(pr[:, :, c:c + 2 * DH * DW].rearrange("p t (h d) -> p t h d", d=DW)[:, :, :, 0:DROT], 2, 2 * DH, DROT)
                dve.sem_inc(diff_ready.sem, 1)
                up = HD ** 0.5
                for dst, c in ((fq, C_FQ), (fk, C_FK)):
                    lk(dve.tensor_copy(dst[:, :, :, 0:HD], pr[:, :, c:c + FH * HD].rearrange("p t (h d) -> p t h d", d=HD)))
                lk(dve.memset(fq[:, :, :, HD + 1:HD + 2], 1.0))
                lk(dve.memset(fk[:, :, :, HD:HD + 1], 1.0))
                dve.wait_ge(*cum_done.at2(l, 1))
                cum = mp[:, 3, 0:NT * FH].rearrange("p (t h) -> p t h", t=NT)
                lk(dve.tensor_scalar(fq[:, :, :, HD:HD + 1].rearrange("p t h a -> p t (h a)"), cum, up, None, ALU.mult))
                dve.tensor_scalar(fk[:, :, :, HD + 1:HD + 2].rearrange("p t h a -> p t (h a)"), cum, -up, None, ALU.mult).then_inc(fox_ready.sem, 1)
                for i in range(AJ + 4):
                    j = i - 1
                    if 0 <= j < AJ:
                        scale, m = job_operands(j)[3:]
                        dve.wait_ge(*s2_done.at2(l, j + 1))
                        if j >= 3:
                            dve.wait_ge(*p2_done.at2(l, j - 2))
                        lk(dve.scalar_tensor_tensor(out=sc2[:, j % 3, :], in0=mp[:, 1, 0:3 * P], scalar=scale,
                                                    in1=m[:, :], op0=ALU.mult, op1=ALU.add))
                        dve.tensor_reduce(nmax2[:, j % 3, 0:1], sc2[:, j % 3, 0:P], AX.X, ALU.max, negate=True)
                        dve.tensor_reduce(nmax2[:, j % 3, 1:2], sc2[:, j % 3, P:3 * P], AX.X, ALU.max, negate=True).then_inc(s2_max.sem, 1)
                    j = i - 4
                    if 0 <= j < AJ:
                        dve.wait_ge(*e2_done.at2(l, 2 * j + 2))
                        lk(dve.reciprocal(rinv2[:, j % 3, :], rsum2[:, j % 3, :]))
                        dve.wait_ge(*o2_done.at2(l, j + 1))
                        for t in range(NT):
                            if j < MH:
                                dst = oa[:, t, HD * j:HD * (j + 1)]
                            elif j < MH + 2 * DH:
                                m, h = (j - MH) % 2, (j - MH) // 2
                                dst = od[:, t, HD * h:HD * (h + 1)] if m else oa[:, t, HD * (MH + h):HD * (MH + h + 1)]
                            else:
                                dst = oa[:, t, HD * (j - DH):HD * (j - DH + 1)]
                            ins = dve.tensor_scalar(dst, mp[:, 3, HD * t:HD * (t + 1)], rinv2[:, j % 3, t:t + 1], None, ALU.mult)
                            if t == 0:
                                lk(ins)
                        ins.then_inc(o2_taken.sem, 1)
                dve.wait_ge(*o2_taken.at2(l, AJ))
                d1 = oa[:, :, HD * MH:HD * (MH + DH)]
                lk(dve.scalar_tensor_tensor(out=d1, in0=od[:, :, :], scalar=nlam[:, :], in1=d1, op0=ALU.mult, op1=ALU.add))
                lk(dve.tensor_tensor(od[:, :, :], d1, d1, ALU.mult))
                n = NT * DH
                lk(dve.tensor_reduce(rt[:, 0:n].rearrange("p (t h) -> p t h", t=NT), od[:, :, :].rearrange("p t (h d) -> p t h d", d=HD), AX.X, ALU.add))
                dve.tensor_scalar(rv[:, 0:n], rt[:, 0:n], 1.0 / HD, EPS, ALU.mult, ALU.add).then_inc(rv2_ready.sem, 1)
                reciprocal_root(n, rs2_ready.at2(l, 2), lk)
                d1h = d1.rearrange("p t (h d) -> p t h d", d=HD)
                lk(dve.tensor_tensor(d1h, d1h, rr[:, 0:n].rearrange("p (t h) -> p t h", t=NT).unsqueeze(3).broadcast_to((P, NT, DH, HD)), ALU.mult))
                dve.tensor_tensor(d1h, d1h, subc[:, :].unsqueeze(1).unsqueeze(1).broadcast_to((P, NT, DH, HD)), ALU.mult).then_inc(oa_ready.sem, 1)
                spread(X2_O, (2, 2, 2, 2), (xt_hi, xt_lo))
                for s in range(S2_OUT, S2_MOE):
                    split(s + 2)
                    if s % 2 == (S2_OUT + 1) % 2:
                        n = (s - S2_OUT) // 2
                        q = J2_OUT + n
                        dve.wait_ge(*w_used.at2(l, job2_end(q) + 1))
                        xs = x[:, :, COLS * n:COLS * (n + 1)]
                        dve.scalar_tensor_tensor(out=xs, in0=xs, scalar=ALPHA, in1=gp[:, q % 2, :, :], op0=ALU.mult, op1=ALU.add).then_inc(x2_sum.sem, 1)
                        dve.wait_ge(*x2_sum.at2(l, n + 1))
                        dve.sem_inc(pair_free[q % 2].sem, 2)
                layer_norm(x, ln_sum.at2(l, 2), ln_sq.at2(l, 2), rs2_ready.at2(l, 3), lnw_in.at2(l, 32), lk)
                spread(X2_H, (2, 2, 2, 2), (xt_hi, xt_lo))
                dve.wait_ge(*h_ready.at2(l, 2))

                def beats(dst, v):
                    d = cmp1[:, 0:v.shape[1], :].rearrange("p g (i j) -> p g i j", i=4)
                    e_ = cmp2[:, 0:v.shape[1], :].rearrange("p g (i j) -> p g i j", i=4)
                    shape = (P, v.shape[1], 4, 4)
                    vi, vj = v.unsqueeze(3).broadcast_to(shape), v.unsqueeze(2).broadcast_to(shape)
                    lk(dve.tensor_tensor(d, vj, vi, ALU.is_ge))
                    lk(dve.tensor_tensor(e_, vj, vi, ALU.is_gt))
                    for a, c in ((cmp1, 0), (cmp2, 1)):
                        w = a[:, 0:v.shape[1], :]
                        lk(dve.tensor_tensor(w, w, order[:, c, :].unsqueeze(1).broadcast_to((P, v.shape[1], 16)), ALU.mult))
                    lk(dve.tensor_tensor(d, d, e_, ALU.add))
                    lk(dve.tensor_reduce(dst, d, AX.X, ALU.add))

                dve.wait_ge(*rsc_ready.at2(l, 1))
                lk(dve.tensor_tensor(rb[:, :, :], rsc[:, :, :], rbias[:, :].unsqueeze(1).broadcast_to((P, NT, NE)), ALU.add))
                four = rb[:, :, :].rearrange("p t (g i) -> p (t g) i", i=4)
                beats(rank[:, :, :], four)
                lk(dve.tensor_scalar(rank[:, :, :], rank[:, :, :], 2.0, None, ALU.is_lt))
                lk(dve.tensor_tensor(cmp1[:, :, 0:4], four, rank[:, :, :], ALU.mult))
                lk(dve.tensor_reduce(gs[:, :], cmp1[:, :, 0:4], AX.X, ALU.add))
                beats(gr[:, :].rearrange("p (t g) -> p t g", t=NT), gs[:, :].rearrange("p (t g) -> p t g", t=NT))
                lk(dve.tensor_scalar(gr[:, :], gr[:, :], 1.0, None, ALU.is_lt))
                lk(dve.tensor_tensor(rank[:, :, :], rank[:, :, :], gr[:, :].unsqueeze(2).broadcast_to((P, 8, 4)), ALU.mult))
                dve.sem_inc(chosen.sem, 1)
                lk(dve.tensor_tensor(dg[:, :, :], rsc[:, :, :], rank[:, :, :].rearrange("p (t g) i -> p t (g i)", t=NT), ALU.mult))
                lk(dve.tensor_reduce(den[:, :], dg[:, :, :], AX.X, ALU.add))
                lk(dve.reciprocal(den[:, :], den[:, :]))
                for t in range(NT):
                    lk(dve.tensor_scalar(dg[:, t, :], dg[:, t, :], den[:, t:t + 1], None, ALU.mult))

                dve.wait_ge(*chosen_sum.at2(l, 1))
                lk(dve.memset(key[:, :, NE:NE + 1], 0.0))
                lk(dve.tensor_tensor(key[:, :, 0:NE], mp[:, 1, 0:NT * NE].rearrange("p (t n) -> p t n", t=NT),
                                     rank[:, :, :].rearrange("p (t g) i -> p t (g i)", t=NT), ALU.mult))
                lk(dve.tensor_reduce(many[:, :], mp[:, 1, NT * NE:(NT + 1) * NE], AX.X, ALU.max))
                lk(dve.tensor_scalar(many[:, :], many[:, :], float(CAP), None, ALU.is_gt))
                dve.tensor_copy(dense_i[:, :], many[:, :]).then_inc(flag_ready.sem, 1)

                def gated(e, k):
                    dve.wait_ge(*w_used.at2(l, k))
                    dve.wait_ge(*silu2_done.at2(l, e + 1))
                    for t in range(NT):
                        ins = dve.scalar_tensor_tensor(out=ab2[:, t, :], in0=gp[:, 1 - GATE_PAIR, t, :], scalar=dg[:, t, bass.ds(e, 1)],
                                                       in1=sg2[:, t, :], op0=ALU.mult, op1=ALU.mult)
                        if t == 0:
                            ins.then_inc(v_moe, 1)
                            dve.wait_ge(v_moe, l * NE + (e + 1))
                    ins.then_inc(ab2_ready.sem, 1)
                    dve.wait_ge(*ab2_ready.at2(l, e + 1))
                    for p in range(2):
                        dve.sem_inc(pair_free[p].sem, 2)

                def add_y(n, yk, k):
                    p = GATE_PAIR if n == 0 else 1 - GATE_PAIR
                    dve.wait_ge(*w_used.at2(l, k))
                    ys = cen[:, :, COLS * n:COLS * (n + 1)]
                    dve.tensor_tensor(ys, ys, gp[:, p, :, :], ALU.add).then_inc(y_taken.sem, 1)
                    dve.wait_ge(*y_taken.at2(l, yk))
                    dve.sem_inc(pair_free[p].sem, 2)

                def select(k, e):
                    if k is not None:
                        dve.wait_ge(*gathered.at2(l, k))
                    for t in range(NT):
                        ins = dve.tensor_scalar(pick[:, t, :], slots[:, 0:CAP], key[:, t, bass.ds(e, 1)], None, ALU.is_equal)
                        if t == 1:
                            ins.then_inc(pick_ready.sem, 1)

                def select_gates(k, e):
                    if k is not None:
                        dve.wait_ge(*ax_turned.at2(l, k))
                    for t in range(NT):
                        ins = dve.tensor_scalar(place[:, t, :], slots[:, :], key[:, t, bass.ds(e, 1)], dg[:, t, bass.ds(e, 1)],
                                                ALU.is_equal, ALU.mult)
                        if t == 1:
                            ins.then_inc(place_ready.sem, 1)

                def low_tokens(k):
                    dve.wait_ge(*xg_high.at2(l, k))
                    dve.tensor_tensor(xg[:, :, CAP:2 * CAP], bank_tr.rearrange("p (c s) -> p c s", c=KD), xg[:, :, 0:CAP].bitcast(F32),
                                      ALU.subtract).then_inc(xg_low.sem, 1)

                def gate_whole(e):
                    dve.wait_ge(*gate_out.at2(l, e + 1))
                    dve.tensor_tensor(gx, bank_gate[0:CAP, :], gxl, ALU.add).then_inc(gate_sum.sem, 1)

                def gate_up(e):
                    dve.wait_ge(*up_out.at2(l, e + 1))
                    dve.tensor_tensor(ux, bank_up[0:CAP, :], uxl, ALU.add).then_inc(up_sum.sem, 1)
                    dve.wait_ge(*up_sum.at2(l, e + 1))
                    dve.wait_ge(*silux.at2(l, e + 1))
                    dve.tensor_tensor(ax, gx.rearrange("p (a n) -> p a n", a=2), ux.rearrange("p (a n) -> p a n", a=2), ALU.mult).then_inc(ax_ready.sem, 1)
                    dve.wait_ge(*ax_ready.at2(l, e + 1))

                def low_turned(k):
                    dve.wait_ge(*ag_high.at2(l, k))
                    dve.tensor_tensor(ag[:, :, CAP:2 * CAP], bank_tr[:, 0:T].rearrange("p (c s) -> p c s", c=4), ag[:, :, 0:CAP].bitcast(F32),
                                      ALU.subtract).then_inc(ag_low.sem, 1)

                def gathered_experts():
                    dve.memset(back, 0.0).then_inc(y_zero.sem, 1)
                    dve.memset(yx, 0.0).then_inc(y_zero.sem, 1)
                    select(None, 0)
                    low_tokens(1)
                    for i in range(4):
                        split(S2_MOE + i + 2)
                        if i == 0:
                            select(1, 1)
                            select_gates(None, 0)
                        if i == 1:
                            gate_whole(0)
                        if i == 3:
                            gate_up(0)
                            low_tokens(2)
                    with dve.Fori(1, NE) as e:
                        for i in range(6):
                            n = S2_MOE + 6 + i
                            if i not in POOL_SPLITS:
                                split_at(n, (e - 1) * 6 + (n + 1), 4, COLS)
                            if i == 0:
                                select(e + 1, e + 1)
                                low_turned(e)
                                select_gates(e, e)
                            if i == 1:
                                gate_whole(e)
                            if i == 3:
                                gate_up(e)
                                low_tokens(e + 2)
                    low_turned(NE)
                    dve.wait_ge(*y_done.at2(l, 1))
                    for t in range(NT):
                        dve.scalar_tensor_tensor(out=cen[:, t, :], in0=x[:, t, :], scalar=ALPHA,
                                                 in1=mp[:, 2 * t:2 * t + 2, :].rearrange("p a n -> p (a n)"), op0=ALU.mult, op1=ALU.add).then_inc(y_taken.sem, NE)
                    dve.wait_ge(*y_taken.at2(l, 2 * NE))
                    for c, n in ((ft_ready, 2 * NE), (ft_lo, 2 * NE), (ab2_ready, NE), (pair_free[0], 4 * NE), (pair_free[1], 4 * NE)):
                        dve.sem_inc(c.sem, n)
                    dve.sem_inc(v_moe, NE)
                    dve.sem_inc(flag_seen, 1)

                dve.wait_ge(*flag_ready.at2(l, 1))
                dve.sem_inc(loads, 1)
                dense = dve.value_load(dense_i[0:1, 0:1], min_val=0, max_val=1)
                with dve.If(dense == 0):
                    gathered_experts()
                with dve.Else():
                    dve.tensor_scalar(cen[:, :, :], x[:, :, :], ALPHA, None, ALU.mult).then_inc(flag_seen, 1)
                    dve.wait_ge(flag_seen, l + 1)
                    for i in range(4):
                        split(S2_MOE + i + 2)
                    gated(0, S2_MOE + 4)
                    with dve.Fori(1, NE) as e:
                        k = (e - 1) * 6
                        for i in range(6):
                            n = S2_MOE + 6 + i
                            split_at(n, k + (n + 1), 4, COLS)
                            if i == 1:
                                spread(X2_MOE, (2, 2), (mt_hi, mt_lo), 0, (e - 1) * 2 + X2_MOE)
                            if i == 3:
                                gated(e, k + (S2_MOE + 8))
                            if i == 4:
                                add_y(0, (e - 1) * 2 + 1, k + (S2_MOE + 9))
                            if i == 5:
                                add_y(1, (e - 1) * 2 + 2, k + (S2_MOE + 10))
                    spread(X2_LAYER - 2, (2, 2), (mt_hi, mt_lo))
                    add_y(0, 2 * NE - 1, S2_LAYER - 1)
                    add_y(1, 2 * NE, S2_LAYER)
                    for c, n in ((pick_ready, NE + 1), (xg_low, NE + 1), (gate_sum, NE), (up_sum, NE), (ax_ready, NE),
                                 (place_ready, NE), (ag_low, NE), (y_zero, 2)):
                        dve.sem_inc(c.sem, n)
                layer_norm(cen, ln_sum.at2(l, 4), ln_sq.at2(l, 4), rs2_ready.at2(l, 4), lnw_in.at2(l, 64), lk)
                dve.wait_ge(*h_ready.at2(l, 4))
                dve.sem_inc(v_chain, CHAIN2 - chain[0])

        @block.tensor
        def _(pe):
            pe.sem_inc(w_used.sem, w_used.prime)
            pe.sem_inc(acc_read.sem, acc_read.prime)
            for p in range(2):
                pe.sem_inc(pair_free[p].sem, pair_free[p].prime)
            pe.wait_ge(consts_in, 16 * 6)
            pe.wait_ge(params_in, PARAMS)
            pe.wait_ge(zeroed, 2)
            for l in range(LAYERS):
                pe.transpose(mp[:, l, 0:PC_ROWS], stage[:, l, :], ident[0:PC_ROWS, 0:PC_ROWS]).then_inc(params_t, 1)

            with pe.Fori(0, LAYERS) as l:
                def product(s):
                    g = G_OF["split", s]
                    pe.wait_ge(*raw_read[g % RAW].at(l, g // RAW + 1))
                    _, units, cols = weights(("split", s), l)
                    w_hi, w_lo = slot(whi, s % SPLIT, units, cols), slot(wlo, s % SPLIT, units, cols)
                    for q, c0, wide, parts, first, last, name in group_jobs(s):
                        a_hi, a_lo = stationary[name]
                        if first:
                            pe.wait_ge(*pair_free[q % 2].at(l, 2 * (q // 2)))
                        for t in range(NT):
                            ts = slice(P * t, P * (t + 1))
                            for n, (unit, chunk) in enumerate(parts):
                                for m, (a, w) in enumerate(((a_hi, w_hi), (a_hi, w_lo), (a_lo, w_hi))):
                                    mm = pe.matmul(gp[:, q % 2, t, 0:wide], a[:, chunk, ts], w[:, unit, c0:c0 + wide],
                                                   start=first and n == 0 and m == 0, stop=last and n == len(parts) - 1 and m == 2)
                    mm.then_inc(w_used.sem, 1)

                def sum_mod(vec):
                    pe.wait_ge(*acc_done.at(l, vec + 1))
                    a = acc[:, vec % 2, :]
                    if vec in (2, 5):
                        for n in range(2):
                            mm = pe.matmul(mp[:, n, :], ones[:, :], a[:, COLS * n:COLS * (n + 1)], start=True, stop=True)
                    else:
                        bank = {0: 0, 1: 1, 3: 2, 4: 0}[vec]
                        for c in range(KD):
                            mm = pe.matmul(mp[:, bank, c:c + 1], a[:, P * c:P * (c + 1)], ones[:, 0:1], start=True, stop=True)
                    mm.then_inc(acc_read.sem, 1)

                def turn(bank, src, c0, n=2):
                    for k in range(n):
                        for t in range(NT):
                            mm = pe.transpose(mp[:, bank, T * k + P * t:T * k + P * (t + 1)], src[:, t, c0 + P * k:c0 + P * (k + 1)], ident[:, :])
                    return mm

                pe.wait_ge(*mod_taken.at(l, 0))
                sum_mod(0)
                sum_mod(1)
                pe.wait_ge(*mod_taken.at(l, 2))
                pe.wait_ge(*xn_ready.at(l, 2))
                for b in range(4):
                    turn(b, xn1, 2 * P * b).then_inc(tr_done.sem, 1)
                pe.wait_ge(*ft_lo.at(l, X_NORM1 + 4))
                for s in range(10):
                    product(s)
                    if s == 5:
                        sum_mod(2)
                sum_mod(3)

                def scores(h):
                    if h >= 2:
                        pe.wait_ge(*s_max.at(l, h - 1))
                    r, c = slice(HD * (h % 2), HD * (h % 2) + HD), h // 2
                    pe.matmul(mp[:, h % 2, 0:P], qt[r, c, 0:P], kt[r, c, 0:P], start=True, stop=True)
                    pe.matmul(mp[:, h % 2, P:3 * P], qt[r, c, P:T], kt[r, c, :], start=True, stop=True).then_inc(s_done.sem, 1)

                def turn_p(h):
                    pe.wait_ge(*e_done.at(l, 2 * h + 2))
                    if h >= 1:
                        pe.wait_ge(*pt_taken.at(l, h))
                    for a in range(3):
                        mm = pe.transpose(mp[:, 2, P * a:P * (a + 1)], sc[:, h % 2, P * a:P * (a + 1)], ident[:, :])
                    mm.then_inc(pt_done.sem, 1)

                def weigh(h):
                    pe.wait_ge(*pt_taken.at(l, h + 1))
                    if h >= 1:
                        pe.wait_ge(*o_taken.at(l, h))
                    v = u[:, :, 2 * COLS + HD * h:2 * COLS + HD * (h + 1)]
                    pe.matmul(mp[:, 3, 0:HD], pt[:, 0:P], v[:, 0, :], start=True, stop=True)
                    pe.matmul(mp[:, 3, HD:2 * HD], pt[:, P:2 * P], v[:, 0, :], start=True, stop=False)
                    pe.matmul(mp[:, 3, HD:2 * HD], pt[:, 2 * P:3 * P], v[:, 1, :], start=False, stop=True).then_inc(o_done.sem, 1)

                for i in range(12):
                    product(10 + i)
                    if i == 0:
                        pe.wait_ge(*qk_ready.at(l, 1))
                        pe.wait_ge(*mod_taken.at(l, 4))
                        for b in range(4):
                            mm = turn(b, u, 2 * P * b)
                        mm.then_inc(qkt_done.sem, 1)
                    if i == 1:
                        pe.wait_ge(*qkt_taken.at(l, 4))
                        pe.wait_ge(*cu_ready.at(l, 1))
                        for b in range(3):
                            mm = turn(b, u, 3 * COLS + 2 * P * b)
                        mm.then_inc(pct_done.sem, 1)
                    if i == 2:
                        pe.wait_ge(*pct_taken.at(l, 3))
                    if 0 <= i - 4 < HEADS:
                        weigh(i - 4)
                    if 0 <= i - 3 < HEADS:
                        turn_p(i - 3)
                    if 0 <= i - 2 < HEADS:
                        scores(i - 2)
                pe.wait_ge(*s_max.at(l, HEADS))
                sum_mod(4)
                pe.wait_ge(*pooled.at(l, 1))
                for c in range(2):
                    mm = pe.matmul(mp[:, 1, T * c:T * (c + 1)], poolcur[:, c, :], w1[:, c, PAD:PAD + T], start=True, stop=True)
                mm.then_inc(tr_done.sem, 1)
                pe.wait_ge(*o_taken.at(l, HEADS))
                for b in range(2):
                    turn(2 + b, o, 2 * P * b).then_inc(tr_done.sem, 1)
                for s in range(S_BR, S_OUT):
                    if s == S_BR:
                        pe.wait_ge(*ft_lo.at(l, X_POOL + 1))
                    if s == S_BR + 1:
                        pe.wait_ge(*ft_lo.at(l, X_CONV + 1))
                    if s == S_BR + 2:
                        pe.wait_ge(*ft_lo.at(l, X_ATT + 2))
                    product(s)
                pe.wait_ge(*mod_taken.at(l, 5))
                for b in range(4):
                    if b % 2 == 0:
                        pe.wait_ge(*merged_ready.at(l, b // 2 + 1))
                    turn(b, merged, 2 * P * b).then_inc(tr_done.sem, 1)
                pe.wait_ge(*ft_lo.at(l, X_MERGE + 4))
                for s in range(S_OUT, S_FF):
                    product(s)
                pe.wait_ge(*xn_ready.at(l, 4))
                for b in range(4):
                    turn(b, xn2, 2 * P * b).then_inc(tr_done.sem, 1)
                pe.wait_ge(*ft_lo.at(l, X_NORM2 + 4))

                def turn_ab(j):
                    pe.wait_ge(*ab_ready.at(l, j + 1))
                    if j >= 2:
                        pe.wait_ge(*ft_ready.at(l, X_ACT + 2 * (j - 2) + 2))
                    for b in range(2 if j < FF_BLOCKS - 1 else 1):
                        turn(2 * (j % 2) + b if j < FF_BLOCKS - 1 else 2, ab, 2 * P * b).then_inc(tr_done.sem, 1)

                for s in range(S_FF, S_DOWN):
                    product(s)
                    j, r = divmod(s - S_FF, 4)
                    if r == 1 and j >= 1:
                        turn_ab(j - 1)
                for s in range(S_DOWN, S_LAYER):
                    if s == S_DOWN:
                        pe.wait_ge(*ft_lo.at(l, X_ACT + 2 * (FF_BLOCKS - 1)))
                    if s == S_DOWN + 2:
                        turn_ab(FF_BLOCKS - 1)
                    if s == S_DOWN + 3:
                        pe.wait_ge(*ft_ready.at(l, X_ACT + 2 * (FF_BLOCKS - 1)))
                        sum_mod(5)
                    if s == S_LAYER - 2:
                        pe.wait_ge(*ft_lo.at(l, X_LAYER))
                    product(s)

            with pe.Fori(0, LAYERS) as l:
                def multiply(n, k, q, units, cols, chunk0, src, first, last, pair_k):
                    pe.wait_ge(*raw_read[n % RAW].at2(l, k))
                    w_hi, w_lo = slot(whi, n % SPLIT, units, cols), slot(wlo, n % SPLIT, units, cols)
                    a_hi, a_lo = src
                    if first:
                        pe.wait_ge(*pair_free[q % 2].at2(l, pair_k))
                    for t in range(NT):
                        ts = slice(P * t, P * (t + 1))
                        for unit in range(units):
                            for m, (a, w) in enumerate(((a_hi, w_hi), (a_hi, w_lo), (a_lo, w_hi))):
                                mm = pe.matmul(gp[:, q % 2, t, 0:cols], a[:, chunk0 + unit, ts], w[:, unit, :],
                                               start=first and unit == 0 and m == 0, stop=last and unit == units - 1 and m == 2)
                    mm.then_inc(w_used.sem, 1)

                def product(s):
                    _, units, cols = weights2(s, l)
                    if s < S2_UQ:
                        q, h, c, src = s // 2, s % 2, 4 * (s % 2), (xt_hi, xt_lo)
                        first, last = h == 0, h == 1
                    elif s < S2_OUT:
                        q, c, src, first, last = J2_UQ + s - S2_UQ, 0 if s < S2_UKV else 3, (mt_hi, mt_lo), True, True
                    else:
                        h = (s - S2_OUT) % 2
                        q, c, src, first, last = J2_OUT + (s - S2_OUT) // 2, 4 * h, (xt_hi, xt_lo), h == 0, h == 1
                    multiply(s, s // RAW + 1, q, units, cols, c, src, first, last, 2 * (q // 2))

                def turn(bank, src, c0, n=2):
                    for k in range(n):
                        for t in range(NT):
                            mm = pe.transpose(mp[:, bank, T * k + P * t:T * k + P * (t + 1)], src[:, t, c0 + P * k:c0 + P * (k + 1)], ident[:, :])
                    return mm

                pe.wait_ge(*h_ready.at2(l, 0))
                for b in range(4):
                    turn(b, x, 2 * P * b).then_inc(tr_done.sem, 1)
                pe.wait_ge(*ft_lo.at2(l, X2_IN + 4))
                for s in range(S2_UQ):
                    product(s)
                pe.wait_ge(*mla_ready.at2(l, 1))
                for b in range(3):
                    turn(b, pr, 2 * P * b, 2 if b < 2 else 1).then_inc(tr_done.sem, 1)
                pe.wait_ge(*logf_ready.at2(l, 1))
                pe.matmul(mp[:, 3, 0:FH], tri[:, :], fz[:, 0, :], start=True, stop=True)
                pe.matmul(mp[:, 3, FH:2 * FH], ones[:, :], fz[:, 0, :], start=True, stop=False)
                pe.matmul(mp[:, 3, FH:2 * FH], tri[:, :], fz[:, 1, :], start=False, stop=True).then_inc(cum_done.sem, 1)
                pe.wait_ge(*ft_lo.at2(l, X2_MLA + 3))
                for s in range(S2_UQ, S2_OUT):
                    product(s)

                def turn_qk(j):
                    q, k = job_operands(j)[:2]
                    w = job_width(j)
                    if j == 0:
                        pe.wait_ge(*km_ready.at2(l, 1))
                    if j == MH:
                        pe.wait_ge(*diff_ready.at2(l, 1))
                    if j == MH + 2 * DH:
                        pe.wait_ge(*fox_ready.at2(l, 1))
                    if j:
                        pe.wait_ge(*t2_taken.at2(l, j))
                    for i, v in enumerate((q, k)):
                        for t in range(NT):
                            mm = pe.transpose(mp[0:w, 0, T * i + P * t:T * i + P * (t + 1)], v[:, t, :], ident[:, :])
                    mm.then_inc(t2_done.sem, 1)

                def scores(j):
                    w = job_width(j)
                    pe.wait_ge(*t2_taken.at2(l, j + 1))
                    if j:
                        pe.wait_ge(*s2_max.at2(l, j))
                    qk = qkt[0:w, j % 2, :]
                    pe.matmul(mp[:, 1, 0:P], qk[:, 0:P], qk[:, T:T + P], start=True, stop=True)
                    pe.matmul(mp[:, 1, P:3 * P], qk[:, P:T], qk[:, T:2 * T], start=True, stop=True).then_inc(s2_done.sem, 1)

                def turn_p(j):
                    pe.wait_ge(*e2_done.at2(l, 2 * j + 2))
                    if j:
                        pe.wait_ge(*p2_taken.at2(l, j))
                    for a in range(3):
                        mm = pe.transpose(mp[:, 2, P * a:P * (a + 1)], sc2[:, j % 3, P * a:P * (a + 1)], ident[:, :])
                    mm.then_inc(p2_done.sem, 1)

                def weigh(j):
                    pe.wait_ge(*p2_taken.at2(l, j + 1))
                    if j:
                        pe.wait_ge(*o2_taken.at2(l, j))
                    else:
                        pe.wait_ge(*fox_ready.at2(l, 1))
                    v = job_operands(j)[2]
                    pe.matmul(mp[:, 3, 0:HD], pt2[:, 0:P], v[:, 0, :], start=True, stop=True)
                    pe.matmul(mp[:, 3, HD:2 * HD], pt2[:, P:2 * P], v[:, 0, :], start=True, stop=False)
                    pe.matmul(mp[:, 3, HD:2 * HD], pt2[:, 2 * P:3 * P], v[:, 1, :], start=False, stop=True).then_inc(o2_done.sem, 1)

                for i in range(AJ + 4):
                    if 0 <= i - 1 < AJ:
                        scores(i - 1)
                    if i < AJ:
                        turn_qk(i)
                    if 0 <= i - 4 < AJ:
                        weigh(i - 4)
                    if 0 <= i - 3 < AJ:
                        turn_p(i - 3)
                pe.wait_ge(*oa_ready.at2(l, 1))
                for b in range(4):
                    turn(b, oa, 2 * P * b).then_inc(tr_done.sem, 1)
                pe.wait_ge(*ft_lo.at2(l, X2_O + 4))
                for s in range(S2_OUT, S2_MOE):
                    product(s)
                pe.wait_ge(*h_ready.at2(l, 2))
                for b in range(4):
                    turn(b, x, 2 * P * b).then_inc(tr_done.sem, 1)
                pe.wait_ge(*ft_lo.at2(l, X2_H + 4))
                pe.wait_ge(rw_ready, 1)
                for t in range(NT):
                    ts = slice(P * t, P * (t + 1))
                    for c in range(KD):
                        for m, (a, w) in enumerate(((xt_lo, rw_lo), (xt_hi, rw_lo), (xt_lo, rw_hi), (xt_hi, rw_hi))):
                            mm = pe.matmul(mp[:, 0, NE * t:NE * (t + 1)], a[:, c, ts], w[:, c, :],
                                           start=c == 0 and m == 0, stop=c == KD - 1 and m == 3)
                mm.then_inc(logits_done.sem, 1)
                pe.wait_ge(*chosen.at2(l, 1))
                picked = rank[:, :, :].rearrange("p (t g) i -> p t (g i)", t=NT)
                pe.matmul(mp[:, 1, 0:NE], tri[:, :], picked[:, 0, :], start=True, stop=True)
                pe.matmul(mp[:, 1, NE:2 * NE], ones[:, :], picked[:, 0, :], start=True, stop=False)
                pe.matmul(mp[:, 1, NE:2 * NE], tri[:, :], picked[:, 1, :], start=False, stop=True)
                for t in range(NT):
                    mm = pe.matmul(mp[:, 1, 2 * NE:3 * NE], ones[:, :], picked[:, t, :], start=t == 0, stop=t == 1)
                mm.then_inc(chosen_sum.sem, 1)
                xt, mt = (xt_hi, xt_lo), (mt_hi, mt_lo)

                def turn_ab(e, banks_free):
                    pe.wait_ge(*ab2_ready.at2(l, e))
                    pe.wait_ge(*banks_free)
                    for b in range(2):
                        turn(b, ab2, 2 * P * b).then_inc(tr_done.sem, 1)

                def gather(k, first=False):
                    pe.wait_ge(*pick_ready.at2(l, k + 1))
                    if not first:
                        pe.wait_ge(*xg_low.at2(l, k))
                    for c in range(KD):
                        for t in range(NT):
                            mm = pe.matmul(bank_tr[:, CAP * c:CAP * (c + 1)], x[:, t, P * c:P * (c + 1)], pick[:, t, :], start=t == 0, stop=t == 1)
                    mm.then_inc(gathered.sem, 1)

                def stacked(n, count, bank, chunk0, a, first, last):
                    pe.wait_ge(*raw_read[n % RAW].at2(l, count))
                    w_hi, w_lo = slot(whi, n % SPLIT, 4, COLS), slot(wlo, n % SPLIT, 4, COLS)
                    for unit in range(4):
                        for m, w in enumerate((w_hi, w_lo)):
                            mm = pe.matmul(bank, a[:, chunk0 + unit, :], w[:, unit, :], start=first and unit == 0 and m == 0,
                                           stop=last and unit == 3 and m == 1)
                    mm.then_inc(w_used.sem, 1)

                def turn_gathered(k):
                    pe.wait_ge(*ax_ready.at2(l, k))
                    pe.wait_ge(*place_ready.at2(l, k))
                    pe.wait_ge(*xg_low.at2(l, k + 1))
                    for t in range(NT):
                        pe.transpose(bank_tr[:, T + P * t:T + P * (t + 1)], place[:, t, :], ident[:, :])
                    for c in range(4):
                        mm = pe.transpose(bank_tr[:, CAP * c:CAP * (c + 1)], ax[:, c // 2, P * (c % 2):P * (c % 2 + 1)], ident[0:CAP, 0:CAP])
                    mm.then_inc(ax_turned.sem, 1)

                def scatter(half, first=False, last=False):
                    for t in range(NT):
                        mm = pe.matmul(mp[:, 2 * t + half, :], back[:, P * t:P * (t + 1)], yx[:, half, :], start=first, stop=last)
                    return mm

                def gathered_experts():
                    for p in range(2):
                        pe.wait_ge(*pair_free[p].at2(l, uses[p]))
                    gather(0, True)
                    pe.wait_ge(*flag_ready.at2(l, 1))
                    pe.wait_ge(*y_zero.at2(l, 2))
                    for half in range(2):
                        scatter(half, first=True)
                    pe.wait_ge(*xg_low.at2(l, 1))
                    for i in range(4):
                        n = S2_MOE + i
                        stacked(n, n // RAW + 1, (bank_gate, bank_up)[i // 2], 4 * (i % 2), xg, i % 2 == 0, i % 2 == 1)
                    gather(1)
                    with pe.Fori(1, NE) as e:
                        pe.wait_ge(*xg_low.at2(l, e + 1))
                        for i in range(6):
                            n = S2_MOE + 4 + i
                            count = (e - 1) * 2 + (n // RAW + 1)
                            if i < 4:
                                if i == 0:
                                    pe.wait_ge(*yx_ready.at2(l, (e - 1) * 2))
                                if i == 2:
                                    pe.wait_ge(*up_sum.at2(l, e))
                                stacked(n, count, (bank_gate, bank_up)[i // 2], 4 * (i % 2), xg, i % 2 == 0, i % 2 == 1)
                                if i == 0:
                                    scatter(1)
                                    turn_gathered(e)
                            else:
                                if i == 4:
                                    pe.wait_ge(*ag_low.at2(l, e))
                                    gather(e + 1)
                                    pe.wait_ge(*gate_sum.at2(l, e + 1))
                                stacked(n, count, (bank_gate, bank_y1)[i - 4], 0, ag, True, True)
                        pe.wait_ge(*back_ready.at2(l, e))
                        pe.wait_ge(*yx_ready.at2(l, (e - 1) * 2 + 1))
                        scatter(0)
                    pe.wait_ge(*yx_ready.at2(l, 2 * NE - 2))
                    scatter(1)
                    turn_gathered(NE)
                    pe.wait_ge(*ag_low.at2(l, NE))
                    for i in range(2):
                        n = S2_LAYER - 2 + i
                        stacked(n, n // RAW + 1, (bank_gate, bank_y1)[i], 0, ag, True, True)
                    pe.wait_ge(*back_ready.at2(l, NE))
                    pe.wait_ge(*yx_ready.at2(l, 2 * NE))
                    scatter(0, last=True)
                    scatter(1, last=True).then_inc(y_done.sem, 1)
                    pe.sem_inc(tr_done.sem, 2 * NE)

                uses = [2 * sum(1 for q in range(J2_MOE) if q % 2 == p) for p in range(2)]
                pe.wait_ge(*flag_ready.at2(l, 1))
                pe.sem_inc(loads, 1)
                dense = pe.value_load(dense_i[0:1, 0:1], min_val=0, max_val=1)
                with pe.If(dense == 0):
                    gathered_experts()
                with pe.Else():
                    for i in range(4):
                        q = J2_MOE + i // 2
                        multiply(S2_MOE + i, (S2_MOE + i) // RAW + 1, q, 4, COLS, 4 * (i % 2), xt, i % 2 == 0, i % 2 == 1, uses[q % 2])
                    with pe.Fori(1, NE) as e:
                        f = (e - 1) * 2
                        for i in range(6):
                            n = S2_MOE + 4 + i
                            q = J2_MOE + i // 2 if i < 4 else J2_MOE + (i - 4)
                            if i == 4:
                                pe.wait_ge(*ft_lo.at2(l, f + (X2_MOE + 2)))
                            use = (e - 1) * 4 + (uses[q % 2] + 2 + (2 if i >= 4 else 0))
                            multiply(n, (e - 1) * 2 + (n // RAW + 1), q, 4, COLS, 4 * (i % 2) if i < 4 else 0, xt if i < 4 else mt,
                                     i % 2 == 0 or i >= 4, i % 2 == 1 or i >= 4, use)
                            if i == 0:
                                turn_ab(e, rsc_ready.at2(l, 1))
                    turn_ab(NE, rsc_ready.at2(l, 1))
                    pe.wait_ge(*ft_lo.at2(l, X2_LAYER))
                    for i in range(2):
                        n = S2_LAYER - 2 + i
                        q = J2_MOE + i
                        multiply(n, n // RAW + 1, q, 4, COLS, 0, mt, True, True, uses[q % 2] + 2 + 4 * (NE - 1))
                    for c, n in ((gathered, NE + 1), (ax_turned, NE), (y_done, 1)):
                        pe.sem_inc(c.sem, n)


_INS = ["x", "c", "positions", "norm1_w", "norm2_w", "w_ada", "b_ada", "w_in", "pool_w", "pool_scale", "conv_w",
        "q_norm_w", "k_norm_w", "p_pool", "p_conv", "p_attn", "w_out", "w_gate", "w_up", "w_down",
        "positions_2", "ln_in_g_2", "ln_in_b_2", "w_in_2", "mla_q_norm_g_2", "mla_kv_norm_g_2", "mla_w_uq_2", "mla_w_ukv_2",
        "diff_lam_q1_2", "diff_lam_k1_2", "diff_lam_q2_2", "diff_lam_k2_2", "diff_subln_g_2", "fox_f_bias_2", "w_out_2",
        "ln1_g_2", "ln1_b_2", "router_w_2", "router_bias_2", "exp_w_gate_2", "exp_w_up_2", "exp_w_down_2", "ln2_g_2", "ln2_b_2"]


def kernel(**inputs):
    import concourse.bacc as bacc
    from concourse.bass_utils import run_bass_kernel_spmd

    nc = bacc.Bacc("TRN2", target_bir_lowering=False, num_devices=1)
    arrays, A = {}, {}
    for name in _INS:
        a = np.ascontiguousarray(inputs[name])
        arrays[f"in_{name}"] = a
    arrays.update(constants())
    for name, a in arrays.items():
        A[name.removeprefix("in_")] = nc.dram_tensor(name, a.shape, mybir.dt.from_np(a.dtype), kind="ExternalInput").ap()
    out = nc.dram_tensor("out_0", (1, T, D), F32, kind="ExternalOutput").ap()
    program(nc, A, out)
    return run_bass_kernel_spmd(nc, [arrays], core_ids=[0]).results[0]["out_0"]
```

```python
from contextlib import ExitStack

import numpy as np

import concourse.bass as bass
from concourse import mybir

F32 = mybir.dt.float32
F32R = mybir.dt.float32r
I32 = mybir.dt.int32
ALU = mybir.AluOpType
ACT = mybir.ActivationFunctionType
AX = mybir.AxisListType

P = 128
T = 256
D = 1024
KD = D // P
NT = T // P
LAYERS = 2
COLS = 512
UNITS = 4 * COLS
RAW = 3
SPLIT = 3
EPS = 1e-6

HEADS = 8
HD = 64
ROT = 16
WIN = (2, 4, 8, 16)
FF = 2816
FF_CHUNKS = FF // P
FF_BLOCKS = -(-FF // COLS)

WIN_COLS = [1024, 1536, 2048, 0, 512] + [2560 + COLS * j for j in range(6)]
WIN_JOBS = len(WIN_COLS)

S_WIN = 0
S_BR = S_WIN + 2 * WIN_JOBS
S_OUT = S_BR + 4
S_FF = S_OUT + 4
S_DOWN = S_FF + 4 * FF_BLOCKS
S_LAYER = S_DOWN + FF_CHUNKS // 2 + 1
assert S_LAYER % SPLIT == 0

ADA = 4
AHEAD = 2 * ADA + 1
AFTER = {s: AHEAD + s for s in range(12)}
AFTER.update({S_FF + i: AHEAD + 12 + i for i in range(6 * ADA - 1 - 12)})
AFTER[S_DOWN + 6] = 6 * ADA + AHEAD - 1
assert AHEAD % RAW == 0 and max(AFTER) == S_DOWN + 6 and len(AFTER) == 6 * ADA and S_FF + 6 * ADA - 14 < S_DOWN


def ring_order():
    order = []
    for s in range(S_LAYER):
        order.append(("split", s))
        if s in AFTER:
            order.append(("ada", AFTER[s]))
    assert len(order) % RAW == 0
    return order


RING1 = ring_order()
G_LAYER = len(RING1)
G_OF = {item: g for g, item in enumerate(RING1)}

J_BR = WIN_JOBS
J_OUT = J_BR + 6
J_FF = J_OUT + 2
J_DOWN = J_FF + 2 * FF_BLOCKS
J_LAYER = J_DOWN + 2
PAIR_USES = ((J_LAYER + 1) // 2, J_LAYER // 2)

X_NORM1, X_POOL, X_CONV, X_ATT, X_MERGE, X_NORM2, X_ACT = 0, 4, 5, 6, 8, 12, 16
X_LAYER = X_ACT + FF_CHUNKS // 2
FT_LAYER = 10


def ft_index(f):
    return f if f < X_ATT else f - (X_NORM2 - X_ATT)


CHAIN = 1024

PC_BADA, PC_N1, PC_N2, PC_PS, PC_CW, PC_LAYER = 0, 48, 56, 64, 66, 72
PC_ROWS = PC_LAYER + KD
PAD = 16


IN2 = 2212
CQ, CKV, KR = 384, 256, 32
C_KR, C_DQ, C_DK, C_DV, C_FQ, C_FK, C_FV, C_FF = 640, 672, 928, 1184, 1440, 1696, 1952, 2208
MH, MQ, MN = 8, 96, 64
DH, DW, DROT = 4, 32, 8
FH, FW = 4, 66
NE, FE = 16, 512
ALPHA = (2 * LAYERS) ** 0.25
CAP = 64
LN_EPS = 1e-5
IN2_JOBS = -(-IN2 // COLS)
S2_UQ = 2 * IN2_JOBS
S2_UKV = S2_UQ + 2
S2_OUT = S2_UKV + 2
S2_MOE = S2_OUT + 4
S2_LAYER = S2_MOE + 6 * NE
assert S2_MOE % SPLIT == 0 and 6 % SPLIT == 0 and SPLIT == RAW
J2_UQ = IN2_JOBS
J2_UKV = J2_UQ + 2
J2_OUT = J2_UKV + 2
J2_MOE = J2_OUT + 2
J2_LAYER = J2_MOE + 4 * NE
PAIR2_USES = ((J2_LAYER + 1) // 2, J2_LAYER // 2)
X2_IN, X2_MLA, X2_O, X2_MOE = 0, 4, 7, 15
X2_H = 11
X2_LAYER = X2_MOE + 2 * NE
AJ = MH + 2 * DH + FH
CHAIN2 = 2048


def job2_end(q):
    if q < J2_UQ:
        return 2 * q + 1
    return S2_UQ + q - J2_UQ if q < J2_OUT else S2_OUT + 2 * (q - J2_OUT) + 1


class Count:

    def __init__(self, sem, per, prime=0, per2=0):
        self.sem, self.per, self.prime, self.per2 = sem, per, prime, per2

    def at(self, l, k):
        return self.sem, l * self.per + (k + self.prime)

    def at2(self, l, k):
        return self.sem, l * self.per2 + (k + self.prime + LAYERS * self.per)


def group_jobs(s):
    if s < S_BR:
        h = s % 2
        return [(s // 2, 0, COLS, [(i, 4 * h + i) for i in range(4)], h == 0, h == 1, "xt")]
    if s < S_BR + 2:
        b = s - S_BR
        return [(J_BR + 2 * b + n, COLS * n, COLS, [(i, 2 * b + i) for i in range(2)], True, True, "bt") for n in range(2)]
    if s < S_OUT:
        return [(J_BR + 4 + s - S_BR - 2, 0, COLS, [(i, 4 + i) for i in range(4)], True, True, "bt")]
    if s < S_FF:
        j, h = divmod(s - S_OUT, 2)
        return [(J_OUT + j, 0, COLS, [(i, 4 * h + i) for i in range(4)], h == 0, h == 1, "xt")]
    if s < S_DOWN:
        j, h = divmod(s - S_FF, 2)
        return [(J_FF + j, 0, min(COLS, FF - COLS * (j // 2)), [(i, 4 * h + i) for i in range(4)], h == 0, h == 1, "xt")]
    first, units = down_chunks(s - S_DOWN)
    return [(J_DOWN + n, COLS * n, COLS, [(i, first + i) for i in range(units)], s == S_DOWN, s == S_LAYER - 1, "at")
            for n in range(2)]


def down_chunks(i):
    full = FF_CHUNKS // 2 - 1
    return (2 * i, 2) if i < full else (2 * full + i - full, 1)


JOB_END = {q: s for s in range(S_LAYER) for q, _, _, _, _, last, _ in group_jobs(s) if last}


def constants():
    ident = np.eye(P, dtype=np.float32)
    causal = np.where(np.arange(P)[None, :] <= np.arange(P)[:, None], 0.0, -1e30).astype(np.float32)
    mask = np.concatenate([causal, np.zeros((P, P), np.float32), causal], axis=1)
    count = np.zeros((P, 2, T), np.float32)
    for g, w in enumerate(WIN):
        count[64 * (g % 2):64 * (g % 2) + 64, g // 2, :] = np.float32(1.0) / np.minimum(np.arange(T) + 1, w).astype(np.float32)
    chunk = np.where(np.arange(P)[None, :] // 64 <= np.arange(P)[:, None] // 64, 0.0, -1e30).astype(np.float32)
    mask2 = np.concatenate([chunk, np.zeros((P, P), np.float32), chunk], axis=1)
    tri = (np.arange(P)[:, None] <= np.arange(P)[None, :]).astype(np.float32)
    freq = np.concatenate([np.float32(500000.0) ** (-np.arange(0, r, 2, dtype=np.float32) / np.float32(r))
                           for r in (ROT, KR, DROT)]).astype(np.float32)
    i, j = np.arange(4)[:, None], np.arange(4)[None, :]
    order = np.stack([(j < i), (j > i)]).astype(np.float32).reshape(32)
    lam = np.array([[0.8 - 0.6 * np.exp(-0.3 * l), 1 - (0.8 - 0.6 * np.exp(-0.3 * l))] for l in range(LAYERS)]).astype(np.float32)

    def rows(a):
        return np.ascontiguousarray(np.broadcast_to(a.reshape(-1), (P, a.size)))

    return {"c_ident": ident, "c_mask": mask, "c_mask2": mask2, "c_tri": tri, "c_count": count.reshape(P, 2 * T),
            "c_slot": rows(np.tile(np.arange(1, CAP + 1), 2).astype(np.float32)), "c_freq": rows(freq), "c_order": rows(order), "c_lam": rows(lam)}


def program(nc, A, out):
    with ExitStack() as top:
        def sb(name, shape, dt=F32, ctx=top):
            return ctx.enter_context(nc.sbuf_tensor(name, shape, dt))

        def sem(name):
            return top.enter_context(nc.semaphore(name))

        def counted(name, per, prime=0, per2=0):
            return Count(sem(name), per, prime, per2)

        gp = top.enter_context(nc.psum_tensor("gp", [P, 2, NT, COLS], F32))
        mp = top.enter_context(nc.psum_tensor("mp", [P, 4, COLS], F32))

        raw = sb("raw", [P, RAW, UNITS])
        whi = sb("whi", [P, SPLIT, UNITS], F32R)
        wlo = sb("wlo", [P, SPLIT, UNITS], F32R)
        x = sb("x", [P, NT, D])
        xt_hi = sb("xt_hi", [P, KD, T], F32R)
        xt_lo = sb("xt_lo", [P, KD, T], F32R)
        ft = sb("ft", [P, 2, 2 * T])
        ident = sb("ident", [P, P])
        ones = sb("ones", [P, P])
        mask = sb("mask", [P, 3 * P])
        NF = (ROT + KR + DROT) // 2
        freq = sb("freq", [P, NF])
        order = sb("order", [P, 2, 16])
        lamc = sb("lamc", [P, LAYERS, 2])
        posi = sb("posi", [P, 2, NT], I32)
        posf = sb("posf", [P, 2, NT])
        ang = sb("ang", [P, NT, 2, NF])
        angk = sb("angk", [P, NT, 2, NF])
        cos2, sin2 = ([sb(f"{n}{r}", [P, NT, r]) for r in (ROT, KR, DROT)] for n in ("cos", "sin"))
        rv = sb("rv", [P, 32])
        rs = sb("rs", [P, 32])
        rr = sb("rr", [P, 32])
        rt = sb("rt", [P, 32])
        ssq = sb("ssq", [P, NT])

        one = ExitStack()
        acc = sb("acc", [P, 2, D], ctx=one)
        grow = sb("grow", [P, 2, D], ctx=one)
        count = sb("count", [P, 2, T], ctx=one)
        stage = sb("stage", [PC_ROWS, LAYERS, P], ctx=one)
        pcol = sb("pcol", [P, LAYERS, PC_ROWS], ctx=one)
        pcur = sb("pcur", [P, PC_LAYER], ctx=one)
        cact = sb("cact", [P, KD], ctx=one)
        csig = sb("csig", [P, KD], ctx=one)
        qkw = sb("qkw", [P, LAYERS, 2, HD], ctx=one)
        qkcur = sb("qkcur", [P, 2, HD], ctx=one)
        poolcur = sb("poolcur", [P, 2, P], ctx=one)
        poolw = sb("poolw", [P, LAYERS, 2, P], ctx=one)
        modc = sb("modc", [P, 6, KD], ctx=one)
        scol = sb("scol", [P, 2, KD], ctx=one)
        mix = ExitStack()
        u = sb("u", [P, NT, 5 * COLS], ctx=mix)
        gl = sb("gl", [P, NT, 6 * COLS], ctx=mix)
        qt = sb("qt", [P, 4, T], ctx=mix)
        kt = sb("kt", [P, 4, T], ctx=mix)
        bt_hi = sb("bt_hi", [P, 8, T], F32R, ctx=mix)
        bt_lo = sb("bt_lo", [P, 8, T], F32R, ctx=mix)
        sc = sb("sc", [P, 2, 3 * P], ctx=mix)
        pt = sb("pt", [P, 3 * P], ctx=mix)
        nmax = sb("nmax", [P, 2, NT], ctx=mix)
        rsum = sb("rsum", [P, 2, NT], ctx=mix)
        rinv = sb("rinv", [P, 2, NT], ctx=mix)
        w1 = sb("w1", [P, 2, PAD + T], ctx=mix)
        pp, zp, w2 = (u[:, :, 3 * COLS + i * (PAD + T):3 * COLS + (i + 1) * (PAD + T)] for i in range(3))
        bg = sb("bg", [P, 2, T], ctx=mix)
        mix.close()
        ffn = ExitStack()
        at_hi = sb("at_hi", [P, FF_CHUNKS, T], F32R, ctx=ffn)
        at_lo = sb("at_lo", [P, FF_CHUNKS, T], F32R, ctx=ffn)
        sg = sb("sg", [P, NT, COLS], ctx=ffn)
        ab = sb("ab", [P, NT, COLS], ctx=ffn)
        xn2 = sb("xn2", [P, NT, D], ctx=ffn)
        ffn.close()
        one.close()

        two = ExitStack()
        mask2 = sb("mask2", [P, 3 * P], ctx=two)
        tri = sb("tri", [P, P], ctx=two)
        lnw = sb("lnw", [P, 2, D], ctx=two)
        cen = sb("cen", [P, NT, D], ctx=two)
        stats = sb("stats", [P, NT, 12], ctx=two)
        lsum4 = sb("lsum4", [P, 2 * NT], ctx=two)
        mean = sb("mean", [P, NT, 2], ctx=two)
        cg = sb("cg", [P, LAYERS, CQ + CKV], ctx=two)
        lamr = sb("lamr", [P, LAYERS, 4, DW], ctx=two)
        subg = sb("subg", [P, LAYERS, HD], ctx=two)
        fbias = sb("fbias", [P, LAYERS, FH], ctx=two)
        rw = sb("rw", [P, KD, NE], ctx=two)
        rw2 = sb("rw2", [P, KD, 2, NE], F32R, ctx=two)
        rbias = sb("rbias", [P, NE], ctx=two)
        cgc = sb("cgc", [P, CQ + CKV], ctx=two)
        subc = sb("subc", [P, HD], ctx=two)
        lamt = sb("lamt", [P, 2, DW], ctx=two)
        lame = sb("lame", [P, 2], ctx=two)
        nlam = sb("nlam", [P, 1], ctx=two)
        lamq = sb("lamq", [P, 4, DW], ctx=two)
        lami = sb("lami", [P, 1], ctx=two)
        fbc = sb("fbc", [P, FH], ctx=two)
        pr = sb("pr", [P, NT, IN2], ctx=two)
        mt_hi = sb("mt_hi", [P, 6, T], F32R, ctx=two)
        mt_lo = sb("mt_lo", [P, 6, T], F32R, ctx=two)
        rt1 = sb("rt1", [P, NT * MH * KR], ctx=two)
        rt2 = sb("rt2", [P, NT * MH * KR], ctx=two)
        nmax2 = sb("nmax2", [P, 3, NT], ctx=two)
        rsum2 = sb("rsum2", [P, 3, NT], ctx=two)
        rinv2 = sb("rinv2", [P, 3, NT], ctx=two)
        fz = sb("fz", [P, NT, FH], ctx=two)
        fe = sb("fe", [P, NT, FH], ctx=two)
        fl = sb("fl", [P, NT, FH], ctx=two)
        rsc = sb("rsc", [P, NT, NE], ctx=two)
        rb = sb("rb", [P, NT, NE], ctx=two)
        cmp1 = sb("cmp1", [P, 8, 16], ctx=two)
        cmp2 = sb("cmp2", [P, 8, 16], ctx=two)
        rank = sb("rank", [P, 8, 4], ctx=two)
        gs = sb("gs", [P, 8], ctx=two)
        gr = sb("gr", [P, 8], ctx=two)
        den = sb("den", [P, NT], ctx=two)
        dg = sb("dg", [P, NT, NE], ctx=two)
        slots = sb("slots", [P, 2 * CAP], ctx=two)
        key = sb("key", [P, NT, NE + 1], ctx=two)
        many = sb("many", [P, 1], ctx=two)
        dense_i = sb("dense_i", [P, 1], I32, ctx=two)
        heads = ExitStack()
        qm = sb("qm", [P, NT, MH, MQ], ctx=heads)
        km = sb("km", [P, NT, MH, MQ], ctx=heads)
        vm = sb("vm", [P, NT, MH, HD], ctx=heads)
        fq = sb("fq", [P, NT, FH, FW], ctx=heads)
        fk = sb("fk", [P, NT, FH, FW], ctx=heads)
        od = sb("od", [P, NT, DH * HD], ctx=heads)
        qkt = sb("qkt", [P, 2, 4 * P], ctx=heads)
        sc2 = sb("sc2", [P, 3, 3 * P], ctx=heads)
        pt2 = sb("pt2", [P, 3 * P], ctx=heads)
        heads.close()
        raw_more = sb("raw_more", [P, RAW, UNITS], ctx=two)
        two.close()
        sg2, ab2 = pr[:, :, 0:COLS], pr[:, :, COLS:2 * COLS]
        gx, ux, gxl, uxl = pr[0:CAP, 0, 0:COLS], pr[0:CAP, 1, 0:COLS], pr[0:CAP, 0, COLS:D], pr[0:CAP, 1, COLS:D]
        ax, yx = pr[0:CAP, :, D:D + COLS // 2], pr[:, :, D + COLS:2 * D]
        pick, place = pr[:, :, D + COLS // 2:D + COLS // 2 + CAP], pr[:, :, D + COLS // 2 + CAP:D + COLS // 2 + 3 * CAP]
        back = cgc[:, 0:T]
        xg, ag = xt_hi[:, :, 0:2 * CAP], mt_hi[:, 0:4, 0:2 * CAP]
        oa = cen
        xn1 = gl[:, :, 0:D]
        merged = u[:, :, 3 * COLS:5 * COLS]
        o = u[:, :, 0:COLS]
        stationary = {"xt": (xt_hi, xt_lo), "bt": (bt_hi, bt_lo), "at": (at_hi, at_lo)}

        landed = [counted(f"landed{i}", 16 * G_LAYER // RAW, 16 * AHEAD // RAW, 16 * (S2_MOE // RAW + NE)) for i in range(RAW)]
        raw_read = [counted(f"raw_read{i}", G_LAYER // RAW, 1 + AHEAD // RAW, S2_MOE // RAW + NE) for i in range(RAW)]
        landed_more = [counted(f"landed_more{i}", 0, 0, 16 * NE) for i in range(RAW)]
        more_read = [counted(f"more_read{i}", 0, 1, NE) for i in range(RAW)]
        hi_done = counted("hi_done", S_LAYER, 0, S2_LAYER)
        w_used = counted("w_used", S_LAYER, SPLIT, S2_LAYER)
        pair_free = [counted(f"pair_free{p}", 2 * PAIR_USES[p], 2, 2 * PAIR2_USES[p]) for p in range(2)]
        consts_in, x_in, params_in, params_t, zeroed = map(sem, ("consts_in", "x_in", "params_in", "params_t", "zeroed"))
        stage_in, positions_in = map(sem, ("stage_in", "positions_in"))
        params_ready, csig_ready, ang_ready, rope_ready = map(sem, ("params_ready", "csig_ready", "ang_ready", "rope_ready"))
        acc_done = counted("acc_done", 6)
        acc_read = counted("acc_read", 6, 2)
        mod_taken = counted("mod_taken", 6, 1)
        grow_in = counted("grow_in", 32)
        sq_done = counted("sq_done", 6)
        rv_ready = counted("rv_ready", 3)
        rs_ready = counted("rs_ready", 3)
        rr_ready = counted("rr_ready", 3)
        xn_ready = counted("xn_ready", 4)
        tr_done = counted("tr_done", X_LAYER - 1, 0, X2_LAYER)
        ft_ready = counted("ft_ready", FT_LAYER)
        ft_hi = counted("ft_hi", X_LAYER, 0, X2_LAYER)
        ft_lo = counted("ft_lo", X_LAYER, 2, X2_LAYER)
        x_final = counted("x_final", 4, 1)
        qk_ready = counted("qk_ready", 1)
        qkt_done = counted("qkt_done", 1)
        qkt_taken = counted("qkt_taken", 4)
        cu_ready = counted("cu_ready", 1)
        pct_done = counted("pct_done", 1)
        pct_taken = counted("pct_taken", 3)
        pads_zero = counted("pads_zero", 2)
        s_done = counted("s_done", HEADS)
        s_max = counted("s_max", HEADS)
        e_done = counted("e_done", 2 * HEADS)
        pt_done = counted("pt_done", HEADS)
        pt_taken = counted("pt_taken", HEADS)
        o_done = counted("o_done", HEADS)
        o_taken = counted("o_taken", HEADS)
        pooled = counted("pooled", 1)
        gates_ready = counted("gates_ready", 6)
        merged_ready = counted("merged_ready", 2)
        silu_done = counted("silu_done", FF_BLOCKS)
        ab_ready = counted("ab_ready", FF_BLOCKS)
        column_0 = sem("column_0")
        lnw_in = counted("lnw_in", 0, 32, 64)
        params2_in = sem("params2_in")
        rw_ready = counted("rw_ready", 0, 0, 1)
        rw_high = counted("rw_high", 0, 0, 1)
        h_ready = counted("h_ready", 0, 2, 4)
        rv2_ready = counted("rv2_ready", 0, 1, 4)
        rs2_ready = counted("rs2_ready", 0, 1, 4)
        mla_sq = counted("mla_sq", 0, 0, 4)
        mla_ready = counted("mla_ready", 0, 0, 1)
        lam_sum = counted("lam_sum", 0, 0, 1)
        lam_exp = counted("lam_exp", 0, 0, 1)
        fz_ready = counted("fz_ready", 0, 0, 1)
        fe_ready = counted("fe_ready", 0, 0, 1)
        fl_ready = counted("fl_ready", 0, 0, 1)
        logf_ready = counted("logf_ready", 0, 0, 1)
        cum_done = counted("cum_done", 0, 0, 1)
        diff_ready = counted("diff_ready", 0, 0, 1)
        fox_ready = counted("fox_ready", 0, 0, 1)
        km_ready = counted("km_ready", 0, 0, 1)
        t2_done = counted("t2_done", 0, 0, AJ)
        t2_taken = counted("t2_taken", 0, 0, AJ)
        s2_done = counted("s2_done", 0, 0, AJ)
        s2_max = counted("s2_max", 0, 0, AJ)
        e2_done = counted("e2_done", 0, 0, 2 * AJ)
        p2_done = counted("p2_done", 0, 0, AJ)
        p2_taken = counted("p2_taken", 0, 0, AJ)
        o2_done = counted("o2_done", 0, 0, AJ)
        o2_taken = counted("o2_taken", 0, 0, AJ)
        oa_ready = counted("oa_ready", 0, 0, 1)
        logits_done = counted("logits_done", 0, 0, 1)
        logit_sum = counted("logit_sum", 0, 0, 1)
        rsc_ready = counted("rsc_ready", 0, 0, 1)
        silu2_done = counted("silu2_done", 0, 0, NE)
        ab2_ready = counted("ab2_ready", 0, 0, NE)
        x2_sum = counted("x2_sum", 0, 0, 2)
        y_taken = counted("y_taken", 0, 0, 2 * NE)
        chosen = counted("chosen", 0, 0, 1)
        chosen_sum = counted("chosen_sum", 0, 0, 1)
        flag_ready = counted("flag_ready", 0, 0, 1)
        flag_seen = sem("flag_seen")
        loads = sem("loads")
        pick_ready = counted("pick_ready", 0, 0, NE + 1)
        gathered = counted("gathered", 0, 0, NE + 1)
        xg_high = counted("xg_high", 0, 0, NE + 1)
        xg_low = counted("xg_low", 0, 0, NE + 1)
        gate_out = counted("gate_out", 0, 0, NE)
        gate_sum = counted("gate_sum", 0, 0, NE)
        silux = counted("silux", 0, 0, NE)
        up_out = counted("up_out", 0, 0, NE)
        up_sum = counted("up_sum", 0, 0, NE)
        ax_ready = counted("ax_ready", 0, 0, NE)
        place_ready = counted("place_ready", 0, 0, NE)
        ax_turned = counted("ax_turned", 0, 0, NE)
        back_ready = counted("back_ready", 0, 0, NE)
        ag_high = counted("ag_high", 0, 0, NE)
        ag_low = counted("ag_low", 0, 0, NE)
        yx_ready = counted("yx_ready", 0, 2, 2 * NE)
        y_zero = counted("y_zero", 0, 0, 2)
        y_done = counted("y_done", 0, 0, 1)
        out_done = sem("out_done")
        rows_free = sem("rows_free")
        v_chain = sem("v_chain")
        v_moe = sem("v_moe")

        block = top.enter_context(nc.Block())

        def weights(item, l):
            kind, n = item
            if kind == "ada":
                vec, i = divmod(n % (6 * ADA), ADA)
                return A["w_ada"][(l + 1) % LAYERS if n >= 6 * ADA else l, 2 * P * i:2 * P * (i + 1), D * vec:D * (vec + 1)], 2, D
            h = n % 2
            if n < S_BR:
                c = WIN_COLS[n // 2]
                return A["w_in"][l, 4 * P * h:4 * P * (h + 1), c:c + COLS], 4, COLS
            if n < S_BR + 2:
                return A[("p_pool", "p_conv")[n - S_BR]][l, :, :], 2, D
            if n < S_OUT:
                j = n - S_BR - 2
                return A["p_attn"][l, :, COLS * j:COLS * (j + 1)], 4, COLS
            if n < S_FF:
                j = (n - S_OUT) // 2
                return A["w_out"][l, 4 * P * h:4 * P * (h + 1), COLS * j:COLS * (j + 1)], 4, COLS
            if n < S_DOWN:
                j, r = divmod(n - S_FF, 4)
                wide = min(COLS, FF - COLS * j)
                return A["w_gate" if r < 2 else "w_up"][l, 4 * P * h:4 * P * (h + 1), COLS * j:COLS * j + wide], 4, wide
            first, units = down_chunks(n - S_DOWN)
            return A["w_down"][l, P * first:P * (first + units), :], units, D

        def weights2(s, l):
            if s < S2_UQ:
                j, h = divmod(s, 2)
                wide = min(COLS, IN2 - COLS * j)
                return A["w_in_2"][l, 4 * P * h:4 * P * (h + 1), COLS * j:COLS * j + wide], 4, wide
            if s < S2_UKV:
                wide = MH * MQ // 2
                return A["mla_w_uq_2"][l, :, wide * (s - S2_UQ):wide * (s - S2_UQ + 1)], 3, wide
            if s < S2_OUT:
                return A["mla_w_ukv_2"][l, :, COLS * (s - S2_UKV):COLS * (s - S2_UKV + 1)], 2, COLS
            j, h = divmod(s - S2_OUT, 2)
            return A["w_out_2"][l, 4 * P * h:4 * P * (h + 1), COLS * j:COLS * (j + 1)], 4, COLS

        def expert_weights(l, e, i):
            if i < 4:
                return A["exp_w_gate_2" if i < 2 else "exp_w_up_2"][l, e, 4 * P * (i % 2):4 * P * (i % 2 + 1), :]
            return A["exp_w_down_2"][l, e, :, COLS * (i - 4):COLS * (i - 3)]

        def slot(buf, n, units, cols):
            return buf[:, n, 0:units * cols].rearrange("p (k n) -> p k n", k=units)

        def ring2(n):
            if n < S2_MOE:
                return raw, landed[n % RAW], raw_read[n % RAW], n // RAW
            turns, m = divmod(n - S2_MOE, 2 * RAW)
            if m < RAW:
                return raw, landed[m], raw_read[m], S2_MOE // RAW + turns
            return raw_more, landed_more[m - RAW], more_read[m - RAW], turns

        def job_width(j):
            return MQ if j < MH else DW if j < MH + 2 * DH else FW

        def job_operands(j):
            if j < MH:
                return qm[:, :, j, :], km[:, :, j, :], vm[:, :, j, :], MQ ** -0.5, mask2
            if j < MH + 2 * DH:
                i = j - MH
                return (pr[:, :, C_DQ + DW * i:C_DQ + DW * (i + 1)], pr[:, :, C_DK + DW * i:C_DK + DW * (i + 1)],
                        pr[:, :, C_DV + HD * (i // 2):C_DV + HD * (i // 2 + 1)], DW ** -0.5, mask2)
            i = j - MH - 2 * DH
            return fq[:, :, i, :], fk[:, :, i, :], pr[:, :, C_FV + HD * i:C_FV + HD * (i + 1)], HD ** -0.5, mask

        MOD_BANK = (0, 1, 0, 2, 0, 2)
        GATE_PAIR = J2_MOE % 2
        bank_gate, bank_up, bank_y1, bank_tr = gp[:, 0, 0, :], gp[:, 0, 1, :], gp[:, 1, 0, :], gp[:, 1, 1, :]
        small = bank_y1

        def chunks(bank):
            return bank.rearrange("p (k t) -> p k t", k=2)

        @block.sync
        def _(sp):
            for name, tile in (("c_ident", ident[:, :]), ("c_mask", mask[:, :]),
                               ("c_count", count[:, :, :].rearrange("p a t -> p (a t)")), ("c_freq", freq[:, :]),
                               ("c_order", order[:, :, :].rearrange("p a n -> p (a n)")),
                               ("c_lam", lamc[:, :, :].rearrange("p l n -> p (l n)"))):
                sp.dma_start(tile, A[name]).then_inc(consts_in, 16)
            def load_group(item, l, g):
                src, units, cols = weights(item, l)
                sp.dma_start(slot(raw, g % RAW, units, cols),
                             src.rearrange("(k p) n -> p k n", p=P)).then_inc(landed[g % RAW].sem, 16)

            for n in range(AHEAD):
                if n >= RAW:
                    sp.wait_ge(*raw_read[n % RAW].at(0, (n - AHEAD) // RAW))
                load_group(("ada", n), 0, n)
                if n == 0:
                    sp.dma_start(x[:, :, :], A["x"].rearrange("b (t p) d -> p (b t) d", p=P)).then_inc(x_in, 16)
            with sp.Fori(0, LAYERS) as l:
                for g, item in enumerate(RING1):
                    sp.wait_ge(*raw_read[g % RAW].at(l, g // RAW))
                    if item == ("split", 2 * WIN_COLS.index(0)):
                        sp.sem_inc(column_0, 1)
                    if item[0] == "ada" and item[1] >= 6 * ADA:
                        sp.sem_inc(column_0, 1)
                        with sp.If(l < LAYERS - 1):
                            load_group(item, l, g)
                        with sp.Else():
                            sp.sem_inc(landed[g % RAW].sem, 16)
                    else:
                        load_group(item, l, g)
            with sp.Fori(0, LAYERS) as l:
                def load(n, turn, src, units, cols):
                    buf, there, read, before = ring2(n)
                    if n == S2_MOE + RAW:
                        sp.wait_ge(*oa_ready.at2(l, 1))
                    sp.wait_ge(*read.at2(l, turn + before))
                    sp.dma_start(slot(buf, n % RAW, units, cols), src.rearrange("(k p) n -> p k n", p=P)).then_inc(there.sem, 16)

                for s in range(S2_MOE):
                    src, units, cols = weights2(s, l)
                    load(s, 0, src, units, cols)
                for i in range(4):
                    load(S2_MOE + i, 0, expert_weights(l, 0, i), 4, COLS)
                with sp.Fori(1, NE) as e:
                    for i in range(6):
                        load(S2_MOE + 4 + i, e - 1, expert_weights(l, e if i < 4 else e - 1, i), 4, COLS)
                for i in range(4, 6):
                    load(S2_LAYER - 6 + i, 0, expert_weights(l, NE - 1, i), 4, COLS)
            sp.wait_ge(*h_ready.at2(LAYERS, 0))
            sp.dma_start(out.rearrange("b (t p) d -> p (b t) d", p=P), x[:, :, :]).then_inc(out_done, 16)
            sp.wait_ge(out_done, 16)

        @block.gpsimd
        def _(pool):
            for i, name in enumerate(("positions", "positions_2")):
                for t in range(NT):
                    pool.dma_start(posi[:, i, t:t + 1],
                                   A[name][0, P * t:P * (t + 1)].rearrange("(p a) -> p a", a=1)).then_inc(positions_in, 16)
            pool.memset(ones[:, :], 1.0).then_inc(zeroed, 1)
            pool.memset(poolw[:, :, :, :], 0.0).then_inc(zeroed, 1)
            pool.wait_ge(zeroed, 2)
            for l in range(LAYERS):
                for i, name in enumerate(("q_norm_w", "k_norm_w")):
                    pool.dma_start(qkw[:, l, i, :], A[name][l].partition_broadcast(P)).then_inc(params_in, 16)
                for g in range(4):
                    h = 64 * (g % 2)
                    pool.dma_start(poolw[h:h + 64, l, g // 2, h:h + 64], A["pool_w"][l, g, :, :]).then_inc(params_in, 16)
            with pool.Fori(0, LAYERS) as l:
                pool.wait_ge(*x_final.at(l, 0))
                for i, vec in enumerate((2, 5)):
                    pool.dma_start(grow[:, i, :],
                                   A["b_ada"][l, D * vec:D * (vec + 1)].partition_broadcast(P)).then_inc(grow_in.sem, 16)
            pool.wait_ge(*x_final.at(LAYERS, 0))

            def norm_rows(gain, bias):
                pool.dma_start(lnw[:, 0, :], gain.partition_broadcast(P)).then_inc(lnw_in.sem, 16)
                pool.dma_start(lnw[:, 1, :], bias.partition_broadcast(P)).then_inc(lnw_in.sem, 16)

            norm_rows(A["ln_in_g_2"], A["ln_in_b_2"])
            pool.dma_start(mask2[:, :], A["c_mask2"]).then_inc(params2_in, 16)
            pool.dma_start(tri[:, :], A["c_tri"]).then_inc(params2_in, 16)
            pool.dma_start(slots[:, :], A["c_slot"]).then_inc(params2_in, 16)
            for l in range(LAYERS):
                for dst, src in ((cg[:, l, 0:CQ], A["mla_q_norm_g_2"]), (cg[:, l, CQ:CQ + CKV], A["mla_kv_norm_g_2"]),
                                 (lamr[:, l, 0, :], A["diff_lam_q1_2"]), (lamr[:, l, 1, :], A["diff_lam_q2_2"]),
                                 (lamr[:, l, 2, :], A["diff_lam_k1_2"]), (lamr[:, l, 3, :], A["diff_lam_k2_2"]),
                                 (subg[:, l, :], A["diff_subln_g_2"]), (fbias[:, l, :], A["fox_f_bias_2"])):
                    pool.dma_start(dst, src[l].partition_broadcast(P)).then_inc(params2_in, 16)
            pool.dma_start(rw[:, :, :], A["router_w_2"].rearrange("(k p) n -> p k n", p=P)).then_inc(params2_in, 16)
            pool.dma_start(rbias[:, :], A["router_bias_2"].partition_broadcast(P)).then_inc(params2_in, 16)
            with pool.Fori(0, LAYERS) as l:
                pool.wait_ge(*h_ready.at2(l, 0))
                pool.sem_inc(rows_free, 1)
                norm_rows(A["ln1_g_2"][l], A["ln1_b_2"][l])
                pool.wait_ge(*h_ready.at2(l, 2))
                pool.sem_inc(rows_free, 1)
                norm_rows(A["ln2_g_2"][l], A["ln2_b_2"][l])

        PARAMS = 16 * LAYERS * 6
        STAGE = 16 * LAYERS * 6
        PARAMS2 = 16 * (LAYERS * 8 + 5)

        @block.scalar
        def _(act):
            for l in range(LAYERS):
                rows = ((A["b_ada"][l], PC_BADA, 48), (A["norm1_w"][l], PC_N1, KD), (A["norm2_w"][l], PC_N2, KD),
                        (A["pool_scale"][l], PC_PS, 2), (A["c"][0], PC_LAYER, KD))
                for src, at, n in rows:
                    act.dma_start(stage[at:at + n, l, :], src.rearrange("(a p) -> a p", p=P)).then_inc(stage_in, 16)
                act.dma_start(stage[PC_CW:PC_CW + 6, l, :],
                              A["conv_w"][l].rearrange("k (a p) -> (k a) p", p=P)).then_inc(stage_in, 16)
            act.sem_inc(yx_ready.sem, yx_ready.prime)
            act.wait_ge(ang_ready, 1)
            act.activation(angk[:, :, :, :], ang[:, :, :, :], ACT.Sin).then_inc(rope_ready, 1)
            act.wait_ge(params_ready, LAYERS)
            act.activation(csig[:, :], pcol[:, 0, PC_LAYER:PC_ROWS], ACT.Sigmoid).then_inc(csig_ready, 1)
            act.wait_ge(x_in, 16)

            with act.Fori(0, LAYERS) as l:
                def split(s):
                    g = G_OF["split", s]
                    _, units, cols = weights(("split", s), l)
                    act.wait_ge(*landed[g % RAW].at(l, 16 * (g // RAW + 1)))
                    act.wait_ge(*w_used.at(l, s + 1 - SPLIT))
                    act.activation(slot(whi, s % SPLIT, units, cols), slot(raw, g % RAW, units, cols),
                                   ACT.Copy).then_inc(hi_done.sem, 1)

                def high_plain(bank, f, dst):
                    act.wait_ge(*tr_done.at(l, f))
                    act.activation(dst, chunks(mp[:, bank, :]), ACT.Copy).then_inc(ft_hi.sem, 1)

                def high(f, dst):
                    act.wait_ge(*ft_ready.at(l, ft_index(f) + 1))
                    act.activation(dst, chunks(ft[:, f % 2, :]), ACT.Copy).then_inc(ft_hi.sem, 1)

                def root(i, n):
                    act.wait_ge(*rv_ready.at(l, i + 1))
                    act.activation(rs[:, 0:n], rv[:, 0:n], ACT.Sqrt).then_inc(rs_ready.sem, 1)

                def normalise(xn, i):
                    for t in range(NT):
                        act.activation(xn[:, t, :], x[:, t, :], ACT.Square, accum_out=ssq[:, t:t + 1]).then_inc(sq_done.sem, 1)
                    root(i, NT)
                    act.wait_ge(*rr_ready.at(l, i + 1))
                    for t in range(NT):
                        act.activation(xn[:, t, :], x[:, t, :], ACT.Copy, scale=rr[:, t:t + 1]).then_inc(xn_ready.sem, 1)

                def take_w_in(j):
                    act.wait_ge(*w_used.at(l, JOB_END[j] + 1))
                    if j < 5:
                        act.activation(u[:, 0, COLS * j:COLS * (j + 1)], gp[:, j % 2, 0, :], ACT.Copy).then_inc(pair_free[j % 2].sem, 1)
                    else:
                        act.activation(gl[:, :, COLS * (j - 5):COLS * (j - 4)], gp[:, j % 2, :, :], ACT.Copy).then_inc(pair_free[j % 2].sem, 2)

                act.wait_ge(*x_final.at(l, 0))
                normalise(xn1, 0)
                split(0)
                split(1)
                for b in range(4):
                    high(X_NORM1 + b, xt_hi[:, 2 * b:2 * b + 2, :])
                for s in range(10):
                    split(s + 2)
                    if s % 2:
                        take_w_in(s // 2)
                    if s == 5:
                        act.wait_ge(*pair_free[0].at(l, 2))
                        act.wait_ge(*pair_free[1].at(l, 2))
                        for t in range(NT):
                            act.activation(gl[:, t, 0:D], u[:, t, 0:D], ACT.Square).then_inc(sq_done.sem, 1)
                    if s == 6:
                        root(1, 2 * NT * HEADS)
                for i in range(12):
                    split(10 + i + 2)
                    if i % 2:
                        take_w_in(5 + i // 2)
                    if i == 0:
                        act.wait_ge(*qkt_done.at(l, 1))
                        for b in range(4):
                            dst = (qt, kt)[b // 2][:, 2 * (b % 2):2 * (b % 2) + 2, :]
                            act.activation(dst, chunks(mp[:, b, :]), ACT.Copy).then_inc(qkt_taken.sem, 1)
                    if i == 1:
                        act.wait_ge(*pct_done.at(l, 1))
                        for b, dst in enumerate((pp[:, :, PAD:PAD + T], zp[:, :, PAD:PAD + T], bg[:, :, :])):
                            act.activation(dst, chunks(mp[:, b, :]), ACT.Copy).then_inc(pct_taken.sem, 1)
                    h = i - 2
                    if 0 <= h < HEADS:
                        act.wait_ge(*s_max.at(l, h + 1))
                        for t, (a, b) in enumerate(((0, P), (P, 3 * P))):
                            act.activation(sc[:, h % 2, a:b], sc[:, h % 2, a:b], ACT.Exp, bias=nmax[:, h % 2, t:t + 1],
                                           accum_out=rsum[:, h % 2, t:t + 1]).then_inc(e_done.sem, 1)
                    h = i - 3
                    if 0 <= h < HEADS:
                        act.wait_ge(*pt_done.at(l, h + 1))
                        act.activation(pt[:, :], mp[:, 2, 0:3 * P], ACT.Copy).then_inc(pt_taken.sem, 1)
                high(X_POOL, bt_hi[:, 0:2, :])
                high(X_CONV, bt_hi[:, 2:4, :])
                for i in range(6):
                    act.wait_ge(*pair_free[(5 + i) % 2].at(l, 2 * ((5 + i) // 2) + 2))
                    act.activation(gl[:, :, COLS * i:COLS * (i + 1)], gl[:, :, COLS * i:COLS * (i + 1)], ACT.Sigmoid).then_inc(gates_ready.sem, 1)
                    if i == 1:
                        for b in range(2):
                            high_plain(2 + b, X_ATT + b, bt_hi[:, 4 + 2 * b:6 + 2 * b, :])
                for s in range(S_BR, S_OUT):
                    split(s + 2)
                for b in range(4):
                    high_plain(b, X_MERGE + b, xt_hi[:, 2 * b:2 * b + 2, :])
                for s in range(S_OUT, S_FF):
                    split(s + 2)
                act.wait_ge(*x_final.at(l, 2))
                normalise(xn2, 2)
                for b in range(4):
                    high(X_NORM2 + b, xt_hi[:, 2 * b:2 * b + 2, :])
                for s in range(S_FF, S_DOWN):
                    split(s + 2)
                    j, r = divmod(s - S_FF, 4)
                    wide = min(COLS, FF - COLS * j)
                    if r == 2:
                        if j >= 1:
                            for b in range(2):
                                high_plain(2 * ((j - 1) % 2) + b, X_ACT + 2 * (j - 1) + b, at_hi[:, 4 * (j - 1) + 2 * b:4 * (j - 1) + 2 * b + 2, :])
                            act.wait_ge(*ab_ready.at(l, j))
                        q = J_FF + 2 * j
                        act.wait_ge(*w_used.at(l, JOB_END[q] + 1))
                        act.activation(sg[:, :, 0:wide], gp[:, q % 2, :, 0:wide], ACT.Silu).then_inc(silu_done.sem, 1)
                for s in range(S_DOWN, S_LAYER - 2):
                    split(s + 2)
                    if s == S_DOWN + 1:
                        high_plain(2, X_ACT + 2 * (FF_BLOCKS - 1), at_hi[:, FF_CHUNKS - 2:FF_CHUNKS, :])

            def layer_norm_root(variances):
                act.wait_ge(*variances)
                act.activation(rs[:, 0:NT], rv[:, 0:NT], ACT.Sqrt).then_inc(rs2_ready.sem, 1)

            layer_norm_root((rv2_ready.sem, 1))

            with act.Fori(0, LAYERS) as l:
                def split_at(n, turn, units, cols):
                    buf, there, _, before = ring2(n)
                    act.wait_ge(*there.at2(l, turn * 16 + 16 * (before + 1)))
                    act.wait_ge(*w_used.at2(l, turn * 6 + (n + 1 - SPLIT)))
                    act.activation(slot(whi, n % SPLIT, units, cols), slot(buf, n % RAW, units, cols),
                                   ACT.Copy).then_inc(hi_done.sem, 1)

                def split(s):
                    units, cols = weights2(s, l)[1:] if s < S2_MOE else (4, COLS)
                    split_at(s, 0, units, cols)

                def high(bank, f, dst, n=2):
                    act.wait_ge(*tr_done.at2(l, f + 1))
                    act.activation(dst, mp[:, bank, 0:T * n].rearrange("p (k t) -> p k t", k=n), ACT.Copy).then_inc(ft_hi.sem, 1)

                def high_x(f0):
                    for b in range(4):
                        high(b, f0 + b, xt_hi[:, 2 * b:2 * b + 2, :])

                def take(q, dst):
                    act.wait_ge(*w_used.at2(l, job2_end(q) + 1))
                    act.activation(dst, gp[:, q % 2, 0, 0:dst.shape[-1]], ACT.Copy).then_inc(pair_free[q % 2].sem, 1)

                split(0)
                split(1)
                high_x(X2_IN)
                for s in range(S2_UQ):
                    split(s + 2)
                    if s == 1:
                        act.wait_ge(params2_in, PARAMS2)
                        act.activation(rw2[:, :, 0, :], rw[:, :, :], ACT.Copy).then_inc(rw_high.sem, 1)
                    if s % 2:
                        j = s // 2
                        take(j, pr[:, 0, COLS * j:min(COLS * (j + 1), IN2)])
                    if s == 3:
                        act.wait_ge(*pair_free[0].at2(l, 2))
                        act.wait_ge(*pair_free[1].at2(l, 2))
                        for t in range(NT):
                            act.activation(rt1[:, 0:CQ], pr[:, t, 0:CQ], ACT.Square, accum_out=lsum4[:, t:t + 1]).then_inc(mla_sq.sem, 1)
                            act.activation(rt2[:, 0:CKV], pr[:, t, CQ:CQ + CKV], ACT.Square, accum_out=lsum4[:, 2 + t:3 + t]).then_inc(mla_sq.sem, 1)
                            act.wait_ge(*mla_sq.at2(l, 2 * t + 2))
                        act.wait_ge(*rv2_ready.at2(l, 1))
                        act.activation(rs[:, 0:4], rv[:, 0:4], ACT.Sqrt).then_inc(rs2_ready.sem, 1)
                for b in range(3):
                    n = 2 if b < 2 else 1
                    high(b, X2_MLA + b, mt_hi[:, 2 * b:2 * b + n, :], n)
                act.wait_ge(*fz_ready.at2(l, 1))
                act.activation(fe[:, :, :], fe[:, :, :], ACT.Exp).then_inc(fe_ready.sem, 1)
                act.wait_ge(*lam_sum.at2(l, 1))
                act.activation(lame[:, :], lame[:, :], ACT.Exp).then_inc(lam_exp.sem, 1)
                act.wait_ge(*fe_ready.at2(l, 1))
                act.activation(fl[:, :, :], fe[:, :, :], ACT.Ln, bias=1.0).then_inc(fl_ready.sem, 1)
                for s in range(S2_UQ, S2_OUT):
                    split(s + 2)
                    q = J2_UQ + s - S2_UQ
                    if s < S2_UKV:
                        h = 4 * (s - S2_UQ)
                        take(q, qm[:, 0, h:h + 4, :].rearrange("p h d -> p (h d)"))
                for i in range(AJ + 4):
                    if i < AJ:
                        act.wait_ge(*t2_done.at2(l, i + 1))
                        w = job_width(i)
                        act.activation(qkt[0:w, i % 2, :], mp[0:w, 0, :], ACT.Copy).then_inc(t2_taken.sem, 1)
                    j = i - 2
                    if 0 <= j < AJ:
                        act.wait_ge(*s2_max.at2(l, j + 1))
                        if j >= 3:
                            act.wait_ge(*o2_taken.at2(l, j - 2))
                        for t, (a, b) in enumerate(((0, P), (P, 3 * P))):
                            act.activation(sc2[:, j % 3, a:b], sc2[:, j % 3, a:b], ACT.Exp, bias=nmax2[:, j % 3, t:t + 1],
                                           accum_out=rsum2[:, j % 3, t:t + 1]).then_inc(e2_done.sem, 1)
                    j = i - 3
                    if 0 <= j < AJ:
                        act.wait_ge(*p2_done.at2(l, j + 1))
                        act.activation(pt2[:, :], mp[:, 2, 0:3 * P], ACT.Copy).then_inc(p2_taken.sem, 1)
                act.wait_ge(*rv2_ready.at2(l, 2))
                act.activation(rs[:, 0:NT * DH], rv[:, 0:NT * DH], ACT.Sqrt).then_inc(rs2_ready.sem, 1)
                high_x(X2_O)
                for s in range(S2_OUT, S2_MOE):
                    split(s + 2)
                layer_norm_root(rv2_ready.at2(l, 3))
                high_x(X2_H)
                act.wait_ge(*logit_sum.at2(l, 1))
                act.activation(rsc[:, :, :], rsc[:, :, :], ACT.Sigmoid).then_inc(rsc_ready.sem, 1)

                def silu(e, k):
                    act.wait_ge(*w_used.at2(l, k))
                    act.wait_ge(*ab2_ready.at2(l, e))
                    act.activation(sg2, gp[:, GATE_PAIR, :, :], ACT.Silu).then_inc(silu2_done.sem, 1)

                def part(src, dst, done):
                    act.activation(dst, src[CAP:2 * CAP, :], ACT.Copy).then_inc(done.sem, 1)

                def high_tokens(k):
                    act.wait_ge(*gathered.at2(l, k))
                    act.activation(xg[:, :, 0:CAP], bank_tr.rearrange("p (c s) -> p c s", c=KD), ACT.Copy).then_inc(xg_high.sem, 1)

                def take_turned(k):
                    act.wait_ge(*ax_turned.at2(l, k))
                    act.activation(back, bank_tr[:, T:2 * T], ACT.Copy).then_inc(back_ready.sem, 1)
                    act.activation(ag[:, :, 0:CAP], bank_tr[:, 0:T].rearrange("p (c s) -> p c s", c=4), ACT.Copy).then_inc(ag_high.sem, 1)

                def gate_part(n, e):
                    act.wait_ge(*w_used.at2(l, n))
                    if not isinstance(e, int):
                        act.wait_ge(*gate_sum.at2(l, e))
                    part(bank_gate, gxl, gate_out)

                def silu_x(e):
                    act.wait_ge(*gate_sum.at2(l, e + 1))
                    act.activation(gx, gx, ACT.Silu).then_inc(silux.sem, 1)

                def up_part(n, e):
                    act.wait_ge(*w_used.at2(l, n))
                    if not isinstance(e, int):
                        act.wait_ge(*up_sum.at2(l, e))
                    part(bank_up, uxl, up_out)

                def result(n, half):
                    act.wait_ge(*w_used.at2(l, n))
                    act.activation(yx[:, half, :], (bank_gate, bank_y1)[half], ACT.Copy).then_inc(yx_ready.sem, 1)

                def gathered_experts():
                    high_tokens(1)
                    for i in range(4):
                        split(S2_MOE + i + 2)
                        if i == 1:
                            gate_part(S2_MOE + 2, 0)
                        if i == 2:
                            silu_x(0)
                        if i == 3:
                            up_part(S2_MOE + 4, 0)
                            high_tokens(2)
                    with act.Fori(1, NE) as e:
                        k = (e - 1) * 6
                        for i in range(6):
                            n = S2_MOE + 6 + i
                            split_at(n, e - 1, 4, COLS)
                            if i == 0:
                                take_turned(e)
                            if i == 1:
                                gate_part(k + (S2_MOE + 6), e)
                            if i == 2:
                                silu_x(e)
                            if i == 3:
                                up_part(k + (S2_MOE + 8), e)
                                high_tokens(e + 2)
                            if i >= 4:
                                result(k + (S2_MOE + 5 + i), i - 4)
                    take_turned(NE)
                    for half in range(2):
                        result(S2_LAYER - 1 + half, half)
                    act.sem_inc(ft_hi.sem, 2 * NE)
                    act.sem_inc(silu2_done.sem, NE)

                act.wait_ge(*flag_ready.at2(l, 1))
                act.sem_inc(loads, 1)
                dense = act.value_load(dense_i[0:1, 0:1], min_val=0, max_val=1)
                with act.If(dense == 0):
                    gathered_experts()
                with act.Else():
                    for i in range(4):
                        split(S2_MOE + i + 2)
                        if i == 1:
                            silu(0, S2_MOE + 2)
                    with act.Fori(1, NE) as e:
                        k = (e - 1) * 6
                        for i in range(6):
                            n = S2_MOE + 6 + i
                            split_at(n, e - 1, 4, COLS)
                            if i == 1:
                                f = (e - 1) * 2
                                for b in range(2):
                                    high(b, f + (X2_MOE + b), mt_hi[:, 2 * b:2 * b + 2, :])
                                silu(e, k + (S2_MOE + 6))
                    for b in range(2):
                        high(b, X2_LAYER - 2 + b, mt_hi[:, 2 * b:2 * b + 2, :])
                    for c, n in ((xg_high, NE + 1), (gate_out, NE), (silux, NE), (up_out, NE), (back_ready, NE), (ag_high, NE), (yx_ready, 2 * NE)):
                        act.sem_inc(c.sem, n)
                layer_norm_root(rv2_ready.at2(l, 4))

        @block.vector
        def _(dve):
            chain = [0]

            def link(ins, base=0):
                chain[0] += 1
                assert chain[0] < CHAIN
                ins.then_inc(v_chain, 1)
                dve.wait_ge(v_chain, base + chain[0])

            for slot_read in raw_read:
                dve.sem_inc(slot_read.sem, 1)
            for slot_read in more_read:
                dve.sem_inc(slot_read.sem, slot_read.prime)
            def ada(n, g, l, lk):
                vec, i = divmod(n, ADA)
                dve.wait_ge(*landed[g % RAW].at(l, 16 * (g // RAW + 1)))
                if i == 0:
                    dve.wait_ge(*acc_read.at(l, vec - 1))
                w, a = slot(raw, g % RAW, 2, D), acc[:, vec % 2, :]
                for k in range(2):
                    j = 2 * i + k
                    c = cact[:, j:j + 1]
                    if j == 0:
                        ins = dve.tensor_scalar(a, w[:, k, :], c, None, ALU.mult)
                    else:
                        ins = dve.scalar_tensor_tensor(out=a, in0=w[:, k, :], scalar=c, in1=a, op0=ALU.mult, op1=ALU.add)
                    if k == 0:
                        lk(ins)
                ins.then_inc(raw_read[g % RAW].sem, 1)
                dve.wait_ge(*raw_read[g % RAW].at(l, g // RAW + 1))
                if i == ADA - 1:
                    dve.sem_inc(acc_done.sem, 1)

            dve.sem_inc(x_final.sem, x_final.prime)
            dve.sem_inc(mod_taken.sem, mod_taken.prime)
            dve.sem_inc(ft_lo.sem, ft_lo.prime)
            dve.wait_ge(consts_in, 16 * 6)
            dve.wait_ge(positions_in, 16 * 2 * NT)
            link(dve.tensor_copy(posf[:, :, :], posi[:, :, :]))
            for t in range(NT):
                for i in range(2):
                    for which, a, b in ((0, 0, ROT // 2), (1, ROT // 2, NF)):
                        link(dve.tensor_scalar(ang[:, t, i, a:b], freq[:, a:b], posf[:, which, t:t + 1], None, ALU.mult))
            for i, quarter in enumerate((0.25, 0.0)):
                link(dve.tensor_scalar(angk[:, :, i, :], ang[:, :, i, :], float(1.0 / (2 * np.pi)), quarter, ALU.mult, ALU.add))
            nearest = 1.5 * 2.0 ** 23
            link(dve.tensor_scalar(angk[:, :, :, :], angk[:, :, :, :], nearest, None, ALU.add))
            link(dve.tensor_scalar(angk[:, :, :, :], angk[:, :, :, :], nearest, None, ALU.subtract))
            two_pi = 6.28125
            parts = [two_pi, float(np.round((2 * np.pi - two_pi) * 2.0 ** 22) / 2.0 ** 22)]
            parts.append(float(2 * np.pi - sum(parts)))
            for c in parts:
                for i in range(2):
                    link(dve.scalar_tensor_tensor(out=ang[:, :, i, :], in0=angk[:, :, i, :], scalar=-c, in1=ang[:, :, i, :],
                                                  op0=ALU.mult, op1=ALU.add))
            link(dve.tensor_scalar(ang[:, :, 0, :], ang[:, :, 0, :], float(np.pi / 2), None, ALU.add))
            dve.tensor_scalar(ang[:, :, :, :], ang[:, :, :, :], 3.1415925, -3.1415925, ALU.min, ALU.max).then_inc(ang_ready, 1)
            dve.wait_ge(rope_ready, 1)
            a = 0
            for c, sn in zip(cos2, sin2):
                h = c.shape[2] // 2
                for i in range(2):
                    link(dve.tensor_copy(c[:, :, h * i:h * (i + 1)], angk[:, :, 0, a:a + h]))
                link(dve.tensor_scalar(sn[:, :, 0:h], angk[:, :, 1, a:a + h], -1.0, None, ALU.mult))
                link(dve.tensor_copy(sn[:, :, h:2 * h], angk[:, :, 1, a:a + h]))
                a += h
            dve.wait_ge(params_t, LAYERS)
            for l in range(LAYERS):
                dve.tensor_copy(pcol[:, l, :], mp[:, l, 0:PC_ROWS]).then_inc(params_ready, 1)
            dve.wait_ge(csig_ready, 1)
            link(dve.tensor_tensor(cact[:, :], pcol[:, 0, PC_LAYER:PC_ROWS], csig[:, :], ALU.mult))
            for n in range(AHEAD):
                ada(n, n - AHEAD, 0, link)
            dve.wait_ge(params_in, PARAMS)
            dve.wait_ge(x_in, 16)
            dve.sem_inc(v_chain, CHAIN - chain[0])
            chain[0] = 0

            with dve.Fori(0, LAYERS) as l:
                def lk(ins):
                    link(ins, (l + 1) * CHAIN)

                def split(s):
                    g = G_OF["split", s]
                    _, units, cols = weights(("split", s), l)
                    dve.wait_ge(*hi_done.at(l, s + 1))
                    dve.tensor_tensor(slot(wlo, s % SPLIT, units, cols), slot(raw, g % RAW, units, cols),
                                      slot(whi, s % SPLIT, units, cols).bitcast(F32), ALU.subtract).then_inc(raw_read[g % RAW].sem, 1)
                    if s in AFTER:
                        ada(AFTER[s], G_OF["ada", AFTER[s]], l, lk)

                def take_mod(vec):
                    dve.wait_ge(*acc_read.at(l, vec + 1))
                    if vec in (2, 5):
                        i = vec // 3
                        dve.wait_ge(*grow_in.at(l, 32))
                        b = MOD_BANK[vec]
                        dve.tensor_tensor(grow[:, i, :], mp[:, b:b + 2, :].rearrange("p a n -> p (a n)"), grow[:, i, :], ALU.add).then_inc(mod_taken.sem, 1)
                    else:
                        bank = MOD_BANK[vec]
                        dve.tensor_tensor(modc[:, vec, :], mp[:, bank, 0:KD], pcur[:, KD * vec:KD * (vec + 1)], ALU.add).then_inc(mod_taken.sem, 1)

                def norm_columns(i, vec):
                    dve.wait_ge(*mod_taken.at(l, vec + 2))
                    at = (PC_N1, PC_N2)[i]
                    lk(dve.scalar_tensor_tensor(out=scol[:, i, :], in0=modc[:, vec + 1, :], scalar=1.0,
                                                in1=pcur[:, at:at + KD], op0=ALU.add, op1=ALU.mult))

                def rsqrt(i, n):
                    dve.wait_ge(*rs_ready.at(l, i + 1))
                    lk(dve.reciprocal(rr[:, 0:n], rs[:, 0:n]))
                    lk(dve.tensor_tensor(rt[:, 0:n], rr[:, 0:n], rr[:, 0:n], ALU.mult))
                    lk(dve.tensor_tensor(rt[:, 0:n], rt[:, 0:n], rv[:, 0:n], ALU.mult))
                    lk(dve.tensor_scalar(rt[:, 0:n], rt[:, 0:n], -0.5, 1.5, ALU.mult, ALU.add))
                    dve.tensor_tensor(rr[:, 0:n], rr[:, 0:n], rt[:, 0:n], ALU.mult).then_inc(rr_ready.sem, 1)

                def row_norm(i):
                    dve.wait_ge(*sq_done.at(l, 2 * i + 2))
                    dve.tensor_scalar(rv[:, 0:NT], ssq[:, :], 1.0 / D, EPS, ALU.mult, ALU.add).then_inc(rv_ready.sem, 1)
                    rsqrt(i, NT)

                def low(f, hi, lo):
                    dve.wait_ge(*ft_hi.at(l, f + 1))
                    dve.tensor_tensor(lo, chunks(ft[:, f % 2, :]), hi.bitcast(F32), ALU.subtract).then_inc(ft_lo.sem, 1)

                def ft_free(f):
                    dve.wait_ge(*ft_lo.at(l, f - 1))

                def bank_done(f):
                    dve.wait_ge(*tr_done.at(l, f + 1 - (f > X_CONV)))
                    ft_free(f)

                def lows(f0, n, dst, c0, bank0=0):
                    hi, lo = dst
                    for b in range(n):
                        c = c0 + 2 * b
                        dve.wait_ge(*ft_hi.at(l, f0 + b + 1))
                        dve.tensor_tensor(lo[:, c:c + 2, :], chunks(mp[:, bank0 + b, :]), hi[:, c:c + 2, :].bitcast(F32),
                                          ALU.subtract).then_inc(ft_lo.sem, 1)

                def spread(f0, n, dst, c0, copy, bank0=0):
                    hi, lo = dst
                    for b in range(n + 1):
                        if b < n:
                            copy(f0 + b, bank0 + b)
                        if b:
                            c = c0 + 2 * (b - 1)
                            low(f0 + b - 1, hi[:, c:c + 2, :], lo[:, c:c + 2, :])

                def normed(i, vec):
                    def copy(f, bank):
                        bank_done(f)
                        for k in range(2):
                            c = 2 * bank + k
                            ins = dve.tensor_scalar(ft[:, f % 2, T * k:T * (k + 1)], mp[:, bank, T * k:T * (k + 1)],
                                                    scol[:, i, c:c + 1], modc[:, vec, c:c + 1], ALU.mult, ALU.add)
                            if k == 0:
                                lk(ins)
                        ins.then_inc(ft_ready.sem, 1)
                    return copy

                def take_w_in(j):
                    dve.wait_ge(*w_used.at(l, JOB_END[j] + 1))
                    dve.tensor_copy(u[:, 1, COLS * j:COLS * (j + 1)], gp[:, j % 2, 1, :]).then_inc(pair_free[j % 2].sem, 1)

                def qk_norm_rope(stage):
                    qk = u[:, :, 0:2 * COLS].rearrange("p t (h d) -> p t h d", d=HD)
                    n = 2 * NT * HEADS
                    half = ROT // 2
                    t1 = w1[:, :, 0:T].rearrange("p a (h d) -> p a h d", d=ROT)
                    t2 = sc[:, :, 0:T].rearrange("p a (h d) -> p a h d", d=ROT)
                    if stage == 0:
                        dve.wait_ge(*sq_done.at(l, 4))
                        lk(dve.tensor_reduce(rt[:, 0:n].rearrange("p (t h) -> p t h", t=NT),
                                             gl[:, :, 0:D].rearrange("p t (h d) -> p t h d", d=HD), AX.X, ALU.add))
                        dve.tensor_scalar(rv[:, 0:n], rt[:, 0:n], 1.0 / HD, EPS, ALU.mult, ALU.add).then_inc(rv_ready.sem, 1)
                    if stage == 1:
                        rsqrt(1, n)
                        dve.wait_ge(*rr_ready.at(l, 2))
                        rb = rr[:, 0:n].rearrange("p (t h) -> p t h", t=NT).unsqueeze(3).broadcast_to((P, NT, 2 * HEADS, HD))
                        lk(dve.tensor_tensor(qk, qk, rb, ALU.mult))
                    if stage == 2:
                        for i in range(2):
                            part = u[:, :, COLS * i:COLS * (i + 1)].rearrange("p t (h d) -> p t h d", d=HD)
                            wb = qkcur[:, i, :].unsqueeze(1).unsqueeze(1).broadcast_to((P, NT, HEADS, HD))
                            lk(dve.tensor_tensor(part, part, wb, ALU.mult))
                    if stage == 3:
                        cb = cos2[0][:, :, :].unsqueeze(2).broadcast_to((P, NT, 2 * HEADS, ROT))
                        lk(dve.tensor_tensor(t1, qk[:, :, :, 0:ROT], cb, ALU.mult))
                        for i in range(2):
                            sb_ = sin2[0][:, :, half * i:half * (i + 1)].unsqueeze(2).broadcast_to((P, NT, 2 * HEADS, half))
                            lk(dve.tensor_tensor(t2[:, :, :, half * i:half * (i + 1)], qk[:, :, :, half * (1 - i):half * (2 - i)], sb_, ALU.mult))
                        dve.tensor_tensor(qk[:, :, :, 0:ROT], t1, t2, ALU.add).then_inc(qk_ready.sem, 1)

                def pool_windows():
                    e = PAD + T
                    dve.wait_ge(*pct_taken.at(l, 1))
                    dve.memset(pp[:, :, 0:PAD], 0.0).then_inc(pads_zero.sem, 1)
                    dve.memset(zp[:, :, 0:PAD], 0.0).then_inc(pads_zero.sem, 1)
                    dve.wait_ge(*pads_zero.at(l, 2))
                    lk(dve.tensor_tensor(w1[:, :, 1:e], pp[:, :, 1:e], pp[:, :, 0:e - 1], ALU.add))
                    lk(dve.tensor_tensor(w2[:, :, 3:e], w1[:, :, 3:e], w1[:, :, 1:e - 2], ALU.add))
                    lk(dve.tensor_tensor(w1[:, 1, 7:e], w2[:, 1, 7:e], w2[:, 1, 3:e - 4], ALU.add))
                    lk(dve.tensor_tensor(w2[:, 1, PAD:e], w1[:, 1, PAD:e], w1[:, 1, PAD - 8:e - 8], ALU.add))
                    for half, w in ((0, w1), (64, w2)):
                        r = slice(half, half + 64)
                        lk(dve.tensor_tensor(w[r, :, PAD:e], w[r, :, PAD:e], count[r, :, :], ALU.mult))
                        ins = dve.tensor_tensor(w1[r, :, PAD:e], w[r, :, PAD:e], pp[r, :, PAD:e], ALU.subtract)
                        if half == 0:
                            lk(ins)
                    ins.then_inc(pooled.sem, 1)

                conv_y = ft[:, X_CONV % 2, :].rearrange("p (a t) -> p a t", a=2)

                def short_conv():
                    dve.wait_ge(*pct_taken.at(l, 3))
                    ft_free(X_CONV)
                    y = conv_y
                    for a in range(2):
                        for k in (2, 1, 0):
                            w = pcur[:, PC_CW + 2 * k + a:PC_CW + 2 * k + a + 1]
                            z = zp[:, a, PAD - 2 + k:PAD - 2 + k + T]
                            if k == 2:
                                lk(dve.tensor_scalar(y[:, a, :], z, w, None, ALU.mult))
                            else:
                                lk(dve.scalar_tensor_tensor(out=y[:, a, :], in0=z, scalar=w, in1=y[:, a, :], op0=ALU.mult, op1=ALU.add))

                def soft_max(h):
                    dve.wait_ge(*s_done.at(l, h + 1))
                    lk(dve.scalar_tensor_tensor(out=sc[:, h % 2, :], in0=mp[:, h % 2, 0:3 * P], scalar=HD ** -0.5,
                                                in1=mask[:, :], op0=ALU.mult, op1=ALU.add))
                    dve.tensor_reduce(nmax[:, h % 2, 0:1], sc[:, h % 2, 0:P], AX.X, ALU.max, negate=True)
                    dve.tensor_reduce(nmax[:, h % 2, 1:2], sc[:, h % 2, P:3 * P], AX.X, ALU.max, negate=True).then_inc(s_max.sem, 1)

                def take_o(h):
                    dve.wait_ge(*e_done.at(l, 2 * h + 2))
                    lk(dve.reciprocal(rinv[:, h % 2, :], rsum[:, h % 2, :]))
                    dve.wait_ge(*o_done.at(l, h + 1))
                    for t in range(NT):
                        ins = dve.tensor_scalar(o[:, t, HD * h:HD * (h + 1)], mp[:, 3, HD * t:HD * (t + 1)],
                                                rinv[:, h % 2, t:t + 1], None, ALU.mult)
                        if t == 0:
                            lk(ins)
                    ins.then_inc(o_taken.sem, 1)

                def merge(b, n):
                    q = J_BR + 2 * b + n
                    dve.wait_ge(*w_used.at(l, JOB_END[q] + 1))
                    dve.wait_ge(*gates_ready.at(l, 2 * b + n + 1))
                    gate = gl[:, :, COLS * (2 * b + n):COLS * (2 * b + n + 1)]
                    m = merged[:, :, COLS * n:COLS * (n + 1)]
                    dve.tensor_tensor(m if b == 0 else gate, gp[:, q % 2, :, :], gate, ALU.mult).then_inc(pair_free[q % 2].sem, 2)
                    dve.wait_ge(*pair_free[q % 2].at(l, 2 * (q // 2) + 2))
                    if b == 1:
                        lk(dve.tensor_tensor(m, m, gate, ALU.add))
                    if b == 2:
                        dve.tensor_tensor(m, m, gate, ALU.add).then_inc(merged_ready.sem, 1)

                def residual(q, n, i, tmp):
                    dve.wait_ge(*w_used.at(l, JOB_END[q] + 1))
                    gb = grow[:, i, COLS * n:COLS * (n + 1)].unsqueeze(1).broadcast_to((P, NT, COLS))
                    dve.tensor_tensor(tmp, gp[:, q % 2, :, :], gb, ALU.mult).then_inc(pair_free[q % 2].sem, 2)
                    dve.wait_ge(*pair_free[q % 2].at(l, 2 * (q // 2) + 2))
                    xs = x[:, :, COLS * n:COLS * (n + 1)]
                    dve.tensor_tensor(xs, xs, tmp, ALU.add).then_inc(x_final.sem, 1)

                lk(dve.tensor_copy(pcur[:, :], pcol[:, bass.ds(l, 1), 0:PC_LAYER].rearrange("p a n -> p (a n)")))
                lk(dve.tensor_copy(qkcur[:, :, :].rearrange("p a n -> p (a n)"), qkw[:, bass.ds(l, 1), :, :].rearrange("p a b n -> p (a b n)")))
                lk(dve.tensor_copy(poolcur[:, :, :].rearrange("p a n -> p (a n)"), poolw[:, bass.ds(l, 1), :, :].rearrange("p a b n -> p (a b n)")))
                row_norm(0)
                take_mod(0)
                take_mod(1)
                norm_columns(0, 0)
                split(0)
                split(1)
                spread(X_NORM1, 4, (xt_hi, xt_lo), 0, normed(0, 0))
                for s in range(10):
                    split(s + 2)
                    if s % 2:
                        take_w_in(s // 2)
                    if 5 <= s < 9:
                        qk_norm_rope(s - 5)
                    if s == 7:
                        take_mod(2)
                dve.wait_ge(*pair_free[0].at(l, 6))
                cu = u[:, :, 3 * COLS + 256:4 * COLS]
                dve.tensor_tensor(cu, cu, u[:, :, 4 * COLS + 256:5 * COLS], ALU.mult).then_inc(cu_ready.sem, 1)
                for i in range(12):
                    split(10 + i + 2)
                    if i == 0:
                        take_mod(3)
                    if 0 <= i - 4 < HEADS:
                        take_o(i - 4)
                    if 0 <= i - 2 < HEADS:
                        soft_max(i - 2)
                    if i == 5:
                        pool_windows()
                    if i == 7:
                        short_conv()
                take_mod(4)
                norm_columns(1, 3)

                def pool_scaled(f, bank):
                    bank_done(f)
                    for k in range(2):
                        ins = dve.tensor_scalar(ft[:, f % 2, T * k:T * (k + 1)], mp[:, bank, T * k:T * (k + 1)],
                                                pcur[:, PC_PS + k:PC_PS + k + 1], None, ALU.mult)
                        if k == 0:
                            lk(ins)
                    ins.then_inc(ft_ready.sem, 1)

                spread(X_POOL, 1, (bt_hi, bt_lo), 0, pool_scaled, 1)
                dve.tensor_tensor(conv_y, conv_y, bg[:, :, :], ALU.mult).then_inc(ft_ready.sem, 1)
                low(X_CONV, bt_hi[:, 2:4, :], bt_lo[:, 2:4, :])
                lows(X_ATT, 2, (bt_hi, bt_lo), 4, 2)
                for s in range(S_BR, S_OUT):
                    split(s + 2)
                    for q, _, _, _, _, _, _ in group_jobs(s):
                        merge((q - J_BR) // 2, (q - J_BR) % 2)
                lows(X_MERGE, 4, (xt_hi, xt_lo), 0)
                for s in range(S_OUT, S_FF):
                    split(s + 2)
                    if s % 2 == (S_OUT + 1) % 2:
                        n = (s - S_OUT) // 2
                        residual(J_OUT + n, n, 0, gl[:, :, COLS * n:COLS * (n + 1)])
                row_norm(2)
                spread(X_NORM2, 4, (xt_hi, xt_lo), 0, normed(1, 3))
                for s in range(S_FF, S_DOWN):
                    split(s + 2)
                    j, r = divmod(s - S_FF, 4)
                    wide = min(COLS, FF - COLS * j)
                    if s == S_FF + 5:
                        take_mod(5)
                    if r == 2 and j >= 1:
                        lows(X_ACT + 2 * (j - 1), 2, (at_hi, at_lo), 4 * (j - 1), 2 * ((j - 1) % 2))
                    if r == 3:
                        q = J_FF + 2 * j + 1
                        dve.wait_ge(*w_used.at(l, JOB_END[q] + 1))
                        dve.wait_ge(*silu_done.at(l, j + 1))
                        dve.tensor_tensor(ab[:, :, 0:wide], gp[:, q % 2, :, 0:wide], sg[:, :, 0:wide], ALU.mult).then_inc(ab_ready.sem, 1)
                        dve.wait_ge(*ab_ready.at(l, j + 1))
                        dve.sem_inc(pair_free[q % 2].sem, 2)
                        dve.sem_inc(pair_free[1 - q % 2].sem, 2)
                for s in range(S_DOWN, S_LAYER - 2):
                    split(s + 2)
                    if s == S_DOWN + 1:
                        lows(X_ACT + 2 * (FF_BLOCKS - 1), 1, (at_hi, at_lo), FF_CHUNKS - 2, 2)
                for n in range(2):
                    residual(J_DOWN + n, n, 1, (sg, ab)[n][:, :, :])
                dve.wait_ge(*x_final.at(l, 4))
                dve.sem_inc(v_chain, CHAIN - chain[0])
            chain[0] = 0

            base2 = (LAYERS + 1) * CHAIN

            def reciprocal_root(n, wait, lk):
                dve.wait_ge(*wait)
                lk(dve.reciprocal(rr[:, 0:n], rs[:, 0:n]))
                lk(dve.tensor_tensor(rt[:, 0:n], rr[:, 0:n], rr[:, 0:n], ALU.mult))
                lk(dve.tensor_tensor(rt[:, 0:n], rt[:, 0:n], rv[:, 0:n], ALU.mult))
                lk(dve.tensor_scalar(rt[:, 0:n], rt[:, 0:n], -0.5, 1.5, ALU.mult, ALU.add))
                lk(dve.tensor_tensor(rr[:, 0:n], rr[:, 0:n], rt[:, 0:n], ALU.mult))

            def layer_norm(src, roots, rows, lk):
                for t in range(NT):
                    for h in range(2):
                        ins = dve.bn_stats(stats[:, t, 6 * h:6 * h + 6], src[:, t, COLS * h:COLS * (h + 1)])
                lk(ins)
                dve.sem_inc(loads, 1)
                for t in range(NT):
                    ins = dve.bn_aggr(mean[:, t, :], stats[:, t, :])
                lk(ins)
                dve.tensor_scalar(rv[:, 0:NT], mean[:, :, 1:2].rearrange("p t a -> p (t a)"), LN_EPS, None, ALU.add).then_inc(rv2_ready.sem, 1)
                dve.wait_ge(*rows)
                for t in range(NT):
                    ins = dve.scalar_tensor_tensor(out=cen[:, t, :], in0=src[:, t, :], scalar=mean[:, t, 0:1], in1=lnw[:, 0, :],
                                                   op0=ALU.subtract, op1=ALU.mult)
                lk(ins)
                reciprocal_root(NT, roots, lk)
                for t in range(NT):
                    dve.scalar_tensor_tensor(out=x[:, t, :], in0=cen[:, t, :], scalar=rr[:, t:t + 1], in1=lnw[:, 1, :],
                                             op0=ALU.mult, op1=ALU.add).then_inc(h_ready.sem, 1)

            def lk0(ins):
                link(ins, base2)

            layer_norm(x, (rs2_ready.sem, 1), (lnw_in.sem, 32), lk0)
            dve.sem_inc(v_chain, CHAIN2 - chain[0])
            chain[0] = 0

            with dve.Fori(0, LAYERS) as l:
                def lk(ins):
                    link(ins, l * CHAIN2 + (base2 + CHAIN2))

                def split_at(n, turn, units, cols):
                    buf, _, read, _ = ring2(n)
                    dve.wait_ge(*hi_done.at2(l, turn * 6 + (n + 1)))
                    dve.tensor_tensor(slot(wlo, n % SPLIT, units, cols), slot(buf, n % RAW, units, cols),
                                      slot(whi, n % SPLIT, units, cols).bitcast(F32), ALU.subtract).then_inc(read.sem, 1)

                def split(s):
                    units, cols = weights2(s, l)[1:] if s < S2_MOE else (4, COLS)
                    split_at(s, 0, units, cols)

                def spread(f0, units, dst):
                    hi, lo = dst
                    for b, n in enumerate(units):
                        c = 2 * b
                        dve.wait_ge(*ft_hi.at2(l, f0 + (b + 1)))
                        dve.tensor_tensor(lo[:, c:c + n, :], mp[:, b, 0:T * n].rearrange("p (k t) -> p k t", k=n),
                                          hi[:, c:c + n, :].bitcast(F32), ALU.subtract).then_inc(ft_lo.sem, 1)

                def take(q, t, dst, src=None):
                    dve.wait_ge(*w_used.at2(l, job2_end(q) + 1))
                    src = gp[:, q % 2, t, 0:dst.shape[-1]] if src is None else src
                    dve.tensor_copy(dst, src).then_inc(pair_free[q % 2].sem, 1)

                def rotate(v, r, heads, rot):
                    h = rot // 2
                    n = NT * heads * rot
                    t1 = rt1[:, 0:n].rearrange("p (t h d) -> p t h d", t=NT, d=rot)
                    t2 = rt2[:, 0:n].rearrange("p (t h d) -> p t h d", t=NT, d=rot)
                    lk(dve.tensor_tensor(t1, v, cos2[r][:, :, :].unsqueeze(2).broadcast_to((P, NT, heads, rot)), ALU.mult))
                    for i in range(2):
                        sn = sin2[r][:, :, h * i:h * (i + 1)].unsqueeze(2).broadcast_to((P, NT, heads, h))
                        lk(dve.tensor_tensor(t2[:, :, :, h * i:h * (i + 1)], v[:, :, :, h * (1 - i):h * (2 - i)], sn, ALU.mult))
                    lk(dve.tensor_tensor(v, t1, t2, ALU.add))

                split(0)
                split(1)
                spread(X2_IN, (2, 2, 2, 2), (xt_hi, xt_lo))
                for s in range(S2_UQ):
                    split(s + 2)
                    if s % 2:
                        j = s // 2
                        take(j, 1, pr[:, 1, COLS * j:min(COLS * (j + 1), IN2)])
                    if s == 1:
                        dve.wait_ge(params2_in, PARAMS2)
                        lk(dve.tensor_copy(cgc[:, :], cg[:, bass.ds(l, 1), :].rearrange("p a n -> p (a n)")))
                        lk(dve.tensor_scalar(subc[:, :], subg[:, bass.ds(l, 1), :].rearrange("p a n -> p (a n)"),
                                             lamc[:, bass.ds(l, 1), 1:2].rearrange("p a n -> p (a n)"), None, ALU.mult))
                        lr = lamr[:, bass.ds(l, 1), :, :].rearrange("p a b n -> p (a b) n")
                        lk(dve.tensor_copy(lamq[:, :, :], lr))
                        lk(dve.tensor_tensor(lamt[:, :, :], lamq[:, 0:2, :], lamq[:, 2:4, :], ALU.mult))
                        dve.tensor_reduce(lame[:, :], lamt[:, :, :], AX.X, ALU.add).then_inc(lam_sum.sem, 1)
                        lk(dve.tensor_copy(lami[:, :], lamc[:, bass.ds(l, 1), 0:1].rearrange("p a n -> p (a n)")))
                        lk(dve.tensor_copy(fbc[:, :], fbias[:, bass.ds(l, 1), :].rearrange("p a n -> p (a n)")))
                        dve.wait_ge(*rw_high.at2(l, 1))
                        dve.tensor_tensor(rw2[:, :, 1, :], rw[:, :, :], rw2[:, :, 0, :].bitcast(F32), ALU.subtract).then_inc(rw_ready.sem, 1)
                    if s == 3:
                        dve.wait_ge(*mla_sq.at2(l, 4))
                        lk(dve.tensor_scalar(rv[:, 0:2], lsum4[:, 0:2], 1.0 / CQ, EPS, ALU.mult, ALU.add))
                        dve.tensor_scalar(rv[:, 2:4], lsum4[:, 2:4], 1.0 / CKV, EPS, ALU.mult, ALU.add).then_inc(rv2_ready.sem, 1)
                        reciprocal_root(4, rs2_ready.at2(l, 1), lk)
                        for t in range(NT):
                            for i, (a, b) in enumerate(((0, CQ), (CQ, CQ + CKV))):
                                lk(dve.scalar_tensor_tensor(out=pr[:, t, a:b], in0=pr[:, t, a:b], scalar=rr[:, 2 * i + t:2 * i + t + 1],
                                                            in1=cgc[:, a:b], op0=ALU.mult, op1=ALU.mult))
                        dve.sem_inc(mla_ready.sem, 1)
                dve.wait_ge(*pair_free[0].at2(l, 6))
                dve.wait_ge(*pair_free[1].at2(l, 4))
                lk(dve.tensor_tensor(fz[:, :, :], pr[:, :, C_FF:C_FF + FH], fbc[:, :].unsqueeze(1).broadcast_to((P, NT, FH)), ALU.add))
                lk(dve.tensor_scalar(fe[:, :, :], fz[:, :, :], -1.0, None, ALU.mult))
                dve.tensor_tensor(fe[:, :, :], fz[:, :, :], fe[:, :, :], ALU.min).then_inc(fz_ready.sem, 1)
                spread(X2_MLA, (2, 2, 1), (mt_hi, mt_lo))
                dve.wait_ge(*lam_exp.at2(l, 1))
                lk(dve.tensor_tensor(nlam[:, :], lame[:, 1:2], lame[:, 0:1], ALU.subtract))
                lk(dve.tensor_tensor(nlam[:, :], nlam[:, :], lami[:, :], ALU.subtract))
                dve.wait_ge(*fl_ready.at2(l, 1))
                lk(dve.tensor_scalar(fz[:, :, :], fz[:, :, :], 0.0, None, ALU.min))
                dve.tensor_tensor(fz[:, :, :], fz[:, :, :], fl[:, :, :], ALU.subtract).then_inc(logf_ready.sem, 1)
                for s in range(S2_UQ, S2_OUT):
                    split(s + 2)
                    q = J2_UQ + s - S2_UQ
                    h = 4 * ((s - S2_UQ) % 2)
                    if s < S2_UKV:
                        take(q, 1, qm[:, 1, h:h + 4, :].rearrange("p h d -> p (h d)"))
                    else:
                        for t in range(NT):
                            kv = gp[:, q % 2, t, :].rearrange("p (h d) -> p h d", h=4)
                            dve.wait_ge(*w_used.at2(l, job2_end(q) + 1))
                            lk(dve.tensor_copy(km[:, t, h:h + 4, 0:MN], kv[:, :, 0:MN]))
                            dve.tensor_copy(vm[:, t, h:h + 4, :], kv[:, :, MN:MN + HD]).then_inc(pair_free[q % 2].sem, 1)
                dve.wait_ge(*pair_free[0].at2(l, 8))
                dve.wait_ge(*pair_free[1].at2(l, 6))
                rotate(qm[:, :, :, MN:MQ], 1, MH, KR)
                kr = pr[:, :, C_KR:C_KR + KR].unsqueeze(2)
                rotate(kr, 1, 1, KR)
                lk(dve.tensor_copy(km[:, :, :, MN:MQ], kr.broadcast_to((P, NT, MH, KR))))
                dve.sem_inc(km_ready.sem, 1)
                for c in (C_DQ, C_DK):
                    rotate(pr[:, :, c:c + 2 * DH * DW].rearrange("p t (h d) -> p t h d", d=DW)[:, :, :, 0:DROT], 2, 2 * DH, DROT)
                dve.sem_inc(diff_ready.sem, 1)
                up = HD ** 0.5
                for dst, c in ((fq, C_FQ), (fk, C_FK)):
                    lk(dve.tensor_copy(dst[:, :, :, 0:HD], pr[:, :, c:c + FH * HD].rearrange("p t (h d) -> p t h d", d=HD)))
                lk(dve.memset(fq[:, :, :, HD + 1:HD + 2], 1.0))
                lk(dve.memset(fk[:, :, :, HD:HD + 1], 1.0))
                dve.wait_ge(*cum_done.at2(l, 1))
                cum = mp[:, 3, 0:NT * FH].rearrange("p (t h) -> p t h", t=NT)
                lk(dve.tensor_scalar(fq[:, :, :, HD:HD + 1].rearrange("p t h a -> p t (h a)"), cum, up, None, ALU.mult))
                dve.tensor_scalar(fk[:, :, :, HD + 1:HD + 2].rearrange("p t h a -> p t (h a)"), cum, -up, None, ALU.mult).then_inc(fox_ready.sem, 1)
                for i in range(AJ + 4):
                    j = i - 1
                    if 0 <= j < AJ:
                        scale, m = job_operands(j)[3:]
                        dve.wait_ge(*s2_done.at2(l, j + 1))
                        if j >= 3:
                            dve.wait_ge(*p2_done.at2(l, j - 2))
                        lk(dve.scalar_tensor_tensor(out=sc2[:, j % 3, :], in0=mp[:, 1, 0:3 * P], scalar=scale,
                                                    in1=m[:, :], op0=ALU.mult, op1=ALU.add))
                        dve.tensor_reduce(nmax2[:, j % 3, 0:1], sc2[:, j % 3, 0:P], AX.X, ALU.max, negate=True)
                        dve.tensor_reduce(nmax2[:, j % 3, 1:2], sc2[:, j % 3, P:3 * P], AX.X, ALU.max, negate=True).then_inc(s2_max.sem, 1)
                    j = i - 4
                    if 0 <= j < AJ:
                        dve.wait_ge(*e2_done.at2(l, 2 * j + 2))
                        lk(dve.reciprocal(rinv2[:, j % 3, :], rsum2[:, j % 3, :]))
                        dve.wait_ge(*o2_done.at2(l, j + 1))
                        for t in range(NT):
                            if j < MH:
                                dst = oa[:, t, HD * j:HD * (j + 1)]
                            elif j < MH + 2 * DH:
                                m, h = (j - MH) % 2, (j - MH) // 2
                                dst = od[:, t, HD * h:HD * (h + 1)] if m else oa[:, t, HD * (MH + h):HD * (MH + h + 1)]
                            else:
                                dst = oa[:, t, HD * (j - DH):HD * (j - DH + 1)]
                            ins = dve.tensor_scalar(dst, mp[:, 3, HD * t:HD * (t + 1)], rinv2[:, j % 3, t:t + 1], None, ALU.mult)
                            if t == 0:
                                lk(ins)
                        ins.then_inc(o2_taken.sem, 1)
                dve.wait_ge(*o2_taken.at2(l, AJ))
                d1 = oa[:, :, HD * MH:HD * (MH + DH)]
                lk(dve.scalar_tensor_tensor(out=d1, in0=od[:, :, :], scalar=nlam[:, :], in1=d1, op0=ALU.mult, op1=ALU.add))
                lk(dve.tensor_tensor(od[:, :, :], d1, d1, ALU.mult))
                n = NT * DH
                lk(dve.tensor_reduce(rt[:, 0:n].rearrange("p (t h) -> p t h", t=NT), od[:, :, :].rearrange("p t (h d) -> p t h d", d=HD), AX.X, ALU.add))
                dve.tensor_scalar(rv[:, 0:n], rt[:, 0:n], 1.0 / HD, EPS, ALU.mult, ALU.add).then_inc(rv2_ready.sem, 1)
                reciprocal_root(n, rs2_ready.at2(l, 2), lk)
                d1h = d1.rearrange("p t (h d) -> p t h d", d=HD)
                lk(dve.tensor_tensor(d1h, d1h, rr[:, 0:n].rearrange("p (t h) -> p t h", t=NT).unsqueeze(3).broadcast_to((P, NT, DH, HD)), ALU.mult))
                dve.tensor_tensor(d1h, d1h, subc[:, :].unsqueeze(1).unsqueeze(1).broadcast_to((P, NT, DH, HD)), ALU.mult).then_inc(oa_ready.sem, 1)
                spread(X2_O, (2, 2, 2, 2), (xt_hi, xt_lo))
                for s in range(S2_OUT, S2_MOE):
                    split(s + 2)
                    if s % 2 == (S2_OUT + 1) % 2:
                        n = (s - S2_OUT) // 2
                        q = J2_OUT + n
                        dve.wait_ge(*w_used.at2(l, job2_end(q) + 1))
                        xs = x[:, :, COLS * n:COLS * (n + 1)]
                        dve.scalar_tensor_tensor(out=xs, in0=xs, scalar=ALPHA, in1=gp[:, q % 2, :, :], op0=ALU.mult, op1=ALU.add).then_inc(x2_sum.sem, 1)
                        dve.wait_ge(*x2_sum.at2(l, n + 1))
                        dve.sem_inc(pair_free[q % 2].sem, 2)
                layer_norm(x, rs2_ready.at2(l, 3), lnw_in.at2(l, 32), lk)
                spread(X2_H, (2, 2, 2, 2), (xt_hi, xt_lo))
                dve.wait_ge(*h_ready.at2(l, 2))

                def beats(dst, v):
                    d = cmp1[:, 0:v.shape[1], :].rearrange("p g (i j) -> p g i j", i=4)
                    e_ = cmp2[:, 0:v.shape[1], :].rearrange("p g (i j) -> p g i j", i=4)
                    shape = (P, v.shape[1], 4, 4)
                    vi, vj = v.unsqueeze(3).broadcast_to(shape), v.unsqueeze(2).broadcast_to(shape)
                    lk(dve.tensor_tensor(d, vj, vi, ALU.is_ge))
                    lk(dve.tensor_tensor(e_, vj, vi, ALU.is_gt))
                    for a, c in ((cmp1, 0), (cmp2, 1)):
                        w = a[:, 0:v.shape[1], :]
                        lk(dve.tensor_tensor(w, w, order[:, c, :].unsqueeze(1).broadcast_to((P, v.shape[1], 16)), ALU.mult))
                    lk(dve.tensor_tensor(d, d, e_, ALU.add))
                    lk(dve.tensor_reduce(dst, d, AX.X, ALU.add))

                dve.memset(back, 0.0).then_inc(y_zero.sem, 1)
                dve.memset(yx, 0.0).then_inc(y_zero.sem, 1)
                dve.wait_ge(*logits_done.at2(l, 1))
                parts = small[:, 0:2 * NE * NT].rearrange("p (t a n) -> p t a n", t=NT, a=2)
                lk(dve.tensor_copy(rb[:, :, :], parts[:, :, 1, :]))
                dve.tensor_tensor(rsc[:, :, :], parts[:, :, 0, :], rb[:, :, :], ALU.add).then_inc(logit_sum.sem, 1)
                dve.wait_ge(*rsc_ready.at2(l, 1))
                lk(dve.tensor_tensor(rb[:, :, :], rsc[:, :, :], rbias[:, :].unsqueeze(1).broadcast_to((P, NT, NE)), ALU.add))
                four = rb[:, :, :].rearrange("p t (g i) -> p (t g) i", i=4)
                beats(rank[:, :, :], four)
                lk(dve.tensor_scalar(rank[:, :, :], rank[:, :, :], 2.0, None, ALU.is_lt))
                lk(dve.tensor_tensor(cmp1[:, :, 0:4], four, rank[:, :, :], ALU.mult))
                lk(dve.tensor_reduce(gs[:, :], cmp1[:, :, 0:4], AX.X, ALU.add))
                beats(gr[:, :].rearrange("p (t g) -> p t g", t=NT), gs[:, :].rearrange("p (t g) -> p t g", t=NT))
                lk(dve.tensor_scalar(gr[:, :], gr[:, :], 1.0, None, ALU.is_lt))
                lk(dve.tensor_tensor(rank[:, :, :], rank[:, :, :], gr[:, :].unsqueeze(2).broadcast_to((P, 8, 4)), ALU.mult))
                dve.sem_inc(chosen.sem, 1)
                lk(dve.tensor_tensor(dg[:, :, :], rsc[:, :, :], rank[:, :, :].rearrange("p (t g) i -> p t (g i)", t=NT), ALU.mult))
                lk(dve.tensor_reduce(den[:, :], dg[:, :, :], AX.X, ALU.add))
                lk(dve.reciprocal(den[:, :], den[:, :]))
                for t in range(NT):
                    lk(dve.tensor_scalar(dg[:, t, :], dg[:, t, :], den[:, t:t + 1], None, ALU.mult))

                dve.wait_ge(*chosen_sum.at2(l, 1))
                lk(dve.memset(key[:, :, NE:NE + 1], 0.0))
                lk(dve.tensor_tensor(key[:, :, 0:NE], small[:, 0:NT * NE].rearrange("p (t n) -> p t n", t=NT),
                                     rank[:, :, :].rearrange("p (t g) i -> p t (g i)", t=NT), ALU.mult))
                lk(dve.tensor_reduce(many[:, :], small[:, NT * NE:(NT + 1) * NE], AX.X, ALU.max))
                lk(dve.tensor_scalar(many[:, :], many[:, :], float(CAP), None, ALU.is_gt))
                dve.tensor_copy(dense_i[:, :], many[:, :]).then_inc(flag_ready.sem, 1)

                def gated(e, k):
                    dve.wait_ge(*w_used.at2(l, k))
                    dve.wait_ge(*silu2_done.at2(l, e + 1))
                    for t in range(NT):
                        ins = dve.scalar_tensor_tensor(out=ab2[:, t, :], in0=gp[:, 1 - GATE_PAIR, t, :], scalar=dg[:, t, bass.ds(e, 1)],
                                                       in1=sg2[:, t, :], op0=ALU.mult, op1=ALU.mult)
                        if t == 0:
                            ins.then_inc(v_moe, 1)
                            dve.wait_ge(v_moe, l * NE + (e + 1))
                    ins.then_inc(ab2_ready.sem, 1)
                    dve.wait_ge(*ab2_ready.at2(l, e + 1))
                    for p in range(2):
                        dve.sem_inc(pair_free[p].sem, 2)

                def add_y(n, yk, k):
                    p = GATE_PAIR if n == 0 else 1 - GATE_PAIR
                    dve.wait_ge(*w_used.at2(l, k))
                    ys = cen[:, :, COLS * n:COLS * (n + 1)]
                    dve.tensor_tensor(ys, ys, gp[:, p, :, :], ALU.add).then_inc(y_taken.sem, 1)
                    dve.wait_ge(*y_taken.at2(l, yk))
                    dve.sem_inc(pair_free[p].sem, 2)

                def select(k, e):
                    if k is not None:
                        dve.wait_ge(*gathered.at2(l, k))
                    for t in range(NT):
                        ins = dve.tensor_scalar(pick[:, t, :], slots[:, 0:CAP], key[:, t, bass.ds(e, 1)], None, ALU.is_equal)
                        if t == 1:
                            ins.then_inc(pick_ready.sem, 1)

                def select_gates(k, e):
                    if k is not None:
                        dve.wait_ge(*ax_turned.at2(l, k))
                    for t in range(NT):
                        ins = dve.tensor_scalar(place[:, t, :], slots[:, :], key[:, t, bass.ds(e, 1)], dg[:, t, bass.ds(e, 1)],
                                                ALU.is_equal, ALU.mult)
                        if t == 1:
                            ins.then_inc(place_ready.sem, 1)

                def low_tokens(k):
                    dve.wait_ge(*xg_high.at2(l, k))
                    dve.tensor_tensor(xg[:, :, CAP:2 * CAP], bank_tr.rearrange("p (c s) -> p c s", c=KD), xg[:, :, 0:CAP].bitcast(F32),
                                      ALU.subtract).then_inc(xg_low.sem, 1)

                def gate_whole(e):
                    dve.wait_ge(*gate_out.at2(l, e + 1))
                    dve.tensor_tensor(gx, bank_gate[0:CAP, :], gxl, ALU.add).then_inc(gate_sum.sem, 1)

                def gate_up(e):
                    dve.wait_ge(*up_out.at2(l, e + 1))
                    dve.tensor_tensor(ux, bank_up[0:CAP, :], uxl, ALU.add).then_inc(up_sum.sem, 1)
                    dve.wait_ge(*up_sum.at2(l, e + 1))
                    dve.wait_ge(*silux.at2(l, e + 1))
                    dve.tensor_tensor(ax, gx.rearrange("p (a n) -> p a n", a=2), ux.rearrange("p (a n) -> p a n", a=2), ALU.mult).then_inc(ax_ready.sem, 1)
                    dve.wait_ge(*ax_ready.at2(l, e + 1))

                def low_turned(k):
                    dve.wait_ge(*ag_high.at2(l, k))
                    dve.tensor_tensor(ag[:, :, CAP:2 * CAP], bank_tr[:, 0:T].rearrange("p (c s) -> p c s", c=4), ag[:, :, 0:CAP].bitcast(F32),
                                      ALU.subtract).then_inc(ag_low.sem, 1)

                def gathered_experts():
                    select(None, 0)
                    low_tokens(1)
                    for i in range(4):
                        split(S2_MOE + i + 2)
                        if i == 0:
                            select(1, 1)
                            select_gates(None, 0)
                        if i == 1:
                            gate_whole(0)
                        if i == 3:
                            gate_up(0)
                            low_tokens(2)
                    with dve.Fori(1, NE) as e:
                        for i in range(6):
                            n = S2_MOE + 6 + i
                            split_at(n, e - 1, 4, COLS)
                            if i == 0:
                                select(e + 1, e + 1)
                                low_turned(e)
                                select_gates(e, e)
                            if i == 1:
                                gate_whole(e)
                            if i == 3:
                                gate_up(e)
                                low_tokens(e + 2)
                    low_turned(NE)
                    dve.wait_ge(*y_done.at2(l, 1))
                    for t in range(NT):
                        dve.scalar_tensor_tensor(out=cen[:, t, :], in0=x[:, t, :], scalar=ALPHA,
                                                 in1=mp[:, 2 * t:2 * t + 2, :].rearrange("p a n -> p (a n)"), op0=ALU.mult, op1=ALU.add).then_inc(y_taken.sem, NE)
                    dve.wait_ge(*y_taken.at2(l, 2 * NE))
                    for c, n in ((ft_lo, 2 * NE), (ab2_ready, NE), (pair_free[0], 4 * NE), (pair_free[1], 4 * NE)):
                        dve.sem_inc(c.sem, n)
                    dve.sem_inc(v_moe, NE)
                    dve.sem_inc(flag_seen, 1)

                dve.wait_ge(*flag_ready.at2(l, 1))
                dve.sem_inc(loads, 1)
                dense = dve.value_load(dense_i[0:1, 0:1], min_val=0, max_val=1)
                with dve.If(dense == 0):
                    gathered_experts()
                with dve.Else():
                    dve.tensor_scalar(cen[:, :, :], x[:, :, :], ALPHA, None, ALU.mult).then_inc(flag_seen, 1)
                    dve.wait_ge(flag_seen, l + 1)
                    for i in range(4):
                        split(S2_MOE + i + 2)
                    gated(0, S2_MOE + 4)
                    with dve.Fori(1, NE) as e:
                        k = (e - 1) * 6
                        for i in range(6):
                            n = S2_MOE + 6 + i
                            split_at(n, e - 1, 4, COLS)
                            if i == 1:
                                spread((e - 1) * 2 + X2_MOE, (2, 2), (mt_hi, mt_lo))
                            if i == 3:
                                gated(e, k + (S2_MOE + 8))
                            if i == 4:
                                add_y(0, (e - 1) * 2 + 1, k + (S2_MOE + 9))
                            if i == 5:
                                add_y(1, (e - 1) * 2 + 2, k + (S2_MOE + 10))
                    spread(X2_LAYER - 2, (2, 2), (mt_hi, mt_lo))
                    add_y(0, 2 * NE - 1, S2_LAYER - 1)
                    add_y(1, 2 * NE, S2_LAYER)
                    for c, n in ((pick_ready, NE + 1), (xg_low, NE + 1), (gate_sum, NE), (up_sum, NE), (ax_ready, NE),
                                 (place_ready, NE), (ag_low, NE)):
                        dve.sem_inc(c.sem, n)
                layer_norm(cen, rs2_ready.at2(l, 4), lnw_in.at2(l, 64), lk)
                dve.wait_ge(*h_ready.at2(l, 4))
                dve.sem_inc(v_chain, CHAIN2 - chain[0])

        @block.tensor
        def _(pe):
            pe.sem_inc(w_used.sem, w_used.prime)
            pe.sem_inc(acc_read.sem, acc_read.prime)
            for p in range(2):
                pe.sem_inc(pair_free[p].sem, pair_free[p].prime)
            pe.wait_ge(consts_in, 16 * 6)
            pe.wait_ge(stage_in, STAGE)
            pe.wait_ge(zeroed, 2)
            for l in range(LAYERS):
                pe.transpose(mp[:, l, 0:PC_ROWS], stage[:, l, :], ident[0:PC_ROWS, 0:PC_ROWS]).then_inc(params_t, 1)

            def sum_mod(vec, l):
                pe.wait_ge(*acc_done.at(l, vec + 1))
                a = acc[:, vec % 2, :]
                if vec in (2, 5):
                    for n in range(2):
                        mm = pe.matmul(mp[:, MOD_BANK[vec] + n, :], ones[:, :], a[:, COLS * n:COLS * (n + 1)], start=True, stop=True)
                else:
                    bank = MOD_BANK[vec % 6]
                    for c in range(KD):
                        mm = pe.matmul(mp[:, bank, c:c + 1], a[:, P * c:P * (c + 1)], ones[:, 0:1], start=True, stop=True)
                mm.then_inc(acc_read.sem, 1)

            pe.wait_ge(params_ready, LAYERS)
            sum_mod(0, 0)
            sum_mod(1, 0)


            with pe.Fori(0, LAYERS) as l:
                def product(s):
                    g = G_OF["split", s]
                    pe.wait_ge(*raw_read[g % RAW].at(l, g // RAW + 1))
                    _, units, cols = weights(("split", s), l)
                    w_hi, w_lo = slot(whi, s % SPLIT, units, cols), slot(wlo, s % SPLIT, units, cols)
                    for q, c0, wide, parts, first, last, name in group_jobs(s):
                        a_hi, a_lo = stationary[name]
                        if first:
                            pe.wait_ge(*pair_free[q % 2].at(l, 2 * (q // 2)))
                        for t in range(NT):
                            ts = slice(P * t, P * (t + 1))
                            for n, (unit, chunk) in enumerate(parts):
                                for m, (a, w) in enumerate(((a_hi, w_hi), (a_hi, w_lo), (a_lo, w_hi))):
                                    mm = pe.matmul(gp[:, q % 2, t, 0:wide], a[:, chunk, ts], w[:, unit, c0:c0 + wide],
                                                   start=first and n == 0 and m == 0, stop=last and n == len(parts) - 1 and m == 2)
                    mm.then_inc(w_used.sem, 1)

                def turn(bank, src, c0, n=2):
                    for k in range(n):
                        for t in range(NT):
                            mm = pe.transpose(mp[:, bank, T * k + P * t:T * k + P * (t + 1)], src[:, t, c0 + P * k:c0 + P * (k + 1)], ident[:, :])
                    return mm

                pe.wait_ge(*mod_taken.at(l, 2))
                pe.wait_ge(*xn_ready.at(l, 2))
                for b in range(4):
                    turn(b, xn1, 2 * P * b).then_inc(tr_done.sem, 1)
                for s in range(10):
                    if s < 2:
                        pe.wait_ge(*ft_lo.at(l, X_NORM1 + 2 * s + 2))
                    product(s)
                    if s == 5:
                        sum_mod(2, l)
                sum_mod(3, l)

                def scores(h):
                    if h >= 2:
                        pe.wait_ge(*s_max.at(l, h - 1))
                    r, c = slice(HD * (h % 2), HD * (h % 2) + HD), h // 2
                    pe.matmul(mp[:, h % 2, 0:P], qt[r, c, 0:P], kt[r, c, 0:P], start=True, stop=True)
                    pe.matmul(mp[:, h % 2, P:3 * P], qt[r, c, P:T], kt[r, c, :], start=True, stop=True).then_inc(s_done.sem, 1)

                def turn_p(h):
                    pe.wait_ge(*e_done.at(l, 2 * h + 2))
                    if h >= 1:
                        pe.wait_ge(*pt_taken.at(l, h))
                    for a in range(3):
                        mm = pe.transpose(mp[:, 2, P * a:P * (a + 1)], sc[:, h % 2, P * a:P * (a + 1)], ident[:, :])
                    mm.then_inc(pt_done.sem, 1)

                def weigh(h):
                    pe.wait_ge(*pt_taken.at(l, h + 1))
                    if h >= 1:
                        pe.wait_ge(*o_taken.at(l, h))
                    v = u[:, :, 2 * COLS + HD * h:2 * COLS + HD * (h + 1)]
                    pe.matmul(mp[:, 3, 0:HD], pt[:, 0:P], v[:, 0, :], start=True, stop=True)
                    pe.matmul(mp[:, 3, HD:2 * HD], pt[:, P:2 * P], v[:, 0, :], start=True, stop=False)
                    pe.matmul(mp[:, 3, HD:2 * HD], pt[:, 2 * P:3 * P], v[:, 1, :], start=False, stop=True).then_inc(o_done.sem, 1)

                for i in range(12):
                    product(10 + i)
                    if i == 0:
                        pe.wait_ge(*qk_ready.at(l, 1))
                        pe.wait_ge(*mod_taken.at(l, 4))
                        for b in range(4):
                            mm = turn(b, u, 2 * P * b)
                        mm.then_inc(qkt_done.sem, 1)
                    if i == 1:
                        pe.wait_ge(*qkt_taken.at(l, 4))
                        pe.wait_ge(*cu_ready.at(l, 1))
                        for b in range(3):
                            mm = turn(b, u, 3 * COLS + 2 * P * b)
                        mm.then_inc(pct_done.sem, 1)
                    if i == 2:
                        pe.wait_ge(*pct_taken.at(l, 3))
                    if 0 <= i - 4 < HEADS:
                        weigh(i - 4)
                    if 0 <= i - 3 < HEADS:
                        turn_p(i - 3)
                    if 0 <= i - 2 < HEADS:
                        scores(i - 2)
                pe.wait_ge(*s_max.at(l, HEADS))
                sum_mod(4, l)
                pe.wait_ge(*pooled.at(l, 1))
                for c in range(2):
                    mm = pe.matmul(mp[:, 1, T * c:T * (c + 1)], poolcur[:, c, :], w1[:, c, PAD:PAD + T], start=True, stop=True)
                mm.then_inc(tr_done.sem, 1)
                pe.wait_ge(*o_taken.at(l, HEADS))
                for b in range(2):
                    turn(2 + b, o, 2 * P * b).then_inc(tr_done.sem, 1)
                for s in range(S_BR, S_OUT):
                    if s == S_BR:
                        pe.wait_ge(*ft_lo.at(l, X_POOL + 1))
                    if s == S_BR + 1:
                        pe.wait_ge(*ft_lo.at(l, X_CONV + 1))
                    if s == S_BR + 2:
                        pe.wait_ge(*ft_lo.at(l, X_ATT + 2))
                    product(s)
                pe.wait_ge(*mod_taken.at(l, 5))
                for b in range(4):
                    if b % 2 == 0:
                        pe.wait_ge(*merged_ready.at(l, b // 2 + 1))
                    turn(b, merged, 2 * P * b).then_inc(tr_done.sem, 1)
                for s in range(S_OUT, S_FF):
                    if s < S_OUT + 2:
                        pe.wait_ge(*ft_lo.at(l, X_MERGE + 2 * (s - S_OUT) + 2))
                    product(s)
                pe.wait_ge(*xn_ready.at(l, 4))
                for b in range(4):
                    turn(b, xn2, 2 * P * b).then_inc(tr_done.sem, 1)

                def turn_ab(j):
                    pe.wait_ge(*ab_ready.at(l, j + 1))
                    if j >= 2:
                        pe.wait_ge(*ft_lo.at(l, X_ACT + 2 * (j - 2) + 2))
                    for b in range(2 if j < FF_BLOCKS - 1 else 1):
                        turn(2 * (j % 2) + b if j < FF_BLOCKS - 1 else 2, ab, 2 * P * b).then_inc(tr_done.sem, 1)

                for s in range(S_FF, S_DOWN):
                    if s < S_FF + 2:
                        pe.wait_ge(*ft_lo.at(l, X_NORM2 + 2 * (s - S_FF) + 2))
                    product(s)
                    j, r = divmod(s - S_FF, 4)
                    if s == S_FF + 3:
                        sum_mod(5, l)
                    if r == 1 and j >= 1:
                        if j == 2:
                            pe.wait_ge(*mod_taken.at(l, 6))
                        turn_ab(j - 1)
                for s in range(S_DOWN, S_LAYER):
                    if s == S_DOWN:
                        pe.wait_ge(*ft_lo.at(l, X_ACT + 2 * (FF_BLOCKS - 1)))
                    if s == S_DOWN + 2:
                        turn_ab(FF_BLOCKS - 1)
                    if s == S_DOWN + 3:
                        pe.wait_ge(*ft_lo.at(l, X_ACT + 2 * (FF_BLOCKS - 1)))
                        sum_mod(6, l)
                        sum_mod(7, l)
                    if s == S_LAYER - 2:
                        pe.wait_ge(*ft_lo.at(l, X_LAYER))
                    product(s)

            with pe.Fori(0, LAYERS) as l:
                def low_ready(n, turn):
                    _, _, read, before = ring2(n)
                    pe.wait_ge(*read.at2(l, turn + (before + 1)))

                def multiply(n, turn, q, units, cols, chunk0, src, first, last, pair_k):
                    low_ready(n, turn)
                    w_hi, w_lo = slot(whi, n % SPLIT, units, cols), slot(wlo, n % SPLIT, units, cols)
                    a_hi, a_lo = src
                    if first:
                        pe.wait_ge(*pair_free[q % 2].at2(l, pair_k))
                    for t in range(NT):
                        ts = slice(P * t, P * (t + 1))
                        for unit in range(units):
                            for m, (a, w) in enumerate(((a_hi, w_hi), (a_hi, w_lo), (a_lo, w_hi))):
                                mm = pe.matmul(gp[:, q % 2, t, 0:cols], a[:, chunk0 + unit, ts], w[:, unit, :],
                                               start=first and unit == 0 and m == 0, stop=last and unit == units - 1 and m == 2)
                    mm.then_inc(w_used.sem, 1)

                def product(s):
                    _, units, cols = weights2(s, l)
                    if s < S2_UQ:
                        q, h, c, src = s // 2, s % 2, 4 * (s % 2), (xt_hi, xt_lo)
                        first, last = h == 0, h == 1
                    elif s < S2_OUT:
                        q, c, src, first, last = J2_UQ + s - S2_UQ, 0 if s < S2_UKV else 3, (mt_hi, mt_lo), True, True
                    else:
                        h = (s - S2_OUT) % 2
                        q, c, src, first, last = J2_OUT + (s - S2_OUT) // 2, 4 * h, (xt_hi, xt_lo), h == 0, h == 1
                    multiply(s, 0, q, units, cols, c, src, first, last, 2 * (q // 2))

                def turn(bank, src, c0, n=2):
                    for k in range(n):
                        for t in range(NT):
                            mm = pe.transpose(mp[:, bank, T * k + P * t:T * k + P * (t + 1)], src[:, t, c0 + P * k:c0 + P * (k + 1)], ident[:, :])
                    return mm

                pe.wait_ge(*h_ready.at2(l, 0))
                for b in range(4):
                    turn(b, x, 2 * P * b).then_inc(tr_done.sem, 1)
                for s in range(S2_UQ):
                    if s < 2:
                        pe.wait_ge(*ft_lo.at2(l, X2_IN + 2 * s + 2))
                    product(s)
                pe.wait_ge(*mla_ready.at2(l, 1))
                for b in range(3):
                    turn(b, pr, 2 * P * b, 2 if b < 2 else 1).then_inc(tr_done.sem, 1)
                pe.wait_ge(*logf_ready.at2(l, 1))
                pe.matmul(mp[:, 3, 0:FH], tri[:, :], fz[:, 0, :], start=True, stop=True)
                pe.matmul(mp[:, 3, FH:2 * FH], ones[:, :], fz[:, 0, :], start=True, stop=False)
                pe.matmul(mp[:, 3, FH:2 * FH], tri[:, :], fz[:, 1, :], start=False, stop=True).then_inc(cum_done.sem, 1)
                pe.wait_ge(*ft_lo.at2(l, X2_MLA + 3))
                for s in range(S2_UQ, S2_OUT):
                    product(s)

                def turn_qk(j):
                    q, k = job_operands(j)[:2]
                    w = job_width(j)
                    if j == 0:
                        pe.wait_ge(*km_ready.at2(l, 1))
                    if j == MH:
                        pe.wait_ge(*diff_ready.at2(l, 1))
                    if j == MH + 2 * DH:
                        pe.wait_ge(*fox_ready.at2(l, 1))
                    if j:
                        pe.wait_ge(*t2_taken.at2(l, j))
                    for i, v in enumerate((q, k)):
                        for t in range(NT):
                            mm = pe.transpose(mp[0:w, 0, T * i + P * t:T * i + P * (t + 1)], v[:, t, :], ident[:, :])
                    mm.then_inc(t2_done.sem, 1)

                def scores(j):
                    w = job_width(j)
                    pe.wait_ge(*t2_taken.at2(l, j + 1))
                    if j:
                        pe.wait_ge(*s2_max.at2(l, j))
                    qk = qkt[0:w, j % 2, :]
                    pe.matmul(mp[:, 1, 0:P], qk[:, 0:P], qk[:, T:T + P], start=True, stop=True)
                    pe.matmul(mp[:, 1, P:3 * P], qk[:, P:T], qk[:, T:2 * T], start=True, stop=True).then_inc(s2_done.sem, 1)

                def turn_p(j):
                    pe.wait_ge(*e2_done.at2(l, 2 * j + 2))
                    if j:
                        pe.wait_ge(*p2_taken.at2(l, j))
                    for a in range(3):
                        mm = pe.transpose(mp[:, 2, P * a:P * (a + 1)], sc2[:, j % 3, P * a:P * (a + 1)], ident[:, :])
                    mm.then_inc(p2_done.sem, 1)

                def weigh(j):
                    pe.wait_ge(*p2_taken.at2(l, j + 1))
                    if j:
                        pe.wait_ge(*o2_taken.at2(l, j))
                    else:
                        pe.wait_ge(*fox_ready.at2(l, 1))
                    v = job_operands(j)[2]
                    pe.matmul(mp[:, 3, 0:HD], pt2[:, 0:P], v[:, 0, :], start=True, stop=True)
                    pe.matmul(mp[:, 3, HD:2 * HD], pt2[:, P:2 * P], v[:, 0, :], start=True, stop=False)
                    pe.matmul(mp[:, 3, HD:2 * HD], pt2[:, 2 * P:3 * P], v[:, 1, :], start=False, stop=True).then_inc(o2_done.sem, 1)

                for i in range(AJ + 4):
                    if 0 <= i - 1 < AJ:
                        scores(i - 1)
                    if i < AJ:
                        turn_qk(i)
                    if 0 <= i - 4 < AJ:
                        weigh(i - 4)
                    if 0 <= i - 3 < AJ:
                        turn_p(i - 3)
                pe.wait_ge(*oa_ready.at2(l, 1))
                for b in range(4):
                    turn(b, oa, 2 * P * b).then_inc(tr_done.sem, 1)
                for s in range(S2_OUT, S2_MOE):
                    if s < S2_OUT + 2:
                        pe.wait_ge(*ft_lo.at2(l, X2_O + 2 * (s - S2_OUT) + 2))
                    product(s)
                def scatter(half, first=False, last=False):
                    for t in range(NT):
                        mm = pe.matmul(mp[:, 2 * t + half, :], back[:, P * t:P * (t + 1)], yx[:, half, :], start=first, stop=last)
                    return mm

                uses = [2 * sum(1 for q in range(J2_MOE) if q % 2 == p) for p in range(2)]
                pe.wait_ge(*h_ready.at2(l, 2))
                for b in range(4):
                    turn(b, x, 2 * P * b).then_inc(tr_done.sem, 1)
                pe.wait_ge(*ft_lo.at2(l, X2_H + 4))
                pe.wait_ge(*rw_ready.at2(l, 1))
                for p in range(2):
                    pe.wait_ge(*pair_free[p].at2(l, uses[p]))
                for t in range(NT):
                    ts = slice(P * t, P * (t + 1))
                    for c in range(KD):
                        for m, a in enumerate((xt_lo, xt_hi)):
                            mm = pe.matmul(small[:, 2 * NE * t:2 * NE * (t + 1)], a[:, c, ts], rw2[:, c, :, :].rearrange("p a n -> p (a n)"),
                                           start=c == 0 and m == 0, stop=c == KD - 1 and m == 1)
                mm.then_inc(logits_done.sem, 1)
                pe.wait_ge(*chosen.at2(l, 1))
                picked = rank[:, :, :].rearrange("p (t g) i -> p t (g i)", t=NT)
                pe.matmul(small[:, 0:NE], tri[:, :], picked[:, 0, :], start=True, stop=True)
                pe.matmul(small[:, NE:2 * NE], ones[:, :], picked[:, 0, :], start=True, stop=False)
                pe.matmul(small[:, NE:2 * NE], tri[:, :], picked[:, 1, :], start=False, stop=True)
                for t in range(NT):
                    mm = pe.matmul(small[:, 2 * NE:3 * NE], ones[:, :], picked[:, t, :], start=t == 0, stop=t == 1)
                mm.then_inc(chosen_sum.sem, 1)
                xt, mt = (xt_hi, xt_lo), (mt_hi, mt_lo)

                def turn_ab(e, banks_free):
                    pe.wait_ge(*ab2_ready.at2(l, e))
                    pe.wait_ge(*banks_free)
                    for b in range(2):
                        turn(b, ab2, 2 * P * b).then_inc(tr_done.sem, 1)

                def gather(k, first=False):
                    pe.wait_ge(*pick_ready.at2(l, k + 1))
                    if not first:
                        pe.wait_ge(*xg_low.at2(l, k))
                    for c in range(KD):
                        for t in range(NT):
                            mm = pe.matmul(bank_tr[:, CAP * c:CAP * (c + 1)], x[:, t, P * c:P * (c + 1)], pick[:, t, :], start=t == 0, stop=t == 1)
                    mm.then_inc(gathered.sem, 1)

                def stacked(n, turn, bank, chunk0, a, first, last):
                    low_ready(n, turn)
                    w_hi, w_lo = slot(whi, n % SPLIT, 4, COLS), slot(wlo, n % SPLIT, 4, COLS)
                    for unit in range(4):
                        for m, w in enumerate((w_hi, w_lo)):
                            mm = pe.matmul(bank, a[:, chunk0 + unit, :], w[:, unit, :], start=first and unit == 0 and m == 0,
                                           stop=last and unit == 3 and m == 1)
                    mm.then_inc(w_used.sem, 1)

                def turn_gathered(k):
                    pe.wait_ge(*ax_ready.at2(l, k))
                    pe.wait_ge(*place_ready.at2(l, k))
                    pe.wait_ge(*xg_low.at2(l, k + 1))
                    for t in range(NT):
                        pe.transpose(bank_tr[:, T + P * t:T + P * (t + 1)], place[:, t, :], ident[:, :])
                    for c in range(4):
                        mm = pe.transpose(bank_tr[:, CAP * c:CAP * (c + 1)], ax[:, c // 2, P * (c % 2):P * (c % 2 + 1)], ident[0:CAP, 0:CAP])
                    mm.then_inc(ax_turned.sem, 1)

                def gathered_experts():
                    gather(0, True)
                    pe.wait_ge(*y_zero.at2(l, 2))
                    for half in range(2):
                        scatter(half, first=True)
                    pe.wait_ge(*xg_low.at2(l, 1))
                    for i in range(4):
                        n = S2_MOE + i
                        stacked(n, 0, (bank_gate, bank_up)[i // 2], 4 * (i % 2), xg, i % 2 == 0, i % 2 == 1)
                    gather(1)
                    with pe.Fori(1, NE) as e:
                        pe.wait_ge(*xg_low.at2(l, e + 1))
                        for i in range(6):
                            n = S2_MOE + 4 + i
                            if i < 4:
                                if i == 0:
                                    pe.wait_ge(*yx_ready.at2(l, (e - 1) * 2))
                                if i == 2:
                                    pe.wait_ge(*up_sum.at2(l, e))
                                stacked(n, e - 1, (bank_gate, bank_up)[i // 2], 4 * (i % 2), xg, i % 2 == 0, i % 2 == 1)
                                if i == 0:
                                    scatter(1)
                                    turn_gathered(e)
                            else:
                                if i == 4:
                                    pe.wait_ge(*ag_low.at2(l, e))
                                    gather(e + 1)
                                    pe.wait_ge(*gate_sum.at2(l, e + 1))
                                stacked(n, e - 1, (bank_gate, bank_y1)[i - 4], 0, ag, True, True)
                        pe.wait_ge(*back_ready.at2(l, e))
                        pe.wait_ge(*yx_ready.at2(l, (e - 1) * 2 + 1))
                        scatter(0)
                    pe.wait_ge(*yx_ready.at2(l, 2 * NE - 2))
                    scatter(1)
                    turn_gathered(NE)
                    pe.wait_ge(*ag_low.at2(l, NE))
                    for i in range(2):
                        n = S2_LAYER - 2 + i
                        stacked(n, 0, (bank_gate, bank_y1)[i], 0, ag, True, True)
                    pe.wait_ge(*back_ready.at2(l, NE))
                    pe.wait_ge(*yx_ready.at2(l, 2 * NE))
                    scatter(0, last=True)
                    scatter(1, last=True).then_inc(y_done.sem, 1)
                    pe.sem_inc(tr_done.sem, 2 * NE)

                pe.wait_ge(*flag_ready.at2(l, 1))
                pe.sem_inc(loads, 1)
                dense = pe.value_load(dense_i[0:1, 0:1], min_val=0, max_val=1)
                with pe.If(dense == 0):
                    gathered_experts()
                with pe.Else():
                    for i in range(4):
                        q = J2_MOE + i // 2
                        multiply(S2_MOE + i, 0, q, 4, COLS, 4 * (i % 2), xt, i % 2 == 0, i % 2 == 1, uses[q % 2])
                    with pe.Fori(1, NE) as e:
                        f = (e - 1) * 2
                        for i in range(6):
                            n = S2_MOE + 4 + i
                            q = J2_MOE + i // 2 if i < 4 else J2_MOE + (i - 4)
                            if i == 4:
                                pe.wait_ge(*ft_lo.at2(l, f + (X2_MOE + 2)))
                            use = (e - 1) * 4 + (uses[q % 2] + 2 + (2 if i >= 4 else 0))
                            multiply(n, e - 1, q, 4, COLS, 4 * (i % 2) if i < 4 else 0, xt if i < 4 else mt,
                                     i % 2 == 0 or i >= 4, i % 2 == 1 or i >= 4, use)
                            if i == 0:
                                turn_ab(e, rsc_ready.at2(l, 1))
                    turn_ab(NE, rsc_ready.at2(l, 1))
                    pe.wait_ge(*ft_lo.at2(l, X2_LAYER))
                    for i in range(2):
                        n = S2_LAYER - 2 + i
                        q = J2_MOE + i
                        multiply(n, 0, q, 4, COLS, 0, mt, True, True, uses[q % 2] + 2 + 4 * (NE - 1))
                    for c, n in ((gathered, NE + 1), (ax_turned, NE), (y_done, 1)):
                        pe.sem_inc(c.sem, n)


_INS = ["x", "c", "positions", "norm1_w", "norm2_w", "w_ada", "b_ada", "w_in", "pool_w", "pool_scale", "conv_w",
        "q_norm_w", "k_norm_w", "p_pool", "p_conv", "p_attn", "w_out", "w_gate", "w_up", "w_down",
        "positions_2", "ln_in_g_2", "ln_in_b_2", "w_in_2", "mla_q_norm_g_2", "mla_kv_norm_g_2", "mla_w_uq_2", "mla_w_ukv_2",
        "diff_lam_q1_2", "diff_lam_k1_2", "diff_lam_q2_2", "diff_lam_k2_2", "diff_subln_g_2", "fox_f_bias_2", "w_out_2",
        "ln1_g_2", "ln1_b_2", "router_w_2", "router_bias_2", "exp_w_gate_2", "exp_w_up_2", "exp_w_down_2", "ln2_g_2", "ln2_b_2"]


def kernel(**inputs):
    import concourse.bacc as bacc
    from concourse.bass_utils import run_bass_kernel_spmd

    nc = bacc.Bacc("TRN2", target_bir_lowering=False, num_devices=1)
    arrays, A = {}, {}
    for name in _INS:
        a = np.ascontiguousarray(inputs[name])
        arrays[f"in_{name}"] = a
    arrays.update(constants())
    for name, a in arrays.items():
        A[name.removeprefix("in_")] = nc.dram_tensor(name, a.shape, mybir.dt.from_np(a.dtype), kind="ExternalInput").ap()
    out = nc.dram_tensor("out_0", (1, T, D), F32, kind="ExternalOutput").ap()
    program(nc, A, out)
    return run_bass_kernel_spmd(nc, [arrays], core_ids=[0]).results[0]["out_0"]
```
